# Optimizing a Trainium2 kernel written in Bass

```python
import math
import jax, jax.numpy as jnp
from jax import lax
import numpy as np

D_MODEL = 1024
BATCH = 1
SEQ = 256
DEPTH = 1

HEAD_DIM = 64
S5_CH = D_MODEL // 4
S5_GROUP = 16
S5_NGROUPS = S5_CH // S5_GROUP
S5_STATE = 64
S5_DT_MIN = 1e-3
S5_DT_MAX = 1e-1
MOBA_HEADS = D_MODEL // 128
MOBA_W = MOBA_HEADS * HEAD_DIM
MOBA_BLOCK = 256
MOBA_TOPK = 3
MOBA_QCHUNK = 32
ROPE_THETA = 500000.0
ROPE_DIMS = HEAD_DIM // 4
RET_HEADS = D_MODEL // 256
RET_W = RET_HEADS * HEAD_DIM
RET_CHUNK = 128
RET_ANGLE_BASE = 10000.0
MIX_W = S5_CH + MOBA_W + RET_W
SPLIT_SIZES = (S5_CH, MOBA_W, MOBA_W, MOBA_W, RET_W, RET_W, RET_W, RET_W)
IN_W = sum(SPLIT_SIZES)
SPLIT_POINTS = tuple(sum(SPLIT_SIZES[:i + 1]) for i in range(len(SPLIT_SIZES) - 1))
PEER_KEYS = 128
PEER_EXPERTS = PEER_KEYS * PEER_KEYS
PEER_HEADS = 8
PEER_TOPK = 16
PEER_QDIM = 128
PEER_CHUNK = 128
EPS = 1e-6

kernel_name = 'hymba_s5_moba_retnet_peer'

def rms_unit(x):
    xf = x.astype(jnp.float32)
    return xf * lax.rsqrt(jnp.mean(xf * xf, axis=-1, keepdims=True) + EPS)

def rms_norm(x, g):
    return (rms_unit(x) * g.astype(jnp.float32)).astype(x.dtype)

def rotate(x, cos, sin):
    m = x.shape[-1] // 2
    x1, x2 = x[..., :m], x[..., m:]
    c = cos[None, :, None, :]
    s = sin[None, :, None, :]
    return jnp.concatenate([x1 * c - x2 * s, x2 * c + x1 * s], axis=-1)

def partial_rope(x, cos, sin):
    return jnp.concatenate([rotate(x[..., :ROPE_DIMS], cos, sin), x[..., ROPE_DIMS:]], axis=-1)

def _ssm_combine(e1, e2):
    a1r, a1i, b1r, b1i = e1
    a2r, a2i, b2r, b2i = e2
    return (a1r * a2r - a1i * a2i,
            a1r * a2i + a1i * a2r,
            a2r * b1r - a2i * b1i + b2r,
            a2r * b1i + a2i * b1r + b2i)

def s5_mixer(u, lam_re, lam_im, log_dt, b_re, b_im, c_re, c_im, d_skip, w_glu):
    bsz, s, _ = u.shape
    uf = u.astype(jnp.float32).reshape(bsz, s, S5_NGROUPS, S5_GROUP)
    lr = lam_re.astype(jnp.float32)
    li = lam_im.astype(jnp.float32)
    dt = jnp.exp(log_dt.astype(jnp.float32))[:, None]
    mag = jnp.exp(lr * dt)
    ar = mag * jnp.cos(li * dt)
    ai = mag * jnp.sin(li * dt)
    den = lr * lr + li * li
    fr = ((ar - 1.0) * lr + ai * li) / den
    fi = (ai * lr - (ar - 1.0) * li) / den
    br = b_re.astype(jnp.float32)
    bi = b_im.astype(jnp.float32)
    bbr = fr[..., None] * br - fi[..., None] * bi
    bbi = fr[..., None] * bi + fi[..., None] * br
    bu_r = jnp.einsum('bsgh,gph->bsgp', uf, bbr)
    bu_i = jnp.einsum('bsgh,gph->bsgp', uf, bbi)
    a_r = jnp.broadcast_to(ar, bu_r.shape)
    a_i = jnp.broadcast_to(ai, bu_i.shape)
    _, _, st_r, st_i = lax.associative_scan(_ssm_combine, (a_r, a_i, bu_r, bu_i), axis=1)
    y = (jnp.einsum('bsgp,ghp->bsgh', st_r, c_re.astype(jnp.float32))
         - jnp.einsum('bsgp,ghp->bsgh', st_i, c_im.astype(jnp.float32))
         + uf * d_skip.astype(jnp.float32).reshape(S5_NGROUPS, S5_GROUP))
    y = jax.nn.gelu(y.reshape(bsz, s, S5_CH))
    y = y * jax.nn.sigmoid(y @ w_glu.astype(jnp.float32))
    return y.astype(u.dtype)

def moba_mixer(q, k, v, gq, gk, cos, sin):
    bsz, s, _ = q.shape
    dtype = v.dtype
    hs = (bsz, s, MOBA_HEADS, HEAD_DIM)
    q = partial_rope(rms_unit(q.reshape(hs)) * gq.astype(jnp.float32), cos, sin).astype(dtype)
    k = partial_rope(rms_unit(k.reshape(hs)) * gk.astype(jnp.float32), cos, sin).astype(dtype)
    q = q.transpose(0, 2, 1, 3)
    k = k.transpose(0, 2, 1, 3)
    v = v.reshape(hs).transpose(0, 2, 1, 3)
    nb = -(-s // MOBA_BLOCK)
    pad = nb * MOBA_BLOCK - s
    padw = ((0, 0), (0, 0), (0, pad), (0, 0))
    kb = jnp.pad(k, padw).reshape(bsz, MOBA_HEADS, nb, MOBA_BLOCK, HEAD_DIM)
    vb = jnp.pad(v, padw).reshape(bsz, MOBA_HEADS, nb, MOBA_BLOCK, HEAD_DIM)
    kmean = jnp.mean(kb, axis=3)
    topk = min(MOBA_TOPK, nb)
    scale = HEAD_DIM ** -0.5
    gather = jax.vmap(jax.vmap(lambda blocks, ix: blocks[ix]))

    def chunk(c):
        start = c * MOBA_QCHUNK
        blk = start // MOBA_BLOCK
        qc = lax.dynamic_slice_in_dim(q, start, MOBA_QCHUNK, axis=2)
        gate = jnp.einsum('bhqd,bhnd->bhqn', qc, kmean).astype(jnp.float32)
        gate = jnp.where(jnp.arange(nb) < blk, gate, -jnp.inf)
        _, idx = lax.top_k(gate, topk)
        valid = jnp.arange(topk) < blk
        sk = gather(kb, idx)
        sv = gather(vb, idx)
        s_sel = jnp.einsum('bhqd,bhqjkd->bhqjk', qc, sk).astype(jnp.float32) * scale
        s_sel = jnp.where(valid[:, None], s_sel, -jnp.inf)
        s_sel = s_sel.reshape(bsz, MOBA_HEADS, MOBA_QCHUNK, topk * MOBA_BLOCK)
        ok = lax.dynamic_index_in_dim(kb, blk, axis=2, keepdims=False)
        ov = lax.dynamic_index_in_dim(vb, blk, axis=2, keepdims=False)
        s_own = jnp.einsum('bhqd,bhkd->bhqk', qc, ok).astype(jnp.float32) * scale
        qpos = start + jnp.arange(MOBA_QCHUNK)
        kpos = blk * MOBA_BLOCK + jnp.arange(MOBA_BLOCK)
        s_own = jnp.where(kpos[None, :] <= qpos[:, None], s_own, -jnp.inf)
        p = jax.nn.softmax(jnp.concatenate([s_sel, s_own], axis=-1), axis=-1)
        p_sel = p[..., :topk * MOBA_BLOCK].reshape(bsz, MOBA_HEADS, MOBA_QCHUNK, topk, MOBA_BLOCK).astype(dtype)
        p_own = p[..., topk * MOBA_BLOCK:].astype(dtype)
        return (jnp.einsum('bhqjk,bhqjkd->bhqd', p_sel, sv)
                + jnp.einsum('bhqk,bhkd->bhqd', p_own, ov))

    out = lax.map(chunk, jnp.arange(s // MOBA_QCHUNK))
    return out.transpose(1, 0, 3, 2, 4).reshape(hs)

def retention_mixer(q, k, v, g, cos, sin):
    bsz, s, _ = q.shape
    dtype = v.dtype
    hs = (bsz, s, RET_HEADS, HEAD_DIM)
    q = rotate(q.astype(jnp.float32).reshape(hs), cos, sin)
    k = rotate(k.astype(jnp.float32).reshape(hs), cos, sin) * (HEAD_DIM ** -0.5)
    v = v.astype(jnp.float32).reshape(hs)
    log_g = jnp.log(1.0 - 2.0 ** (-5.0 - jnp.arange(RET_HEADS, dtype=jnp.float32)))
    n = s // RET_CHUNK
    cs = (bsz, n, RET_CHUNK, RET_HEADS, HEAD_DIM)
    qc, kc, vc = q.reshape(cs), k.reshape(cs), v.reshape(cs)
    i = jnp.arange(RET_CHUNK, dtype=jnp.float32)
    diff = i[:, None] - i[None, :]
    dmask = jnp.where(diff >= 0, jnp.exp(jnp.maximum(diff, 0.0)[None] * log_g[:, None, None]), 0.0)
    inner = jnp.einsum('bnihd,bnjhd->bnhij', qc, kc) * dmask
    inner = jnp.einsum('bnhij,bnjhe->bnihe', inner, vc)
    zeta = jnp.exp((RET_CHUNK - 1.0 - i)[None, :] * log_g[:, None])
    kv = jnp.einsum('bnjhd,hj,bnjhe->nbhde', kc, zeta, vc)
    chunk_decay = jnp.exp(RET_CHUNK * log_g)[None, :, None, None]

    def step(state, kv_n):
        return chunk_decay * state + kv_n, state

    _, r_prev = lax.scan(step, jnp.zeros((bsz, RET_HEADS, HEAD_DIM, HEAD_DIM), jnp.float32), kv)
    xi = jnp.exp((i + 1.0)[None, :] * log_g[:, None])
    cross = jnp.einsum('bnihd,nbhde,hi->bnihe', qc, r_prev, xi)
    o = rms_unit((inner + cross).reshape(hs)).reshape(bsz, s, RET_W)
    return (jax.nn.silu(g.astype(jnp.float32)) * o).astype(dtype)

def peer_layer(h, w_q, sub_keys, u_emb, v_emb):
    bsz, s, d = h.shape
    t = bsz * s
    hf = h.reshape(t, d)
    q = (hf @ w_q).reshape(t, PEER_HEADS, 2, PEER_QDIM // 2)
    sc = jnp.einsum('thcd,hcnd->thcn', q, sub_keys).astype(jnp.float32)
    sv, si = lax.top_k(sc, PEER_TOPK)
    cand_s = (sv[:, :, 0, :, None] + sv[:, :, 1, None, :]).reshape(t, PEER_HEADS, PEER_TOPK * PEER_TOPK)
    cand_i = (si[:, :, 0, :, None] * PEER_KEYS + si[:, :, 1, None, :]).reshape(t, PEER_HEADS, PEER_TOPK * PEER_TOPK)
    fs, fp = lax.top_k(cand_s, PEER_TOPK)
    eidx = jnp.take_along_axis(cand_i, fp, axis=-1)
    gates = jax.nn.softmax(fs, axis=-1).astype(h.dtype)
    nch = t // PEER_CHUNK

    def chunk(args):
        xc, ic, gc = args
        ue = u_emb[ic]
        act = jax.nn.gelu(jnp.einsum('cd,chkd->chk', xc, ue))
        ve = v_emb[ic]
        return jnp.einsum('chk,chkd->cd', gc * act, ve)

    out = lax.map(chunk, (hf.reshape(nch, PEER_CHUNK, d),
                          eidx.reshape(nch, PEER_CHUNK, PEER_HEADS, PEER_TOPK),
                          gates.reshape(nch, PEER_CHUNK, PEER_HEADS, PEER_TOPK)))
    return out.reshape(bsz, s, d)

def setup_inputs(seed: int = 0) -> dict:
    key = jax.random.key(seed)
    ks = jax.random.split(key, 24)
    L, D, f32 = DEPTH, D_MODEL, jnp.float32
    nrm = lambda k, shp, sc: jax.random.normal(k, shp, f32) * sc
    gain = lambda k, n: 1.0 + 0.02 * jax.random.normal(k, (L, n), f32)
    return {
        'x': jax.random.normal(ks[0], (BATCH, SEQ, D), f32),
        'norm1_g': gain(ks[1], D),
        'w_in': nrm(ks[2], (L, D, IN_W), D ** -0.5),
        's5_lam_re': -0.5 + nrm(ks[3], (L, S5_NGROUPS, S5_STATE), 0.01),
        's5_lam_im': math.pi * jnp.arange(S5_STATE, dtype=f32) + nrm(ks[4], (L, S5_NGROUPS, S5_STATE), 0.01),
        's5_log_dt': jax.random.uniform(ks[5], (L, S5_NGROUPS), f32, math.log(S5_DT_MIN), math.log(S5_DT_MAX)),
        's5_b_re': nrm(ks[6], (L, S5_NGROUPS, S5_STATE, S5_GROUP), (2 * S5_GROUP) ** -0.5),
        's5_b_im': nrm(ks[7], (L, S5_NGROUPS, S5_STATE, S5_GROUP), (2 * S5_GROUP) ** -0.5),
        's5_c_re': nrm(ks[8], (L, S5_NGROUPS, S5_GROUP, S5_STATE), (2 * S5_STATE) ** -0.5),
        's5_c_im': nrm(ks[9], (L, S5_NGROUPS, S5_GROUP, S5_STATE), (2 * S5_STATE) ** -0.5),
        's5_d': nrm(ks[10], (L, S5_CH), 1.0),
        's5_w_glu': nrm(ks[11], (L, S5_CH, S5_CH), S5_CH ** -0.5),
        'moba_q_g': gain(ks[12], HEAD_DIM),
        'moba_k_g': gain(ks[13], HEAD_DIM),
        'mix_out_g': gain(ks[14], MIX_W),
        'w_out': nrm(ks[15], (L, MIX_W, D), 0.5 * MIX_W ** -0.5),
        'norm2_g': gain(ks[16], D),
        'peer_w_q': nrm(ks[17], (L, D, PEER_HEADS * PEER_QDIM), D ** -0.5),
        'peer_sub_keys': nrm(ks[18], (L, PEER_HEADS, 2, PEER_KEYS, PEER_QDIM // 2), (PEER_QDIM // 2) ** -0.5),
        'peer_u': nrm(ks[19], (L, PEER_EXPERTS, D), D ** -0.5),
        'peer_v': nrm(ks[20], (L, PEER_EXPERTS, D), D ** -0.5),
    }

def reference(x, norm1_g, w_in, s5_lam_re, s5_lam_im, s5_log_dt, s5_b_re, s5_b_im, s5_c_re, s5_c_im,
              s5_d, s5_w_glu, moba_q_g, moba_k_g, mix_out_g, w_out, norm2_g, peer_w_q, peer_sub_keys,
              peer_u, peer_v):
    s = x.shape[1]
    pos = jnp.arange(s, dtype=jnp.float32)
    inv = ROPE_THETA ** (-jnp.arange(0, ROPE_DIMS, 2, dtype=jnp.float32) / ROPE_DIMS)
    ang = pos[:, None] * inv[None, :]
    rope_cos, rope_sin = jnp.cos(ang), jnp.sin(ang)
    ret_inv = RET_ANGLE_BASE ** (-jnp.linspace(0.0, 1.0, HEAD_DIM // 2, dtype=jnp.float32))
    ret_ang = pos[:, None] * ret_inv[None, :]
    ret_cos, ret_sin = jnp.cos(ret_ang), jnp.sin(ret_ang)
    bsz = x.shape[0]
    for l in range(DEPTH):
        h = rms_norm(x, norm1_g[l])
        proj = h @ w_in[l]
        ua, qb, kb, vb, qc, kc, vc, gc = jnp.split(proj, SPLIT_POINTS, axis=-1)
        ya = s5_mixer(ua, s5_lam_re[l], s5_lam_im[l], s5_log_dt[l], s5_b_re[l], s5_b_im[l],
                      s5_c_re[l], s5_c_im[l], s5_d[l], s5_w_glu[l])
        ya = rms_unit(ya)
        yb = rms_unit(moba_mixer(qb, kb, vb, moba_q_g[l], moba_k_g[l], rope_cos, rope_sin))
        yb = yb.reshape(bsz, s, MOBA_W)
        yc = retention_mixer(qc, kc, vc, gc, ret_cos, ret_sin).astype(jnp.float32)
        y = jnp.concatenate([ya, yb, yc], axis=-1) * mix_out_g[l].astype(jnp.float32)
        x = x + (y.astype(x.dtype) @ w_out[l])
        h2 = rms_norm(x, norm2_g[l])
        x = x + peer_layer(h2, peer_w_q[l], peer_sub_keys[l], peer_u[l], peer_v[l])
    return x


_drawn_inputs = setup_inputs


def setup_inputs(seed=0):
    import zlib

    import numpy as np

    out = dict(_drawn_inputs(seed))
    spreads = {}
    factors = {'norm1_g': 3.977,
     's5_lam_re': 64.0,
     's5_lam_im': 28.024,
     's5_log_dt': 32.68,
     's5_b_re': 38.528,
     's5_b_im': 39.912,
     's5_c_re': 40.104,
     's5_c_im': 40.216,
     'moba_q_g': 8.0,
     'moba_k_g': 8.0,
     'mix_out_g': 6.727,
     'norm2_g': 8.0,
     'peer_w_q': 4.113,
     'peer_sub_keys': 4.102,
     'peer_u': 4.575,
     'peer_v': 4.104}
    for name, (base, spread) in spreads.items():
        noise = np.random.default_rng([zlib.crc32(name.encode()), seed]).standard_normal(out[name].shape)
        drawn = base * np.exp(spread * noise) if base else spread * noise
        out[name] = __import__('jax').numpy.asarray(drawn.astype(out[name].dtype))
    for name, factor in factors.items():
        out[name] = (out[name] * factor).astype(out[name].dtype)
    return out
```

```python
from contextlib import ExitStack

import numpy as np

import concourse.bass as bass
from concourse import mybir

F32 = mybir.dt.float32
F32R = mybir.dt.float32r
U32 = mybir.dt.uint32
ALU = mybir.AluOpType
ACT = mybir.ActivationFunctionType
AX = mybir.AxisListType

P = 128
S = 256
TT = S // P
D = 1024
KC = D // P
EPS = 1e-6

S5_CH, S5_GROUP, S5_STATE = 256, 16, 64
S5_NG = S5_CH // S5_GROUP
S5_T = S5_NG * S5_STATE // P
S5_C = S5_CH // P

HD = 64
MH, MW = 8, 512
RH, RW = 4, 256
ROPE = HD // 4
SCALE = HD ** -0.5
MASKED = -1e30

NKEY = 128
EXPERTS = NKEY * NKEY
PH, PK = 8, 16
HK = PH * PK
NT = EXPERTS // P

CHUNK = 512
W_SLOTS = 3

UN = 4
TURNS = NT // UN
HALF = D // 2
GT = 4
G_TURN0 = TURNS - S // GT // UN
EXP_TURN, ROUTE_TURN = 12, 14
LOWEST = -3e38

TWO_PI = 2 * np.pi
RC1 = 6.28125
RC2 = float(np.array([np.float32(TWO_PI - RC1)]).view(np.uint32).__and__(np.uint32(0xFFFFF000)).view(np.float32)[0])
RC3 = float(TWO_PI - RC1 - RC2)
ROUND = 1.5 * 2.0 ** 23
PI_LOW = 3.1415925

V_G1, V_G2, V_GM = 0, 8, 16
V_LR, V_LI, V_LDT = 24, 32, 40
V_D = 48
V_GQK = 50
V_N = V_GQK + 2 * HD
C_ID, C_IOTA = 0, P
C_RC = 2 * P
C_RS = C_RC + TT * (ROPE // 2)
C_TC = C_RS + TT * (ROPE // 2)
C_TS = C_TC + TT * (HD // 2)
C_N = C_TS + TT * (HD // 2)


class Chain:

    def __init__(self, eng, sem):
        self.eng, self.sem, self.n = eng, sem, 0

    def did(self, ins):
        self.n += 1
        ins.then_inc(self.sem, 1)

    def settle(self):
        self.eng.wait_ge(self.sem, self.n)


def build(nc, x, w_in, vecs, consts, decay, mask, s5_b, s5_c, w_glu, w_out, w_q, keys, u_t, v, out, spill):
    with ExitStack() as ctx:
        def sb(name, shape, dt=F32):
            return ctx.enter_context(nc.sbuf_tensor(name, shape, dt))

        def sem(name):
            return ctx.enter_context(nc.semaphore(name))

        xs = sb("xs", [P, TT, D])
        vec = sb("vec", [P, V_N])
        con = sb("con", [P, C_N])
        small = sb("small", [P, 1024])
        routing = sb("routing", [P, S, NKEY])
        h2_hi = sb("h2_hi", [P, KC, S], F32R)
        h2_lo = sb("h2_lo", [P, KC, S], F32R)
        raw = sb("raw", [P, UN, D])
        w_hi = sb("w_hi", [P, 4, HALF], F32R)
        w_lo = sb("w_lo", [P, 4, HALF], F32R)
        acts = sb("acts", [P, UN, S])
        weighted = sb("weighted", [P, 2, S])
        hot_j = sb("hot_j", [P, 2, GT, NKEY])
        hot_i = sb("hot_i", [P, 2, GT, NKEY])
        route_t = sb("route_t", [P, 3, S])
        ps = ctx.enter_context(nc.psum_tensor("ps", [P, 8, 512], F32))

        ident = con[:, C_ID:C_ID + P]
        iota = con[:, C_IOTA:C_IOTA + P]

        arena = routing[:].rearrange("p a b -> p (a b)")
        cursor = [0]

        def take(n):
            a = cursor[0]
            cursor[0] += n
            assert cursor[0] <= S * NKEY, cursor[0]
            return arena[:, a:a + n]

        w_ring = [take(KC * CHUNK).rearrange("p (k n) -> p k n", k=KC) for _ in range(W_SLOTS)]
        hT = take(KC * S).rearrange("p (k t) -> p k t", k=KC)
        xn = take(TT * D).rearrange("p (t d) -> p t d", t=TT)
        qk = take(TT * 2 * MW).rearrange("p (t d) -> p t d", t=TT)
        mv = take(TT * MW).rearrange("p (t d) -> p t d", t=TT)
        ret = take(TT * 4 * RW).rearrange("p (t d) -> p t d", t=TT)
        uT = take(S5_C * S).rearrange("p (c t) -> p c t", c=S5_C)
        ymix = take(TT * D).rearrange("p (t d) -> p t d", t=TT)
        region = cursor[0]
        r3 = lambda a, k: a.rearrange("p (k t) -> p k t", k=k)
        pc, pS, zr, zi = (r3(take(S5_T * S), S5_T) for _ in range(4))
        xn_states = xn.rearrange("p t d -> p (t d)").rearrange("p (j t) -> p j t", j=S5_T)
        cursor[0] = region
        att = take(3 * 1024)
        attT = take(3 * 1024)
        mqT = take(4 * S).rearrange("p (h t) -> p h t", h=4)
        mkT = take(4 * S).rearrange("p (h t) -> p h t", h=4)
        cursor[0] = region
        rqT = take(2 * S).rearrange("p (h t) -> p h t", h=2)
        rkT = take(2 * S).rearrange("p (h t) -> p h t", h=2)
        rP0 = take(RH * S).rearrange("p (h t) -> p h t", h=RH)
        rP1 = take(RH * P).rearrange("p (h t) -> p h t", h=RH)
        cursor[0] = W_SLOTS * KC * CHUNK + KC * S
        pqT = take(PH * S).rearrange("p (h t) -> p h t", h=PH)
        sc = take(TT * 2 * PH * NKEY).rearrange("p (t c h n) -> p t c h n", t=TT, c=2, h=PH)
        work = take(2 * PH * NKEY).rearrange("p (c h n) -> p c h n", c=2, h=PH)
        work2 = take(2 * PH * NKEY)
        work3 = take(2 * PH * NKEY)
        rawf = raw[:].rearrange("p a b -> p (a b)")
        mask_s = rawf[:, 0:S]
        keys_s = rawf[:, 256:256 + PH * NKEY].rearrange("p (h n) -> p h n", h=PH)
        glu_s = rawf[:, 1280:1280 + S5_C * S5_CH].rearrange("p (c n) -> p c n", c=S5_C)
        bT = rawf[:, 1792:1792 + 4 * P].rearrange("p (a s) -> p a s", a=4)
        b_s = rawf[:, 2304:2304 + 512].rearrange("p (r j c) -> p r j c", r=2, j=S5_T)
        c_s = rawf[:, 2816:2816 + 512].rearrange("p (r j c) -> p r j c", r=2, j=S5_T)
        bb = rawf[:, 3328:3328 + 512].rearrange("p (r j c) -> p r j c", r=2, j=S5_T)
        decay_s = acts[:]
        hj = hot_j[:].rearrange("p a b c -> p (a b c)")
        tmp1 = hj.rearrange("p (j t) -> p j t", j=4)

        x_in, params_in, decay_in = sem("x_in"), sem("params_in"), sem("decay_in")
        w_in_sem = [sem(f"weights_in{i}") for i in range(W_SLOTS)]
        dve_steps, act_steps = sem("dve_steps"), sem("act_steps")
        sumsq_x, var_ready, std_ready, xn_ready = sem("sumsq_x"), sem("var_ready"), sem("std_ready"), sem("xn_ready")
        t_psum, hT_ready = sem("transposes_in_psum"), sem("hT_ready")
        dt_ready, expo_ready, mag_ready = sem("dt_ready"), sem("exponent_ready"), sem("mag_ready")
        ang_ready, trig_ready = sem("angles_ready"), sem("trig_ready")
        bb_ready, bT_psum, bT_ready = sem("bb_ready"), sem("bT_in_psum"), sem("bT_ready")
        u_psum, u_ready = sem("u_in_psum"), sem("u_ready")
        bu_psum, bu_used = sem("bu_in_psum"), sem("bu_used")
        proj_psum, proj_ready = sem("proj_in_psum"), sem("proj_ready")
        states_ready, y_psum, y_lin, y_ready = sem("states_ready"), sem("y_in_psum"), sem("y_linear"), sem("y_ready")
        glu_psum, gate_ready, ya_ready, yaT_psum = sem("glu_in_psum"), sem("glu_gate_ready"), sem("ya_ready"), sem("ya_t_in_psum")
        ya_read = sem("ya_t_read")
        rot_ready, rotT_psum, rotT_ready = sem("rotated_ready"), sem("rotated_t_in_psum"), sem("rotated_t_ready")
        s_psum, max_ready, exp_ready = sem("scores_in_psum"), sem("max_ready"), sem("exp_ready")
        s_read = sem("scores_read")
        pT_psum, pT_ready = sem("probs_t_in_psum"), sem("probs_t_ready")
        o_psum, o_read = sem("heads_out_in_psum"), sem("heads_out_read")
        rs_psum, rp_ready, silu_ready = sem("ret_scores_in_psum"), sem("ret_probs_ready"), sem("silu_ready")
        mix_ready, out_psum = sem("mix_ready"), sem("out_proj_in_psum")
        h2_hi_ready, h2_ready = sem("h2_hi_ready"), sem("h2_ready")
        pq_psum, pq_ready, sc_psum, sc_ready = sem("pq_in_psum"), sem("pq_ready"), sem("keys_scores_in_psum"), sem("keys_scores_ready")
        raw_in = [sem(f"raw_in{i}") for i in range(UN)]
        hi_ready, lo_ready = sem("hi_ready"), sem("lo_ready")
        half_used = sem("half_used")
        act_ready = sem("act_ready")
        spilled = [sem("spilled0"), sem("spilled1")]
        acts_in = [sem("acts_in0"), sem("acts_in1")]
        diff_ready, gate_exp = sem("gate_exponents_ready"), sem("gate_exp_ready")
        tok_ready, route_psum, route_ready = sem("route_rows_ready"), sem("route_t_in_psum"), sem("route_t_ready")
        hot_ready, group_psum, group_done = sem("one_hots_ready"), sem("group_in_psum"), sem("group_done")
        w_steps, w_ready, product_done = sem("weighted_steps"), sem("weighted_ready"), sem("product_done")
        sum_ready, stored = sem("sum_ready"), sem("stored")

        V = nc.vector
        A = nc.scalar

        def cols(off, n):
            return vec[:, off:off + n]

        def sm(off, n):
            return small[:, off:off + n]

        o = [0]

        def tiny(n):
            a = sm(o[0], n)
            o[0] += n
            assert o[0] <= 1024
            return a

        def tiny_as(n, dtype):
            return tiny(n).bitcast(dtype)

        ss_x, rstd = tiny(TT), tiny(32)
        dt, expo, mag, ang, kk, s1, c1, half = (tiny(8) for _ in range(8))
        ar, ai, den, fr, fi, q1, q2, q3 = (tiny(8) for _ in range(8))
        sq_c, sq_s = tiny(64).rearrange("p (n j) -> p n j", j=8), tiny(64).rearrange("p (n j) -> p n j", j=8)
        std = tiny(32)
        hmax, hsum = tiny(16), tiny(16)
        top = tiny(2 * PH * PK).rearrange("p (c h k) -> p c h k", c=2, h=PH)

        w_src = [w_in[:, 0:S5_CH]] + [w_in[:, S5_CH + CHUNK * n:S5_CH + CHUNK * (n + 1)] for n in range(5)]
        w_src += [w_out[:, CHUNK * n:CHUNK * (n + 1)] for n in range(2)]
        w_src += [w_q[:, CHUNK * n:CHUNK * (n + 1)] for n in range(2)]
        W_N = len(w_src)
        idx = tiny_as(2 * PH * PK, U32).rearrange("p (c h k) -> p c h k", c=2, h=PH)
        pos = tiny_as(PH * PK, U32).rearrange("p (h k) -> p h k", h=PH)
        tab = hT.rearrange("p k t -> p (k t)")
        rows = tab[:, 0:768].rearrange("p (t a k) -> p t a k", t=TT, a=3)
        idx_f = tab[:, 768:1024].rearrange("p (c h k) -> p c h k", c=2, h=PH)
        ab = tab[:, 1024:1280].bitcast(U32).rearrange("p (c h k) -> p c h k", c=2, h=PH)
        ab_f = tab[:, 1280:1536].rearrange("p (c h k) -> p c h k", c=2, h=PH)
        top2 = tab[:, 1536:1664].rearrange("p (h k) -> p h k", h=PH)
        gsum = tab[:, 1664:1680].rearrange("p (t h) -> p t h", t=TT)
        block = ctx.enter_context(nc.Block())

        @block.sync
        def _(sp):
            sp.dma_start(xs[:], x.rearrange("(t p) d -> p t d", p=P)).then_inc(x_in, 16)
            sp.dma_start(vec[:], vecs).then_inc(params_in, 16)
            sp.dma_start(con[:], consts).then_inc(params_in, 16)
            sp.dma_start(rawf[:, 2304:2816], s5_b).then_inc(params_in, 16)
            for n in range(W_N):
                if n == 3:
                    sp.dma_start(rawf[:, 2816:3328], s5_c).then_inc(decay_in, 16)
                    sp.dma_start(glu_s, w_glu.rearrange("(c p) n -> p c n", p=P)).then_inc(decay_in, 16)
                    sp.dma_start(mask_s, mask).then_inc(decay_in, 16)
                    sp.dma_start(decay_s, decay).then_inc(decay_in, 16)
                    sp.dma_start(keys_s, keys).then_inc(decay_in, 16)
                if n >= W_SLOTS:
                    old = n - W_SLOTS
                    if old == 0:
                        sp.wait_ge(u_psum, 1)
                    elif old <= 5:
                        sp.wait_ge(proj_psum, TT * old)
                    else:
                        sp.wait_ge(out_psum, TT * (old - 5))
                width = w_src[n].shape[1]
                sp.dma_start(w_ring[n % W_SLOTS][:, :, 0:width],
                             w_src[n].rearrange("(k p) n -> p k n", p=P)).then_inc(w_in_sem[n % W_SLOTS], 16)

            def load_tile(weights, tile, s):
                sp.dma_start(raw[:, s, :], weights[tile]).then_inc(raw_in[s], 16)

            sp.wait_ge(sc_psum, TT)
            for s in range(UN):
                load_tile(u_t, s, s)

            def keys_turn(t, weights, nxt):
                for s in range(UN):
                    sp.wait_ge(lo_ready, 8 * t + 2 * s + 2)
                    load_tile(weights, nxt + s, s)
                    if s % 2:
                        sp.wait_ge(act_ready, UN * t + s + 1)
                        sp.dma_start(spill[2 * t + s // 2], acts[:, s - 1:s + 1, :].rearrange("p a t -> p (a t)"))\
                            .then_inc(spilled[s // 2], 16)

            with sp.Fori(0, TURNS - 1) as t:
                keys_turn(t, u_t, UN * t + UN)
            keys_turn(TURNS - 1, v, 0)

            def load_acts(pair, b):
                sp.dma_start(acts[:, 2 * b:2 * b + 2, :].rearrange("p a t -> p (a t)"), spill[pair])\
                    .then_inc(acts_in[b], 16)

            for b in range(2):
                sp.wait_ge(spilled[b], 16 * TURNS)
            for b in range(2):
                load_acts(b, b)
            with sp.Fori(0, TURNS - 1) as t:
                for s in range(UN):
                    sp.wait_ge(lo_ready, 2 * NT + 8 * t + 2 * s + 2)
                    load_tile(v, UN * t + UN + s, s)
                    if s % 2:
                        sp.wait_ge(product_done, UN * t + s + 1)
                        load_acts(2 * t + 2 + s // 2, s // 2)
            for n in range(2 * TT):
                sp.wait_ge(sum_ready, n + 1)
                h, t = n // TT, n % TT
                sp.dma_start(out[t * P:(t + 1) * P, h * HALF:(h + 1) * HALF],
                             xs[:, t, h * HALF:(h + 1) * HALF]).then_inc(stored, 16)
            sp.wait_ge(stored, 16 * 2 * TT)

        @block.tensor
        def _(pe):
            def chunk_in(n):
                pe.wait_ge(w_in_sem[n % W_SLOTS], 16 * (n // W_SLOTS + 1))
                return w_ring[n % W_SLOTS]

            def transpose_rows(src):
                for k in range(KC):
                    for t in range(TT):
                        mm = pe.transpose(ps[:, k // 2, (k % 2) * S + t * P:(k % 2) * S + (t + 1) * P],
                                          src[:, t, k * P:(k + 1) * P], ident)
                    if k % 2:
                        mm.then_inc(t_psum, 1)

            pe.wait_ge(params_in, 48)
            pe.wait_ge(xn_ready, TT)
            transpose_rows(xn)
            pe.wait_ge(bb_ready, 1)
            for r in range(2):
                for c in range(S5_C):
                    mm = pe.transpose(ps[:, 4, (r * 2 + c) * P:(r * 2 + c + 1) * P],
                                      bb[:, r, 4 * c:4 * c + 4, :].rearrange("p j c -> p (j c)"), ident)
            mm.then_inc(bT_psum, 1)
            w = chunk_in(0)
            pe.wait_ge(hT_ready, KC)
            for c in range(S5_C):
                for k in range(KC):
                    mm = pe.matmul(ps[:, 5, c * S:(c + 1) * S], w[:, k, c * P:(c + 1) * P], hT[:, k, :],
                                   start=(k == 0), stop=(k == KC - 1))
            mm.then_inc(u_psum, 1)

            def project(n):
                w = chunk_in(n)
                if n >= 3:
                    pe.wait_ge(proj_ready, 2 * (n - 2))
                for t in range(TT):
                    for k in range(KC):
                        mm = pe.matmul(ps[:, 2 * ((n - 1) % 2) + t, :], hT[:, k, t * P:(t + 1) * P], w[:, k, :],
                                       start=(k == 0), stop=(k == KC - 1))
                    mm.then_inc(proj_psum, 1)

            def drive(c):
                pe.wait_ge(u_ready, 1)
                pe.wait_ge(bT_ready, 1)
                if c:
                    pe.wait_ge(bu_used, c)
                for r in range(2):
                    for j in range(4):
                        mm = pe.matmul(ps[:, 4 + j, r * S:(r + 1) * S],
                                       bT[32 * j:32 * j + 32, r * 2 + c, :], uT[32 * j:32 * j + 32, c, :],
                                       start=True, stop=True)
                mm.then_inc(bu_psum, 1)

            drive(0)
            project(1)
            drive(1)
            for n in range(2, 6):
                project(n)

            pe.wait_ge(decay_in, 80)
            pe.wait_ge(states_ready, 1)
            for c in range(S5_C):
                for j in range(4):
                    for r, st in ((0, xn_states), (1, zi)):
                        mm = pe.matmul(ps[32 * j:32 * j + 32, 4, c * S:(c + 1) * S], c_s[:, r, 4 * c + j, :],
                                       st[:, 4 * c + j, :], start=(r == 0), stop=(r == 1))
            mm.then_inc(y_psum, 1)
            pe.wait_ge(y_ready, 1)
            for m in range(S5_C):
                for c in range(S5_C):
                    mm = pe.matmul(ps[:, 5, m * S:(m + 1) * S], glu_s[:, c, m * P:(m + 1) * P], uT[:, c, :],
                                   start=(c == 0), stop=(c == S5_C - 1))
            mm.then_inc(glu_psum, 1)
            pe.wait_ge(ya_ready, 1)
            for t in range(TT):
                for c in range(S5_C):
                    mm = pe.transpose(ps[:, 6, t * S5_CH + c * P:t * S5_CH + (c + 1) * P], uT[:, c, t * P:(t + 1) * P], ident)
            mm.then_inc(yaT_psum, 1)

            pe.wait_ge(rot_ready, 1)
            for a in range(2):
                for h in range(4):
                    for t in range(TT):
                        mm = pe.transpose(ps[:, 2 * a + h // 2, (h % 2) * S + t * P:(h % 2) * S + (t + 1) * P],
                                          qk[:, t, a * MW + h * P:a * MW + (h + 1) * P], ident)
            mm.then_inc(rotT_psum, 1)
            pe.wait_ge(rotT_ready, 1)
            for h in range(4):
                for o_ in range(2):
                    r = slice(HD * o_, HD * (o_ + 1))
                    pe.matmul(ps[:, o_, h * P:(h + 1) * P], mqT[r, h, 0:P], mkT[r, h, 0:P], start=True, stop=True)
            for h in range(4):
                for o_ in range(2):
                    r = slice(HD * o_, HD * (o_ + 1))
                    mm = pe.matmul(ps[:, 2 + 2 * o_ + h // 2, (h % 2) * S:(h % 2 + 1) * S], mqT[r, h, P:S], mkT[r, h, :],
                                   start=True, stop=True)
            mm.then_inc(s_psum, 1)
            pe.wait_ge(exp_ready, 16)
            for b in range(6):
                for h in range(4):
                    g = 4 * (b % 2) + h
                    src = att[:, g * P:(g + 1) * P] if b < 2 else \
                        att[:, 1024 + g * S + (b // 2 - 1) * P:1024 + g * S + (b // 2) * P]
                    mm = pe.transpose(ps[:, b, h * P:(h + 1) * P], src, ident)
                mm.then_inc(pT_psum, 1)
            pe.wait_ge(ya_read, 1)
            pe.wait_ge(pT_ready, 6)
            for h in range(MH):
                g = 4 * (h % 2) + h // 2
                c = slice(h * HD, (h + 1) * HD)
                pe.matmul(ps[:, 6, c], attT[:, g * P:(g + 1) * P], mv[:, 0, c], start=True, stop=True)
                pe.matmul(ps[:, 7, c], attT[:, 1024 + g * P:1024 + (g + 1) * P], mv[:, 0, c], start=True, stop=False)
                mm = pe.matmul(ps[:, 7, c], attT[:, 2048 + g * P:2048 + (g + 1) * P], mv[:, 1, c], start=False, stop=True)
            mm.then_inc(o_psum, 1)

            pe.wait_ge(rot_ready, 2)
            for a in range(2):
                for h in range(2):
                    for t in range(TT):
                        mm = pe.transpose(ps[:, a, h * S + t * P:h * S + (t + 1) * P],
                                          ret[:, t, a * RW + h * P:a * RW + (h + 1) * P], ident)
            mm.then_inc(rotT_psum, 1)
            pe.wait_ge(rotT_ready, 2)
            for h in range(2):
                for o_ in range(2):
                    r = slice(HD * o_, HD * (o_ + 1))
                    pe.matmul(ps[:, 2 + o_, h * S:(h + 1) * S], rkT[r, h, 0:P], rqT[r, h, :], start=True, stop=True)
            for h in range(2):
                for o_ in range(2):
                    r = slice(HD * o_, HD * (o_ + 1))
                    mm = pe.matmul(ps[:, 4 + o_, h * P:(h + 1) * P], rkT[r, h, P:S], rqT[r, h, P:S], start=True, stop=True)
            mm.then_inc(rs_psum, 1)
            pe.wait_ge(rp_ready, 1)
            for h in range(RH):
                c = slice(h * HD, (h + 1) * HD)
                vc = slice(2 * RW + h * HD, 2 * RW + (h + 1) * HD)
                pe.matmul(ps[:, 0, c], rP0[:, h, 0:P], ret[:, 0, vc], start=True, stop=True)
                o1 = ps[:, 0, RW + h * HD:RW + (h + 1) * HD]
                pe.matmul(o1, rP0[:, h, P:S], ret[:, 0, vc], start=True, stop=False)
                mm = pe.matmul(o1, rP1[:, h, :], ret[:, 1, vc], start=False, stop=True)
            mm.then_inc(o_psum, 1)

            pe.wait_ge(mix_ready, 1)
            transpose_rows(ymix)
            pe.wait_ge(hT_ready, 2 * KC)
            for n in range(2):
                w = chunk_in(6 + n)
                for t in range(TT):
                    for k in range(KC):
                        mm = pe.matmul(ps[:, 4 + 2 * n + t, :], hT[:, k, t * P:(t + 1) * P], w[:, k, :],
                                       start=(k == 0), stop=(k == KC - 1))
                    mm.then_inc(out_psum, 1)

            pe.wait_ge(xn_ready, 2 * TT)
            transpose_rows(xn)
            pe.wait_ge(hT_ready, 3 * KC)
            for n in range(2):
                w = chunk_in(8 + n)
                for h in range(4):
                    for k in range(KC):
                        mm = pe.matmul(ps[:, 4 + 2 * n + h // 2, (h % 2) * S:(h % 2 + 1) * S],
                                       w[:, k, h * P:(h + 1) * P], hT[:, k, :], start=(k == 0), stop=(k == KC - 1))
                    if h % 2:
                        mm.then_inc(pq_psum, 1)
            pe.wait_ge(pq_ready, 4)
            for t in range(TT):
                for h in range(PH):
                    for c in range(2):
                        r = slice(HD * c, HD * (c + 1))
                        mm = pe.matmul(ps[:, 4 * t + 2 * c + h // 4, (h % 4) * NKEY:(h % 4 + 1) * NKEY],
                                       pqT[r, h, t * P:(t + 1) * P], keys_s[r, h, :], start=True, stop=True)
                mm.then_inc(sc_psum, 1)

            def halves_product(dst, pairs, first, last):
                for i, (s_hi, s_lo, m_hi, m_lo) in enumerate(pairs):
                    end = last and i == len(pairs) - 1
                    pe.matmul(dst, s_hi, m_hi, start=first and i == 0, stop=False)
                    pe.matmul(dst, s_hi, m_lo, start=False, stop=False)
                    mm = pe.matmul(dst, s_lo, m_hi, start=False, stop=end)
                return mm

            def keys_turn(t, groups=None, first=False, first_group=False):
                for s in range(UN):
                    if not (first and s < 2):
                        pe.wait_ge(act_ready, UN * t + s - 1)
                    for h in range(2):
                        pe.wait_ge(lo_ready, 8 * t + 2 * s + h + 1)
                        slot = 2 * (s % 2) + h
                        pairs = [(w_hi[:, slot, k * P:(k + 1) * P], w_lo[:, slot, k * P:(k + 1) * P],
                                  h2_hi[:, 4 * h + k, :], h2_lo[:, 4 * h + k, :]) for k in range(4)]
                        halves_product(ps[:, s % 2, 0:S], pairs, h == 0, h == 1).then_inc(half_used, 1)
                    if groups is not None:
                        g = groups + s
                        pe.wait_ge(hot_ready, g + 1)
                        if not (first_group and s < 2):
                            pe.wait_ge(group_done, g - 1)
                        for q in range(GT):
                            mm = pe.matmul(ps[:, 2 + s % 2, q * P:(q + 1) * P], hot_j[:, s % 2, q, :], hot_i[:, s % 2, q, :],
                                           start=True, stop=True)
                        mm.then_inc(group_psum, 1)

            pe.wait_ge(sc_ready, 8)
            pe.wait_ge(h2_ready, 1)
            keys_turn(0, first=True)
            with pe.Fori(1, ROUTE_TURN) as t:
                keys_turn(t)
            pe.wait_ge(tok_ready, 1)
            for t in range(TT):
                for a in range(3):
                    mm = pe.transpose(ps[:, 4 + t, a * P:(a + 1) * P], rows[:, t, a, :], ident)
            mm.then_inc(route_psum, 1)
            with pe.Fori(ROUTE_TURN, G_TURN0) as t:
                keys_turn(t)
            keys_turn(G_TURN0, groups=0, first_group=True)
            with pe.Fori(G_TURN0 + 1, TURNS) as t:
                keys_turn(t, groups=UN * t - UN * G_TURN0)

            def values_turn(t, first=False, last=False):
                for s in range(UN):
                    pe.wait_ge(w_ready, UN * t + s + 1)
                    for h in range(2):
                        pe.wait_ge(lo_ready, 2 * NT + 8 * t + 2 * s + h + 1)
                        slot = 2 * (s % 2) + h
                        for tt_ in range(TT):
                            r = slice(tt_ * P, (tt_ + 1) * P)
                            mm = halves_product(ps[:, 4 + 2 * h + tt_, :],
                                                [(h2_hi[:, s, r], h2_lo[:, s, r], w_hi[:, slot, :], w_lo[:, slot, :])],
                                                first and s == 0, last and s == UN - 1)
                        mm.then_inc(half_used, 1)

            pe.wait_ge(route_ready, 2)
            values_turn(0, first=True)
            with pe.Fori(1, TURNS - 1) as t:
                values_turn(t)
            values_turn(TURNS - 1, last=True)

        @block.vector
        def _(dve):
            ch = Chain(dve, dve_steps)
            did, settle = ch.did, ch.settle
            n_var = [0]

            def step(ins):
                did(ins)
                settle()

            def rstd_from(sums, n, width):
                V.tensor_scalar(std[:, 0:n], sums, 1.0 / width, EPS, ALU.mult, ALU.add).then_inc(var_ready, 1)
                n_var[0] += 1
                dve.wait_ge(std_ready, n_var[0])
                step(V.reciprocal(rstd[:, 0:n], std[:, 0:n]))

            def tt(out_, a, b, op):
                return V.tensor_tensor(out_, a, b, op)

            dve.wait_ge(sumsq_x, TT)
            rstd_from(ss_x, TT, D)
            for t in range(TT):
                V.tensor_scalar(xn[:, t, :], xs[:, t, :], rstd[:, t:t + 1], None, ALU.mult).then_inc(xn_ready, 1)

            dve.wait_ge(params_in, 48)
            lr, li = cols(V_LR, 8), cols(V_LI, 8)
            dve.wait_ge(dt_ready, 1)
            tt(expo, lr, dt, ALU.mult).then_inc(expo_ready, 1)
            step(tt(ang, li, dt, ALU.mult))
            step(V.tensor_scalar(kk, ang, float(1 / TWO_PI), ROUND, ALU.mult, ALU.add))
            step(V.tensor_scalar(kk, kk, -ROUND, None, ALU.add))
            for part in (RC1, RC2, RC3):
                step(V.scalar_tensor_tensor(ang, kk, -part, ang, ALU.mult, ALU.add))
            step(V.tensor_scalar(ang, ang, -PI_LOW, PI_LOW, ALU.max, ALU.min))
            step(V.tensor_scalar(half, ang, -1.0, None, ALU.mult))
            step(tt(half, half, ang, ALU.min))
            V.tensor_scalar(half, half, float(np.pi / 2), None, ALU.add).then_inc(ang_ready, 1)
            dve.wait_ge(mag_ready, 1)
            dve.wait_ge(trig_ready, 1)
            did(tt(ar, mag, c1, ALU.mult))
            did(tt(ai, mag, s1, ALU.mult))
            did(tt(q1, lr, lr, ALU.mult))
            did(tt(q2, li, li, ALU.mult))
            settle()
            step(tt(den, q1, q2, ALU.add))
            did(V.reciprocal(den, den))
            step(V.tensor_scalar(ar, ar, -1.0, None, ALU.add))
            did(tt(q1, ar, lr, ALU.mult))
            did(tt(q2, ai, li, ALU.mult))
            did(tt(q3, ai, lr, ALU.mult))
            did(tt(kk, ar, li, ALU.mult))
            settle()
            did(tt(fr, q1, q2, ALU.add))
            did(tt(fi, q3, kk, ALU.subtract))
            settle()
            did(tt(fr, fr, den, ALU.mult))
            did(tt(fi, fi, den, ALU.mult))
            settle()
            wide = lambda a: a.unsqueeze(2).to_broadcast([P, S5_T, 32])
            t_a = hj[:, 0:256].rearrange("p (j c) -> p j c", j=S5_T)
            t_b = hj[:, 256:512].rearrange("p (j c) -> p j c", j=S5_T)
            did(tt(bb[:, 0], b_s[:, 0], wide(fr), ALU.mult))
            did(tt(t_a, b_s[:, 1], wide(fi), ALU.mult))
            did(tt(bb[:, 1], b_s[:, 1], wide(fr), ALU.mult))
            did(tt(t_b, b_s[:, 0], wide(fi), ALU.mult))
            settle()
            did(tt(bb[:, 0], bb[:, 0], t_a, ALU.subtract))
            settle()
            tt(bb[:, 1], bb[:, 1], t_b, ALU.add).then_inc(bb_ready, 1)
            dve.wait_ge(bb_ready, 1)

            step(V.tensor_copy(sq_c[:, 0, :], c1))
            step(V.tensor_copy(sq_s[:, 0, :], s1))
            for n in range(1, 8):
                a, b = sq_c[:, n - 1, :], sq_s[:, n - 1, :]
                did(tt(q1, a, a, ALU.mult))
                did(tt(q2, b, b, ALU.mult))
                did(tt(q3, a, b, ALU.mult))
                settle()
                did(tt(sq_c[:, n, :], q1, q2, ALU.subtract))
                did(V.tensor_scalar(sq_s[:, n, :], q3, 2.0, None, ALU.mult))
                settle()
            did(V.memset(pc[:, :, 0:1], 1.0))
            did(V.memset(pS[:, :, 0:1], 0.0))
            settle()
            for n in range(8):
                m = 1 << n
                wc = sq_c[:, n, :].unsqueeze(2).to_broadcast([P, S5_T, m])
                wsn = sq_s[:, n, :].unsqueeze(2).to_broadcast([P, S5_T, m])
                lo_c, lo_s = pc[:, :, 0:m], pS[:, :, 0:m]
                did(tt(pc[:, :, m:2 * m], lo_c, wc, ALU.mult))
                did(tt(zr[:, :, 0:m], lo_s, wsn, ALU.mult))
                did(tt(pS[:, :, m:2 * m], lo_c, wsn, ALU.mult))
                did(tt(zi[:, :, 0:m], lo_s, wc, ALU.mult))
                settle()
                did(tt(pc[:, :, m:2 * m], pc[:, :, m:2 * m], zr[:, :, 0:m], ALU.subtract))
                did(tt(pS[:, :, m:2 * m], pS[:, :, m:2 * m], zi[:, :, 0:m], ALU.add))
                settle()

            for c in range(S5_C):
                js = slice(4 * c, 4 * c + 4)
                bur = ps[:, 4:8, 0:S]
                bui = ps[:, 4:8, S:2 * S]
                tmp2 = xn_states[:, js, :]
                dve.wait_ge(bu_psum, c + 1)
                did(tt(zr[:, js], bur, pc[:, js], ALU.mult))
                did(tt(tmp1, bui, pS[:, js], ALU.mult))
                did(tt(zi[:, js], bui, pc[:, js], ALU.mult))
                if c == 0:
                    dve.wait_ge(t_psum, 4)
                ins = tt(tmp2, bur, pS[:, js], ALU.mult)
                did(ins)
                settle()
                tt(zr[:, js], zr[:, js], tmp1, ALU.add).then_inc(bu_used, 1)
                step(tt(zi[:, js], zi[:, js], tmp2, ALU.subtract))
                dve.wait_ge(bu_used, c + 1)
            for j in range(S5_T):
                for z in (zr, zi):
                    did(V.tensor_tensor_scan(z[:, j, :], mag[:, j:j + 1].to_broadcast([P, S]), z[:, j, :], 0.0,
                                             ALU.mult, ALU.add))
            settle()
            for c in range(S5_C):
                js = slice(4 * c, 4 * c + 4)
                did(tt(xn_states[:, js], pc[:, js], zr[:, js], ALU.mult))
                did(tt(tmp1, pS[:, js], zi[:, js], ALU.mult))
                settle()
                did(tt(xn_states[:, js], xn_states[:, js], tmp1, ALU.subtract))
                did(tt(zr[:, js], pS[:, js], zr[:, js], ALU.mult))
                did(tt(zi[:, js], pc[:, js], zi[:, js], ALU.mult))
                settle()
                step(tt(zi[:, js], zi[:, js], zr[:, js], ALU.add))
            dve.wait_ge(decay_in, 80)
            V.tensor_scalar(c_s[:, 1], c_s[:, 1], -1.0, None, ALU.mult).then_inc(states_ready, 1)
            dve.wait_ge(states_ready, 1)
            dve.wait_ge(y_psum, 1)
            for c in range(S5_C):
                V.scalar_tensor_tensor(uT[:, c, :], uT[:, c, :], cols(V_D + c, 1), ps[:, 4, c * S:(c + 1) * S],
                                       ALU.mult, ALU.add).then_inc(y_lin, 1)
            dve.wait_ge(gate_ready, 1)
            tt(uT[:], uT[:], hj[:, 0:S5_C * S].rearrange("p (c t) -> p c t", c=S5_C), ALU.mult).then_inc(ya_ready, 1)
            dve.wait_ge(yaT_psum, 1)
            y_a = ps[:, 6, :].rearrange("p (t d) -> p t d", t=TT)
            step(V.tensor_copy(ymix[:, :, 0:S5_CH], y_a))
            sq = hj[:, 0:512].rearrange("p (t d) -> p t d", t=TT)
            tt(sq, ymix[:, :, 0:S5_CH], ymix[:, :, 0:S5_CH], ALU.mult).then_inc(ya_read, 1)
            dve.wait_ge(ya_read, 1)
            step(V.tensor_reduce(q1[:, 0:TT], sq, AX.X, ALU.add))
            rstd_from(q1[:, 0:TT], TT, S5_CH)
            for t in range(TT):
                did(V.tensor_scalar(ymix[:, t, 0:S5_CH], ymix[:, t, 0:S5_CH], rstd[:, t:t + 1], None, ALU.mult))
            settle()

            dve.wait_ge(proj_ready, 10)
            scr = xn.rearrange("p t d -> p (t d)")
            sq = scr.rearrange("p (h d) -> p h d", d=HD)
            qkh = qk.rearrange("p t d -> p (t d)").rearrange("p (h d) -> p h d", d=HD)
            step(tt(sq, qkh, qkh, ALU.mult))
            step(V.tensor_reduce(hj[:, 0:32], sq, AX.X, ALU.add))
            rstd_from(hj[:, 0:32], 32, HD)
            step(tt(qkh, qkh, rstd[:, 0:32].unsqueeze(2).to_broadcast([P, 32, HD]), ALU.mult))
            for t in range(TT):
                for a in range(2):
                    q4 = qk[:, t, a * MW:(a + 1) * MW].rearrange("p (h d) -> p h d", h=MH)
                    did(tt(q4, q4, cols(V_GQK + a * HD, HD).unsqueeze(1).to_broadcast([P, MH, HD]), ALU.mult))
            settle()

            def rotate(views, cos, sin, scratch):
                n = 0
                parts = []
                for (x1, x2), co, si in zip(views, cos, sin):
                    size = x1.shape[1] * x1.shape[2]
                    tmp = [scratch[:, n + size * m:n + size * (m + 1)].rearrange("p (h d) -> p h d", h=x1.shape[1])
                           for m in range(2)]
                    n += 2 * size
                    b = lambda a: a.unsqueeze(1).to_broadcast([P, x1.shape[1], x1.shape[2]])
                    did(tt(tmp[0], x2, b(si), ALU.mult))
                    did(tt(tmp[1], x1, b(si), ALU.mult))
                    parts.append((x1, x2, co, tmp, b))
                settle()
                for x1, x2, co, tmp, b in parts:
                    did(tt(x1, x1, b(co), ALU.mult))
                    did(tt(x2, x2, b(co), ALU.mult))
                settle()
                for x1, x2, co, tmp, b in parts:
                    did(tt(x1, x1, tmp[0], ALU.subtract))
                    last = tt(x2, x2, tmp[1], ALU.add)
                    did(last)
                settle()

            hr = ROPE // 2
            rope = [con[:, C_RC + t * hr:C_RC + (t + 1) * hr] for t in range(TT)], \
                   [con[:, C_RS + t * hr:C_RS + (t + 1) * hr] for t in range(TT)]
            per_tile = [qk[:, t, :].rearrange("p (h d) -> p h d", d=HD) for t in range(TT)]
            rotate([(v_[:, :, 0:hr], v_[:, :, hr:ROPE]) for v_ in per_tile], *rope, scr)
            V.tensor_copy(hj[:, 0:1], hj[:, 1:2]).then_inc(rot_ready, 1)
            dve.wait_ge(rot_ready, 1)
            hh = HD // 2
            rope = [con[:, C_TC + t * hh:C_TC + (t + 1) * hh] for t in range(TT)], \
                   [con[:, C_TS + t * hh:C_TS + (t + 1) * hh] for t in range(TT)]
            per_tile = [ret[:, t, 0:2 * RW].rearrange("p (h d) -> p h d", d=HD) for t in range(TT)]
            rotate([(v_[:, :, 0:hh], v_[:, :, hh:HD]) for v_ in per_tile], *rope, scr)
            V.tensor_copy(hj[:, 0:1], hj[:, 1:2]).then_inc(rot_ready, 1)
            dve.wait_ge(rot_ready, 2)

            dve.wait_ge(s_psum, 1)
            a0 = att[:, 0:1024].rearrange("p (h k) -> p h k", h=MH)
            a1 = att[:, 1024:3072].rearrange("p (h k) -> p h k", h=MH)
            s0 = ps[:, 0:2, :].rearrange("p b (h k) -> p (b h) k", h=4)
            s1_ = ps[:, 2:6, :].rearrange("p b (h k) -> p (b h) k", h=2)
            did(V.scalar_tensor_tensor(a0, s0, SCALE, mask_s[:, P:S].unsqueeze(1).to_broadcast([P, MH, P]), ALU.mult, ALU.add))
            did(V.scalar_tensor_tensor(a1, s1_, SCALE, mask_s.unsqueeze(1).to_broadcast([P, MH, S]), ALU.mult, ALU.add))
            settle()
            did(V.tensor_reduce(hmax[:, 0:8], a0, AX.X, ALU.max))
            did(V.tensor_reduce(hmax[:, 8:16], a1, AX.X, ALU.max))
            settle()
            V.tensor_scalar(hmax, hmax, -1.0, None, ALU.mult).then_inc(max_ready, 1)
            dve.wait_ge(exp_ready, 16)
            step(V.reciprocal(hsum, hsum))
            dve.wait_ge(o_psum, 1)
            for t in range(TT):
                o_v = ps[:, 6 + t, :].rearrange("p (p2 o d) -> p o p2 d", o=2, d=HD)
                y_v = ymix[:, t, S5_CH:S5_CH + MW].rearrange("p (p2 o d) -> p o p2 d", o=2, d=HD)
                for o_ in range(2):
                    r_v = hsum[:, 8 * t + 4 * o_:8 * t + 4 * o_ + 4].unsqueeze(2).to_broadcast([P, 4, HD])
                    did(tt(y_v[:, o_], o_v[:, o_], r_v, ALU.mult))
            settle()
            y_b = ymix[:, :, S5_CH:S5_CH + MW].rearrange("p t (h d) -> p t h d", d=HD)
            sq = scr[:, 0:1024].rearrange("p (t h d) -> p t h d", t=TT, d=HD)
            step(tt(sq, y_b, y_b, ALU.mult))
            step(V.tensor_reduce(hj[:, 0:16].rearrange("p (t h) -> p t h", t=TT), sq, AX.X, ALU.add))
            rstd_from(hj[:, 0:16], 16, HD)
            for t in range(TT):
                did(tt(y_b[:, t], y_b[:, t], rstd[:, 8 * t:8 * t + 8].unsqueeze(2).to_broadcast([P, MH, HD]), ALU.mult))
            settle()

            dve.wait_ge(rs_psum, 1)
            dec = decay_s.rearrange("p (h o) i -> p h o i", o=2)
            for o_ in range(2):
                did(tt(rP0.rearrange("p (h o) i -> p h o i", o=2)[:, :, o_],
                       ps[:, 2 + o_, :].rearrange("p (h i) -> p h i", h=2), dec[:, :, o_], ALU.mult))
                did(tt(rP1.rearrange("p (h o) i -> p h o i", o=2)[:, :, o_],
                       ps[:, 4 + o_, 0:256].rearrange("p (h i) -> p h i", h=2), dec[:, :, o_, 0:P], ALU.mult))
            settle()
            V.tensor_copy(hj[:, 0:1], hj[:, 1:2]).then_inc(rp_ready, 1)
            dve.wait_ge(o_psum, 2)
            dve.wait_ge(rp_ready, 1)
            y_c = ymix[:, :, S5_CH + MW:D].rearrange("p t (h d) -> p t h d", d=HD)
            step(V.tensor_copy(ymix[:, :, S5_CH + MW:D], ps[:, 0, :].rearrange("p (t d) -> p t d", t=TT)))
            sq = scr[:, 0:512].rearrange("p (t h d) -> p t h d", t=TT, d=HD)
            step(tt(sq, y_c, y_c, ALU.mult))
            step(V.tensor_reduce(hj[:, 0:8].rearrange("p (t h) -> p t h", t=TT), sq, AX.X, ALU.add))
            rstd_from(hj[:, 0:8], 8, HD)
            for t in range(TT):
                did(tt(y_c[:, t], y_c[:, t], rstd[:, 4 * t:4 * t + 4].unsqueeze(2).to_broadcast([P, RH, HD]), ALU.mult))
            settle()
            dve.wait_ge(silu_ready, 1)
            tt(ymix[:, :, S5_CH + MW:D], ymix[:, :, S5_CH + MW:D], ret[:, :, 3 * RW:4 * RW], ALU.mult).then_inc(mix_ready, 1)

            for n in range(2):
                for t in range(TT):
                    dve.wait_ge(out_psum, 2 * n + t + 1)
                    c = slice(CHUNK * n, CHUNK * (n + 1))
                    did(tt(xs[:, t, c], xs[:, t, c], ps[:, 4 + 2 * n + t, :], ALU.add))
            settle()
            for t in range(TT):
                step(tt(xn[:, t, :], xs[:, t, :], xs[:, t, :], ALU.mult))
            step(V.tensor_reduce(ss_x, xn, AX.X, ALU.add))
            rstd_from(ss_x, TT, D)
            for t in range(TT):
                V.tensor_scalar(xn[:, t, :], xs[:, t, :], rstd[:, t:t + 1], None, ALU.mult).then_inc(xn_ready, 1)
            dve.wait_ge(h2_hi_ready, KC)
            tt(h2_lo[:], hT, h2_hi[:].bitcast(F32), ALU.subtract).then_inc(h2_ready, 1)

            def best(dst, where, src, scratch):
                for d_, s_ in zip(dst, src):
                    did(V.max(d_[:, 0:8], s_))
                settle()
                for d_, w_, s_, x_ in zip(dst, where, src, scratch):
                    did(V.max_index(w_[:, 0:8], d_[:, 0:8], s_))
                    did(V.match_replace(x_, d_[:, 0:8], s_, LOWEST))
                settle()
                for d_, x_ in zip(dst, scratch):
                    did(V.max(d_[:, 8:16], x_))
                settle()
                for d_, w_, x_ in zip(dst, where, scratch):
                    did(V.max_index(w_[:, 8:16], d_[:, 8:16], x_))
                settle()

            ch_rows = [(c, h) for c in range(2) for h in range(PH)]
            shape = [P, PH, PK, PK]
            w2 = work2.rearrange("p (h a b) -> p h a b", h=PH, a=PK)
            w3 = work3.rearrange("p (h a b) -> p h a b", h=PH, a=PK)
            iota_k = iota[:, 0:PK].unsqueeze(1).unsqueeze(1).to_broadcast(shape)
            for t in range(TT):
                dve.wait_ge(sc_ready, 4 * t + 4)
                best([top[:, c, h, :] for c, h in ch_rows], [idx[:, c, h, :] for c, h in ch_rows],
                     [sc[:, t, c, h, :] for c, h in ch_rows], [work[:, c, h, :] for c, h in ch_rows])
                did(V.tensor_copy(idx_f, idx))
                step(tt(w2, top[:, 0].unsqueeze(3).to_broadcast(shape), top[:, 1].unsqueeze(2).to_broadcast(shape), ALU.add))
                pairs = [work2[:, h * 256:(h + 1) * 256] for h in range(PH)]
                best([top2[:, h, :] for h in range(PH)], [pos[:, h, :] for h in range(PH)], pairs,
                     [work3[:, h * 256:(h + 1) * 256] for h in range(PH)])
                did(tt(rows[:, t, 2, :].rearrange("p (h k) -> p h k", h=PH), top2,
                       top2[:, :, 0:1].to_broadcast([P, PH, PK]), ALU.subtract))
                did(V.tensor_scalar(ab[:, 0], pos, 4, None, ALU.logical_shift_right))
                did(V.tensor_scalar(ab[:, 1], pos, PK - 1, None, ALU.bitwise_and))
                settle()
                step(V.tensor_copy(ab_f, ab))
                for c in range(2):
                    step(tt(w2, ab_f[:, c].unsqueeze(3).to_broadcast(shape), iota_k, ALU.is_equal))
                    step(tt(w3, w2, idx_f[:, c].unsqueeze(2).to_broadcast(shape), ALU.mult))
                    step(V.tensor_reduce(rows[:, t, c, :].rearrange("p (h k) -> p h k", h=PH), w3, AX.X, ALU.add))
            V.tensor_copy(top2[:, 0, 0:1], top2[:, 0, 1:2]).then_inc(diff_ready, 1)
            dve.wait_ge(gate_exp, TT)
            gates = rows[:, :, 2, :].rearrange("p t (h k) -> p t h k", h=PH)
            step(V.tensor_reduce(gsum, gates, AX.X, ALU.add))
            step(V.reciprocal(gsum, gsum))
            for t in range(TT):
                did(tt(gates[:, t], gates[:, t], gsum[:, t].unsqueeze(2).to_broadcast([P, PH, PK]), ALU.mult))
            settle()
            V.tensor_copy(top2[:, 0, 0:1], top2[:, 0, 1:2]).then_inc(tok_ready, 1)
            dve.wait_ge(route_ready, TT)

            def one_hots(t, first=False):
                for s in range(UN):
                    g = UN * t + s
                    if not (first and s < 2):
                        dve.wait_ge(group_psum, g - 1)
                    tok = bass.ds(g * GT, GT)
                    tt(hot_j[:, s % 2], iota.unsqueeze(1).to_broadcast([P, GT, P]),
                       route_t[:, 1, tok].unsqueeze(2).to_broadcast([P, GT, P]), ALU.is_equal)
                    for q in range(GT):
                        one = bass.ds(g * GT + q, 1)
                        ins = V.tensor_scalar(hot_i[:, s % 2, q, :], iota, route_t[:, 0, one], route_t[:, 2, one],
                                              ALU.is_equal, ALU.mult)
                    ins.then_inc(hot_ready, 1)

            one_hots(0, first=True)
            with dve.Fori(1, TURNS - G_TURN0) as t:
                one_hots(t)

            dve.wait_ge(group_done, S // GT)

            def weigh(t, first=False):
                for s in range(UN):
                    n = UN * t + s
                    if s % 2 == 0:
                        dve.wait_ge(acts_in[s // 2], 16 * t + 16)
                    if first:
                        dve.wait_ge(half_used, 2 * NT)
                    else:
                        dve.wait_ge(half_used, 2 * NT + 8 * t + 2 * s - 6)
                    tt(weighted[:, s % 2, :], acts[:, s, :], routing[:, :, bass.ds(n, 1)].rearrange("p t o -> p (t o)"),
                       ALU.mult).then_inc(product_done, 1)
                    dve.wait_ge(product_done, n + 1)
                    V.tensor_copy(h2_hi[:, s, :], weighted[:, s % 2, :]).then_inc(w_steps, 1)
                    dve.wait_ge(w_steps, n + 1)
                    tt(h2_lo[:, s, :], weighted[:, s % 2, :], h2_hi[:, s, :].bitcast(F32), ALU.subtract).then_inc(w_ready, 1)

            weigh(0, first=True)
            with dve.Fori(1, TURNS) as t:
                weigh(t)
            for h in range(2):
                dve.wait_ge(half_used, 4 * NT - 1 + h)
                for t in range(TT):
                    c = slice(h * HALF, (h + 1) * HALF)
                    tt(xs[:, t, c], xs[:, t, c], ps[:, 4 + 2 * h + t, :], ALU.add).then_inc(sum_ready, 1)

        @block.scalar
        def _(act):
            ch = Chain(act, act_steps)
            did, settle = ch.did, ch.settle
            n_std = [0]
            n_h = [0]

            def root(n):
                n_std[0] += 1
                act.wait_ge(var_ready, n_std[0])
                A.activation(std[:, 0:n], std[:, 0:n], ACT.Sqrt).then_inc(std_ready, 1)

            def copy_rows_t(gain, extra=False):
                for k in range(KC):
                    act.wait_ge(t_psum, 4 * n_h[0] + k // 2 + 1)
                    A.activation(hT[:, k, :], ps[:, k // 2, (k % 2) * S:(k % 2 + 1) * S], ACT.Copy,
                                 scale=cols(gain + k, 1)).then_inc(hT_ready, 1)
                n_h[0] += 1

            act.wait_ge(x_in, 16)
            for t in range(TT):
                if t:
                    act.wait_ge(sumsq_x, t)
                A.activation(xn[:, t, :], xs[:, t, :], ACT.Square, accum_out=ss_x[:, t:t + 1]).then_inc(sumsq_x, 1)
            root(TT)
            act.wait_ge(params_in, 48)
            A.activation(dt, cols(V_LDT, 8), ACT.Exp).then_inc(dt_ready, 1)
            act.wait_ge(expo_ready, 1)
            A.activation(mag, expo, ACT.Exp).then_inc(mag_ready, 1)
            copy_rows_t(V_G1)
            act.wait_ge(ang_ready, 1)
            did(A.activation(s1, ang, ACT.Sin))
            settle()
            A.activation(c1, half, ACT.Sin).then_inc(trig_ready, 1)
            act.wait_ge(bT_psum, 1)
            A.activation(bT, ps[:, 4, :].rearrange("p (a s) -> p a s", a=4), ACT.Copy).then_inc(bT_ready, 1)
            act.wait_ge(u_psum, 1)
            A.activation(uT, ps[:, 5, :].rearrange("p (c t) -> p c t", c=S5_C), ACT.Copy).then_inc(u_ready, 1)
            dst = [qk[:, :, 0:MW], qk[:, :, MW:2 * MW], mv, ret[:, :, 0:2 * RW], ret[:, :, 2 * RW:4 * RW]]
            for n in range(5):
                for t in range(TT):
                    act.wait_ge(proj_psum, 2 * n + t + 1)
                    A.activation(dst[n][:, t, :], ps[:, 2 * (n % 2) + t, :], ACT.Copy).then_inc(proj_ready, 1)
            act.wait_ge(y_lin, 2)
            A.activation(uT, uT, ACT.Gelu_apprx_tanh).then_inc(y_ready, 1)
            act.wait_ge(glu_psum, 1)
            A.activation(hj[:, 0:S5_C * S], ps[:, 5, :], ACT.Sigmoid).then_inc(gate_ready, 1)
            act.wait_ge(proj_ready, 10)
            A.activation(ret[:, :, 3 * RW:4 * RW], ret[:, :, 3 * RW:4 * RW], ACT.Silu).then_inc(silu_ready, 1)
            root(TT)
            root(32)
            act.wait_ge(rotT_psum, 1)
            for h, d_ in ((0, mqT), (2, mkT)):
                did(A.activation(d_, ps[:, h:h + 2, :].rearrange("p b (h t) -> p (b h) t", h=2), ACT.Copy))
            settle()
            A.activation(small[:, 1023:1024], small[:, 0:1], ACT.Copy).then_inc(rotT_ready, 1)
            act.wait_ge(rotT_ready, 1)
            act.wait_ge(max_ready, 1)
            for g in range(16):
                a = att[:, g * P:(g + 1) * P] if g < 8 else att[:, 1024 + (g - 8) * S:1024 + (g - 7) * S]
                A.activation(a, a, ACT.Exp, bias=hmax[:, g:g + 1], accum_out=hsum[:, g:g + 1]).then_inc(exp_ready, 1)
            for b in range(6):
                act.wait_ge(pT_psum, b + 1)
                A.activation(attT[:, b * 512:(b + 1) * 512], ps[:, b, :], ACT.Copy).then_inc(pT_ready, 1)
            root(16)
            act.wait_ge(rotT_psum, 2)
            did(A.activation(rqT, ps[:, 0, :].rearrange("p (h t) -> p h t", h=2), ACT.Copy))
            did(A.activation(rkT, ps[:, 1, :].rearrange("p (h t) -> p h t", h=2), ACT.Copy))
            settle()
            A.activation(small[:, 1023:1024], small[:, 0:1], ACT.Copy).then_inc(rotT_ready, 1)
            root(8)
            copy_rows_t(V_GM)
            root(TT)
            copy_rows_t(V_G2)
            act.wait_ge(hT_ready, 3 * KC)
            for k in range(KC):
                A.activation(h2_hi[:, k, :], hT[:, k, :], ACT.Copy).then_inc(h2_hi_ready, 1)
            for b in range(4):
                act.wait_ge(pq_psum, b + 1)
                A.activation(pqT[:, 2 * b:2 * b + 2, :], ps[:, 4 + b, :].rearrange("p (h t) -> p h t", h=2),
                             ACT.Copy).then_inc(pq_ready, 1)
            for t in range(TT):
                act.wait_ge(sc_psum, t + 1)
                for b in range(4):
                    A.activation(sc[:, t, b // 2, 4 * (b % 2):4 * (b % 2) + 4, :],
                                 ps[:, 4 * t + b, :].rearrange("p (h n) -> p h n", h=4), ACT.Copy).then_inc(sc_ready, 1)

            def high(n, s, turn, guard=True):
                act.wait_ge(raw_in[s], 16 * turn + 16)
                for h in range(2):
                    if guard:
                        act.wait_ge(half_used, 2 * n + h - 3)
                    A.activation(w_hi[:, 2 * (s % 2) + h, :], raw[:, s, h * HALF:(h + 1) * HALF], ACT.Copy)\
                        .then_inc(hi_ready, 1)

            def keys_turn(t, groups=None, first=False, first_group=False):
                for s in range(UN):
                    n = UN * t + s
                    high(n + 1, (s + 1) % UN, t + (s + 1) // UN, guard=not (first and s == 0))
                    if s % 2 == 0 and not first:
                        act.wait_ge(spilled[s // 2], 16 * t)
                    act.wait_ge(half_used, 2 * n + 2)
                    A.activation(acts[:, s, :], ps[:, s % 2, 0:S], ACT.Gelu_apprx_tanh).then_inc(act_ready, 1)
                    if groups is not None and not (first_group and s == 0):
                        group_out(groups + s - 1, (s - 1) % 2)

            def group_out(g, b):
                act.wait_ge(group_psum, g + 1)
                A.activation(routing[:, bass.ds(g * GT, GT), :], ps[:, 2 + b, :].rearrange("p (t i) -> p t i", t=GT),
                             ACT.Copy).then_inc(group_done, 1)

            high(0, 0, 0, guard=False)
            keys_turn(0, first=True)
            with act.Fori(1, EXP_TURN) as t:
                keys_turn(t)
            act.wait_ge(diff_ready, 1)
            for t in range(TT):
                A.activation(rows[:, t, 2, :], rows[:, t, 2, :], ACT.Exp).then_inc(gate_exp, 1)
            with act.Fori(EXP_TURN, ROUTE_TURN) as t:
                keys_turn(t)
            act.wait_ge(route_psum, 1)
            for t in range(TT):
                A.activation(route_t[:, :, t * P:(t + 1) * P], ps[:, 4 + t, 0:3 * P].rearrange("p (a t) -> p a t", a=3),
                             ACT.Copy).then_inc(route_ready, 1)
            with act.Fori(ROUTE_TURN, G_TURN0) as t:
                keys_turn(t)
            keys_turn(G_TURN0, groups=0, first_group=True)
            with act.Fori(G_TURN0 + 1, TURNS) as t:
                keys_turn(t, groups=UN * t - UN * G_TURN0)
            group_out(S // GT - 1, 1)
            with act.Fori(TURNS, 2 * TURNS - 1) as t:
                for s in range(UN):
                    high(UN * t + s + 1, (s + 1) % UN, t + (s + 1) // UN)
            for s in range(UN - 1):
                high(2 * NT - UN + s + 1, s + 1, 2 * TURNS - 1)

        @block.gpsimd
        def _(pool):
            def low(t):
                for s in range(UN):
                    for h in range(2):
                        pool.wait_ge(hi_ready, 8 * t + 2 * s + h + 1)
                        slot = 2 * (s % 2) + h
                        nc.gpsimd.tensor_tensor(w_lo[:, slot, :], raw[:, s, h * HALF:(h + 1) * HALF],
                                                w_hi[:, slot, :].bitcast(F32), ALU.subtract).then_inc(lo_ready, 1)

            with pool.Fori(0, 2 * TURNS) as t:
                low(t)


def host_constants():
    f = np.float32
    pos = np.arange(S, dtype=f)
    inv = (f(500000.0) ** (-np.arange(0, ROPE, 2, dtype=f) / f(ROPE))).astype(f)
    ang = pos[:, None] * inv[None, :]
    lin = np.linspace(0.0, 1.0, HD // 2, dtype=f)
    rang = pos[:, None] * (f(10000.0) ** (-lin)).astype(f)[None, :]
    tile = lambda a: a.astype(f).reshape(TT, P, -1).transpose(1, 0, 2).reshape(P, -1)
    consts = np.concatenate([np.eye(P, dtype=f), np.broadcast_to(np.arange(P, dtype=f), (P, P)),
                             tile(np.cos(ang)), tile(np.sin(ang)), tile(np.cos(rang)), tile(np.sin(rang))], axis=1)
    log_g = np.log(1.0 - 2.0 ** (-5.0 - np.arange(RH, dtype=np.float64)))
    diff = np.arange(S)[None, :] - np.arange(P)[:, None]
    decay = np.where(diff[:, None, :] >= 0, np.exp(np.maximum(diff, 0)[:, None, :] * log_g[None, :, None]), 0.0)
    decay = (decay * HD ** -0.5).astype(f)
    mask = np.zeros((P, S), f)
    mask[:, P:] = np.where(np.arange(P)[None, :] <= np.arange(P)[:, None], 0.0, MASKED)
    return np.ascontiguousarray(consts), decay, mask


def layout(inputs):
    a = {k: np.asarray(v)[0] if k != "x" else np.asarray(v) for k, v in inputs.items()}
    f = np.float32
    per = lambda v_, n: v_.reshape(n, P).T
    rep = lambda v_: np.broadcast_to(v_, (P, HD))
    vecs = np.concatenate([
        per(a["norm1_g"], KC), per(a["norm2_g"], KC), per(a["mix_out_g"], KC),
        per(a["s5_lam_re"].reshape(-1), S5_T), per(a["s5_lam_im"].reshape(-1), S5_T),
        per(np.repeat(a["s5_log_dt"], S5_STATE), S5_T), per(a["s5_d"], S5_C),
        rep(a["moba_q_g"]), rep(a["moba_k_g"])], axis=1)
    b = np.zeros((P, 2, S5_T, 32), f)
    c = np.zeros((P, 2, S5_T, 32), f)
    for r, (bn, cn) in enumerate((("s5_b_re", "s5_c_re"), ("s5_b_im", "s5_c_im"))):
        for o in range(2):
            rows, at = slice(64 * o, 64 * o + 64), slice(16 * o, 16 * o + 16)
            b[rows, r, :, at] = a[bn][o::2].transpose(1, 0, 2)
            c[rows, r, :, at] = a[cn][o::2].transpose(2, 0, 1)
    consts, decay, mask = host_constants()
    u_t = a["peer_u"].reshape(NT, P, KC, P).transpose(0, 3, 2, 1).reshape(NT, P, D)
    keys = a["peer_sub_keys"].transpose(1, 3, 0, 2).reshape(P, PH, NKEY)
    return {
        "x": a["x"][0], "w_in": a["w_in"], "vecs": vecs, "consts": consts, "decay": decay, "mask": mask,
        "s5_b": b.reshape(P, -1), "s5_c": c.reshape(P, -1), "w_glu": a["s5_w_glu"], "w_out": a["w_out"],
        "w_q": a["peer_w_q"], "keys": keys, "u_t": u_t, "v": a["peer_v"].reshape(NT, P, D),
    }


_OUT = (S, D)


def kernel(**inputs):
    import concourse.bacc as _bacc
    from concourse.bass_utils import run_bass_kernel_spmd as _run

    nc = _bacc.Bacc("TRN2", target_bir_lowering=False, num_devices=1)
    arrays, args = {}, {}
    for name, a in layout(inputs).items():
        a = np.ascontiguousarray(a)
        arrays[f"in_{name}"] = a
        args[name] = nc.dram_tensor(f"in_{name}", a.shape, mybir.dt.from_np(a.dtype), kind="ExternalInput").ap()
    args["out"] = nc.dram_tensor("out_0", _OUT, F32, kind="ExternalOutput").ap()
    args["spill"] = nc.dram_tensor("act_spill", (NT // 2, P, 2 * S), F32, kind="Internal").ap()
    build(nc, **args)
    r = _run(nc, [arrays], core_ids=[0])
    return r.results[0]["out_0"].reshape(1, S, D)
```

```python
from contextlib import ExitStack

import numpy as np

import concourse.bass as bass
from concourse import mybir

F32 = mybir.dt.float32
F32R = mybir.dt.float32r
U32 = mybir.dt.uint32
ALU = mybir.AluOpType
ACT = mybir.ActivationFunctionType
AX = mybir.AxisListType

P = 128
S = 256
TT = S // P
D = 1024
KC = D // P
EPS = 1e-6

S5_CH, S5_GROUP, S5_STATE = 256, 16, 64
S5_NG = S5_CH // S5_GROUP
S5_T = S5_NG * S5_STATE // P
S5_C = S5_CH // P
SEG = P
SEG_LOG = 7

HD = 64
MH, MW = 8, 512
RH, RW = 4, 256
ROPE = HD // 4
SCALE = HD ** -0.5
MASKED = -1e30

NKEY = 128
EXPERTS = NKEY * NKEY
PH, PK = 8, 16
HK = PH * PK
NT = EXPERTS // P

CHUNK = 512
W_SLOTS = 3

TAIL = 4 * KC
UN = 4
TURNS = NT // UN
HALF = D // 2
GT = 4
G_TURN0 = TURNS - S // GT // UN
EXP_TURN, ROUTE_TURN = 12, 14
LOWEST = -3e38

TWO_PI = 2 * np.pi
RC1 = 6.28125
RC2 = float(np.array([np.float32(TWO_PI - RC1)]).view(np.uint32).__and__(np.uint32(0xFFFFF000)).view(np.float32)[0])
RC3 = float(TWO_PI - RC1 - RC2)
ROUND = 1.5 * 2.0 ** 23
PI_LOW = 3.1415925

V_G1, V_G2, V_GM = 0, 8, 16
V_LR, V_LI, V_LDT = 24, 32, 40
V_D = 48
V_GQK = 50
V_N = V_GQK + 2 * HD
C_ID, C_IOTA = 0, P
C_N = 2 * P
C_RC = 0
C_RS = C_RC + TT * (ROPE // 2)
C_TC = C_RS + TT * (ROPE // 2)
C_TS = C_TC + TT * (HD // 2)
ROT_N = C_TS + TT * (HD // 2)


class Chain:

    def __init__(self, eng, sem):
        self.eng, self.sem, self.n = eng, sem, 0

    def did(self, ins):
        self.n += 1
        ins.then_inc(self.sem, 1)

    def settle(self):
        self.eng.wait_ge(self.sem, self.n)


def build(nc, x, w_in, vecs, consts, rots, decay, mask, s5_b, s5_c, w_glu, w_out, w_q, keys, u_t, v, out, spill):
    with ExitStack() as ctx:
        def sb(name, shape, dt=F32):
            return ctx.enter_context(nc.sbuf_tensor(name, shape, dt))

        def sem(name):
            return ctx.enter_context(nc.semaphore(name))

        xs = sb("xs", [P, TT, D])
        vec = sb("vec", [P, V_N])
        con = sb("con", [P, C_N])
        small = sb("small", [P, 512])
        routing = sb("routing", [P, S, NKEY])
        h_hi = sb("h_hi", [P, KC, S], F32R)
        h_lo = sb("h_lo", [P, KC, S], F32R)
        raw = sb("raw", [P, UN, D])
        w_hi = sb("w_hi", [P, 4, HALF], F32R)
        w_lo = sb("w_lo", [P, 4, HALF], F32R)
        acts = sb("acts", [P, UN, S])
        hot_j = sb("hot_j", [P, 2, GT, NKEY], F32R)
        hot_hi = sb("hot_hi", [P, 2, GT, NKEY], F32R)
        hot_lo = sb("hot_lo", [P, 2, GT, NKEY], F32R)
        route_t = sb("route_t", [P, 4, S])
        weighted = route_t[:, 0:2, :]
        ps = ctx.enter_context(nc.psum_tensor("ps", [P, 8, 512], F32))

        ident = con[:, C_ID:C_ID + P]
        iota = con[:, C_IOTA:C_IOTA + P]

        arena = routing[:].rearrange("p a b -> p (a b)")
        cursor = [0]

        def take(n):
            a = cursor[0]
            cursor[0] += n
            assert cursor[0] <= S * NKEY, cursor[0]
            return arena[:, a:a + n]

        w_ring = [take(KC * CHUNK).rearrange("p (k n) -> p k n", k=KC) for _ in range(W_SLOTS)]
        hT = take(KC * S).rearrange("p (k t) -> p k t", k=KC)
        done_proj = hT.rearrange("p k t -> p (k t)")
        xn = take(TT * D).rearrange("p (t d) -> p t d", t=TT)
        qk = take(TT * 2 * MW).rearrange("p (t d) -> p t d", t=TT)
        mv = take(TT * MW).rearrange("p (t d) -> p t d", t=TT)
        ret = take(TT * 4 * RW).rearrange("p (t d) -> p t d", t=TT)
        uT = take(S5_C * S).rearrange("p (c t) -> p c t", c=S5_C)
        ymix = take(TT * D).rearrange("p (t d) -> p t d", t=TT)
        rot_tmp = ymix.rearrange("p t d -> p (t d)")
        region = cursor[0]
        r3 = lambda a, k: a.rearrange("p (k t) -> p k t", k=k)
        pc, pS = (r3(take(S5_T * SEG), S5_T) for _ in range(2))
        zr, zi = (r3(take(S5_T * S), S5_T) for _ in range(2))
        xr = xn.rearrange("p t d -> p (t d)").rearrange("p (j t) -> p j t", j=S5_T)
        att1 = take(MH * S).rearrange("p (g k) -> p g k", g=MH)
        att0 = ymix[:, :, S5_CH:S5_CH + MW].rearrange("p t (g k) -> p t g k", g=4)
        qk_flat = qk.rearrange("p t d -> p (t d)")
        mqT = qk_flat[:, 0:1024].rearrange("p (h t) -> p h t", h=4)
        mkT = qk_flat[:, 1024:2048].rearrange("p (h t) -> p h t", h=4)
        rqT = ret[:, 0, 0:2 * RW].rearrange("p (h t) -> p h t", h=2)
        rkT = ret[:, 1, 0:2 * RW].rearrange("p (h t) -> p h t", h=2)
        rP0 = qk_flat[:, 0:1024].rearrange("p (h t) -> p h t", h=RH)
        rP1 = qk_flat[:, 1024:1536].rearrange("p (h t) -> p h t", h=RH)
        tables = w_ring[1].rearrange("p k n -> p (k n)")
        keys_s = tables[:, 1024:2048].rearrange("p (h n) -> p h n", h=PH)
        cursor[0] = W_SLOTS * KC * CHUNK + 2 * KC * S
        pqT = take(PH * S).rearrange("p (h t) -> p h t", h=PH)
        sc = take(TT * 2 * PH * NKEY).rearrange("p (t c h n) -> p t c h n", t=TT, c=2, h=PH)
        work = take(2 * PH * NKEY).rearrange("p (c h n) -> p c h n", c=2, h=PH)
        work2 = take(2 * PH * NKEY)
        work3 = take(2 * PH * NKEY)
        rawf = raw[:].rearrange("p a b -> p (a b)")
        mask_s = rawf[:, 0:S]
        rot = rawf[:, 256:256 + ROT_N]
        u_tok = rawf[:, 512:1024].rearrange("p (t d) -> p t d", t=TT)
        glu_s = rawf[:, 1280:1280 + S5_C * S5_CH].rearrange("p (c n) -> p c n", c=S5_C)
        bT = rawf[:, 1792:1792 + 4 * P].rearrange("p (a s) -> p a s", a=4)
        b_s = rawf[:, 2304:2304 + 512].rearrange("p (r j c) -> p r j c", r=2, j=S5_T)
        c_s = rawf[:, 2816:2816 + 512].rearrange("p (r j c) -> p r j c", r=2, j=S5_T)
        bb = rawf[:, 3328:3328 + 512].rearrange("p (r j c) -> p r j c", r=2, j=S5_T)
        decay_s = acts[:]
        hj = route_t[:].rearrange("p a b -> p (a b)")
        tmp1 = hj.rearrange("p (j t) -> p j t", j=4)
        x_in, params_in, consts_in = sem("x_in"), sem("params_in"), sem("consts_in")
        w_in_sem = [sem(f"weights_in{i}") for i in range(W_SLOTS)]
        keys_in = sem("keys_in")
        dve_steps, act_steps, pool_steps = sem("dve_steps"), sem("act_steps"), sem("pool_steps")
        sumsq_x, var_ready, std_ready, xn_ready = sem("sumsq_x"), sem("var_ready"), sem("std_ready"), sem("xn_ready")
        rx_ready = sem("rstd_x_ready")
        t_psum, hT_ready = sem("transposes_in_psum"), sem("hT_ready")
        dt_ready, expo_ready, mag_ready = sem("dt_ready"), sem("exponent_ready"), sem("mag_ready")
        ang_ready, trig_ready = sem("angles_ready"), sem("trig_ready")
        bb_ready, bT_psum, bT_ready = sem("bb_ready"), sem("bT_in_psum"), sem("bT_ready")
        u_psum, u_tok_ready, uT_psum, u_ready = sem("u_in_psum"), sem("u_tok_ready"), sem("u_t_in_psum"), sem("u_ready")
        bu_psum, bu_used, drive_ready = sem("bu_in_psum"), sem("bu_used"), sem("drive_ready")
        proj_psum, proj_ready = sem("proj_in_psum"), sem("proj_ready")
        states_ready, y_psum, y_lin, y_ready = sem("states_ready"), sem("y_in_psum"), sem("y_linear"), sem("y_ready")
        glu_psum, gate_ready, ya_ready, yaT_psum = sem("glu_in_psum"), sem("glu_gate_ready"), sem("ya_ready"), sem("ya_t_in_psum")
        qk_sq = sem("qk_squares")
        rot_ready, ret_rot_ready = sem("rotated_ready"), sem("ret_rotated_ready")
        rotT_psum, rotT_ready = sem("rotated_t_in_psum"), sem("rotated_t_ready")
        retT_psum, retT_ready = sem("ret_rotated_t_in_psum"), sem("ret_rotated_t_ready")
        s_psum, s_read, max_ready, exp_ready = sem("scores_in_psum"), sem("scores_read"), sem("max_ready"), sem("exp_ready")
        pT_psum, pT_ready = sem("probs_t_in_psum"), sem("probs_t_ready")
        o_psum, ret_o_psum = sem("moba_out_in_psum"), sem("ret_out_in_psum")
        rs_psum, rp_ready, silu_ready = sem("ret_scores_in_psum"), sem("ret_probs_ready"), sem("silu_ready")
        mix_ready, sum2_ready, sumsq_2 = sem("mix_ready"), sem("residual_ready"), sem("sumsq_2")
        th_ready, tl_ready = sem("transposed_high_ready"), sem("transposed_low_ready")
        pq_ready, sc_psum, sc_ready = sem("pq_ready"), sem("keys_scores_in_psum"), sem("keys_scores_ready")
        raw_in = [sem(f"raw_in{i}") for i in range(UN)]
        hi_ready, lo_ready = sem("hi_ready"), sem("lo_ready")
        half_used = sem("half_used")
        act_ready = sem("act_ready")
        spilled = [sem("spilled0"), sem("spilled1")]
        acts_in = [sem("acts_in0"), sem("acts_in1")]
        diff_ready, gate_exp = sem("gate_exponents_ready"), sem("gate_exp_ready")
        tok_ready, route_psum, route_ready = sem("route_rows_ready"), sem("route_t_in_psum"), sem("route_t_ready")
        hot_ready, group_psum, group_done = sem("one_hots_ready"), sem("group_in_psum"), sem("group_done")
        w_steps, w_ready, product_done = sem("weighted_steps"), sem("weighted_ready"), sem("product_done")
        sum_ready, stored = sem("sum_ready"), sem("stored")

        V = nc.vector
        A = nc.scalar

        def cols(off, n):
            return vec[:, off:off + n]

        def sm(off, n):
            return small[:, off:off + n]

        o = [0]

        def tiny(n):
            a = sm(o[0], n)
            o[0] += n
            assert o[0] <= 512, o[0]
            return a

        ss_x, ss_2, rx, rstd = tiny(TT), tiny(4), tiny(TT), tiny(32)
        dt, expo, mag, ang, kk, s1, c1, half = (tiny(8) for _ in range(8))
        ar, ai, den, fr, fi, q1, q2, q3 = (tiny(8) for _ in range(8))
        z0r, z0i, sums = tiny(8), tiny(8), tiny(32)
        sq_c, sq_s = tiny(64).rearrange("p (n j) -> p n j", j=8), tiny(64).rearrange("p (n j) -> p n j", j=8)
        std = tiny(32)
        hmax, hsum = tiny(16), tiny(16)

        in_cols = [(0, S5_CH), (256, 768), (768, 1280), (1792, 2304), (2304, 2816), (1280, 1792)]
        w_src = [w_in[:, a:b] for a, b in in_cols]
        w_src += [w[:, CHUNK * n:CHUNK * (n + 1)] for w in (w_out, w_q) for n in range(2)]
        W_N = len(w_src)
        top = tables[:, 0:256].rearrange("p (c h k) -> p c h k", c=2, h=PH)
        idx = tables[:, 256:512].bitcast(U32).rearrange("p (c h k) -> p c h k", c=2, h=PH)
        pos = tables[:, 512:640].bitcast(U32).rearrange("p (h k) -> p h k", h=PH)
        tab = hT.rearrange("p k t -> p (k t)")
        rows = tab[:, 0:768].rearrange("p (t a k) -> p t a k", t=TT, a=3)
        idx_f = tab[:, 768:1024].rearrange("p (c h k) -> p c h k", c=2, h=PH)
        ab = tab[:, 1024:1280].bitcast(U32).rearrange("p (c h k) -> p c h k", c=2, h=PH)
        ab_f = tab[:, 1280:1536].rearrange("p (c h k) -> p c h k", c=2, h=PH)
        top2 = tab[:, 1536:1664].rearrange("p (h k) -> p h k", h=PH)
        gsum = tab[:, 1664:1680].rearrange("p (t h) -> p t h", t=TT)
        block = ctx.enter_context(nc.Block())

        @block.sync
        def _(sp):
            sp.dma_start(xs[:], x.rearrange("(t p) d -> p t d", p=P)).then_inc(x_in, 16)
            sp.dma_start(con[:], consts).then_inc(x_in, 16)
            sp.dma_start(vec[:], vecs).then_inc(params_in, 16)
            sp.dma_start(rawf[:, 2304:2816], s5_b).then_inc(params_in, 16)
            for n in range(W_N):
                if n == 2:
                    sp.dma_start(rot, rots).then_inc(consts_in, 16)
                    sp.dma_start(rawf[:, 2816:3328], s5_c).then_inc(consts_in, 16)
                    sp.dma_start(glu_s, w_glu.rearrange("(c p) n -> p c n", p=P)).then_inc(consts_in, 16)
                    sp.dma_start(mask_s, mask).then_inc(consts_in, 16)
                    sp.dma_start(decay_s, decay).then_inc(consts_in, 16)
                old = n - W_SLOTS
                if old == 0:
                    sp.wait_ge(u_psum, 1)
                elif 0 < old <= 5:
                    sp.wait_ge(proj_psum, TT * old)
                elif old > 5:
                    sp.wait_ge(lo_ready, KC * (old - 5))
                width = w_src[n].shape[1]
                sp.dma_start(w_ring[n % W_SLOTS][:, :, 0:width],
                             w_src[n].rearrange("(k p) n -> p k n", p=P)).then_inc(w_in_sem[n % W_SLOTS], 16)

            def load_tile(weights, tile, s):
                sp.dma_start(raw[:, s, :], weights[tile]).then_inc(raw_in[s], 16)

            sp.wait_ge(mix_ready, 1)
            for s in range(UN):
                load_tile(u_t, s, s)
            sp.wait_ge(lo_ready, 2 * KC)
            sp.dma_start(keys_s, keys).then_inc(keys_in, 16)

            def keys_turn(t, weights, nxt, store):
                for s in range(UN):
                    sp.wait_ge(lo_ready, TAIL + 8 * t + 2 * s + 2)
                    load_tile(weights, nxt + s, s)
                    if store and s % 2:
                        sp.wait_ge(act_ready, UN * t + s + 1)
                        sp.dma_start(spill[2 * t + s // 2], acts[:, s - 1:s + 1, :].rearrange("p a t -> p (a t)"))\
                            .then_inc(spilled[s // 2], 16)

            with sp.Fori(0, TURNS - 1) as t:
                keys_turn(t, u_t, UN * t + UN, True)
            keys_turn(TURNS - 1, v, NT - UN, False)

            for b in range(2):
                sp.wait_ge(spilled[b], 16 * (TURNS - 1))
            with sp.Fori(0, TURNS - 1) as t:
                for s in range(UN):
                    sp.wait_ge(lo_ready, TAIL + 2 * NT + 8 * t + 2 * s + 2)
                    load_tile(v, UN * t + s, s)
                    if s % 2:
                        sp.wait_ge(product_done, UN * t + s + 1)
                        sp.dma_start(acts[:, s - 1:s + 1, :].rearrange("p a t -> p (a t)"), spill[2 * t + s // 2])\
                            .then_inc(acts_in[s // 2], 16)
            for n in range(2 * TT):
                sp.wait_ge(sum_ready, n + 1)
                h, t = n // TT, n % TT
                sp.dma_start(out[t * P:(t + 1) * P, h * HALF:(h + 1) * HALF],
                             xs[:, t, h * HALF:(h + 1) * HALF]).then_inc(stored, 16)
            sp.wait_ge(stored, 16 * 2 * TT)

        @block.tensor
        def _(pe):
            def chunk_in(n):
                pe.wait_ge(w_in_sem[n % W_SLOTS], 16 * (n // W_SLOTS + 1))
                return w_ring[n % W_SLOTS]

            def transpose_rows(src):
                for k in range(KC):
                    for t in range(TT):
                        mm = pe.transpose(ps[:, k // 2, (k % 2) * S + t * P:(k % 2) * S + (t + 1) * P],
                                          src[:, t, k * P:(k + 1) * P], ident)
                    if k % 2:
                        mm.then_inc(t_psum, 1)

            def project(n, t):
                w = chunk_in(n)
                if n >= 3:
                    pe.wait_ge(proj_ready, 2 * (n - 3) + t + 1)
                for k in range(KC):
                    mm = pe.matmul(ps[:, 2 * ((n - 1) % 2) + t, :], hT[:, k, t * P:(t + 1) * P], w[:, k, :],
                                   start=(k == 0), stop=(k == KC - 1))
                mm.then_inc(proj_psum, 1)

            def drive(c):
                for r in range(2):
                    for j in range(4):
                        mm = pe.matmul(ps[:, 4 + j, r * S:(r + 1) * S],
                                       bT[32 * j:32 * j + 32, r * 2 + c, :], uT[32 * j:32 * j + 32, c, :],
                                       start=True, stop=True)
                mm.then_inc(bu_psum, 1)

            pe.wait_ge(x_in, 32)
            transpose_rows(xs)
            w = chunk_in(0)
            pe.wait_ge(hT_ready, KC)
            for t in range(TT):
                for k in range(KC):
                    mm = pe.matmul(ps[:, 4, t * S5_CH:(t + 1) * S5_CH], hT[:, k, t * P:(t + 1) * P], w[:, k, 0:S5_CH],
                                   start=(k == 0), stop=(k == KC - 1))
            mm.then_inc(u_psum, 1)
            project(1, 0)
            pe.wait_ge(u_tok_ready, TT)
            for c in range(S5_C):
                for t in range(TT):
                    mm = pe.transpose(ps[:, 5, c * S + t * P:c * S + (t + 1) * P], u_tok[:, t, c * P:(c + 1) * P], ident)
            mm.then_inc(uT_psum, 1)
            pe.wait_ge(bb_ready, 1)
            for r in range(2):
                for c in range(S5_C):
                    mm = pe.transpose(ps[:, 6, (r * 2 + c) * P:(r * 2 + c + 1) * P],
                                      bb[:, r, 4 * c:4 * c + 4, :].rearrange("p j c -> p (j c)"), ident)
            mm.then_inc(bT_psum, 1)
            project(1, 1)
            pe.wait_ge(u_ready, 1)
            pe.wait_ge(bT_ready, 1)
            drive(0)
            project(2, 0)
            project(2, 1)
            pe.wait_ge(bu_used, 1)
            drive(1)
            project(3, 0)
            project(3, 1)

            pe.wait_ge(bu_used, 2)
            pe.wait_ge(rot_ready, 1)
            for a in range(2):
                for h in range(4):
                    for t in range(TT):
                        mm = pe.transpose(ps[:, 4 + 2 * a + h // 2, (h % 2) * S + t * P:(h % 2) * S + (t + 1) * P],
                                          qk[:, t, a * MW + h * P:a * MW + (h + 1) * P], ident)
            mm.then_inc(rotT_psum, 1)
            project(4, 0)
            pe.wait_ge(rotT_ready, 2)
            for h in range(4):
                for o_ in range(2):
                    r = slice(HD * o_, HD * (o_ + 1))
                    mm = pe.matmul(ps[:, 4 + 2 * o_ + h // 2, (h % 2) * S:(h % 2 + 1) * S], mqT[r, h, P:S], mkT[r, h, :],
                                   start=True, stop=True)
            mm.then_inc(s_psum, 1)
            project(4, 1)
            pe.wait_ge(s_read, 1)
            for h in range(4):
                for o_ in range(2):
                    r = slice(HD * o_, HD * (o_ + 1))
                    mm = pe.matmul(ps[:, 4 + o_, h * P:(h + 1) * P], mqT[r, h, 0:P], mkT[r, h, 0:P], start=True, stop=True)
            mm.then_inc(s_psum, 1)
            project(5, 0)
            def turn(bank, blocks):
                for h, src in enumerate(blocks):
                    mm = pe.transpose(ps[:, bank, h * P:(h + 1) * P], src, ident)
                mm.then_inc(pT_psum, 1)

            pe.wait_ge(exp_ready, 8)
            for b in range(2):
                turn(6 + b, [att1[:, 4 * b + h, 0:P] for h in range(4)])
            project(5, 1)
            pe.wait_ge(ret_rot_ready, 1)
            pe.wait_ge(proj_ready, 8)
            for a in range(2):
                for h in range(2):
                    for t in range(TT):
                        mm = pe.transpose(ps[:, 2 + a, h * S + t * P:h * S + (t + 1) * P],
                                          ret[:, t, a * RW + h * P:a * RW + (h + 1) * P], ident)
            mm.then_inc(retT_psum, 1)
            pe.wait_ge(s_read, 2)
            for b in range(2):
                turn(4 + b, [att1[:, 4 * b + h, P:S] for h in range(4)])
            pe.wait_ge(exp_ready, 16)
            pe.wait_ge(pT_ready, 2)
            for b in range(2):
                turn(6 + b, [att0[:, b, h, :] for h in range(4)])
            pe.wait_ge(proj_ready, 10)
            pe.wait_ge(retT_ready, 2)
            for h in range(2):
                for o_ in range(2):
                    r = slice(HD * o_, HD * (o_ + 1))
                    pe.matmul(ps[:, o_, h * S:(h + 1) * S], rkT[r, h, 0:P], rqT[r, h, :], start=True, stop=True)
            for h in range(2):
                for o_ in range(2):
                    r = slice(HD * o_, HD * (o_ + 1))
                    mm = pe.matmul(ps[:, 2 + o_, h * P:(h + 1) * P], rkT[r, h, P:S], rqT[r, h, P:S], start=True, stop=True)
            mm.then_inc(rs_psum, 1)
            pe.wait_ge(pT_ready, 6)
            for h in range(MH):
                g = 4 * (h % 2) + h // 2
                c = slice(h * HD, (h + 1) * HD)
                pe.matmul(ps[:, 4, c], att0[:, g // 4, g % 4, :], mv[:, 0, c], start=True, stop=True)
                pe.matmul(ps[:, 5, c], att1[:, g, 0:P], mv[:, 0, c], start=True, stop=False)
                mm = pe.matmul(ps[:, 5, c], att1[:, g, P:S], mv[:, 1, c], start=False, stop=True)
            mm.then_inc(o_psum, 1)
            pe.wait_ge(consts_in, 80)
            pe.wait_ge(states_ready, 1)
            for c in range(S5_C):
                for j in range(4):
                    for r, st in ((0, xr), (1, zi)):
                        mm = pe.matmul(ps[32 * j:32 * j + 32, 6, c * S:(c + 1) * S], c_s[:, r, 4 * c + j, :],
                                       st[:, 4 * c + j, :], start=(r == 0), stop=(r == 1))
            mm.then_inc(y_psum, 1)
            pe.wait_ge(rp_ready, 1)
            for h in range(RH):
                vc = slice(2 * RW + h * HD, 2 * RW + (h + 1) * HD)
                pe.matmul(ps[:, 0, h * HD:(h + 1) * HD], rP0[:, h, 0:P], ret[:, 0, vc], start=True, stop=True)
                o1 = ps[:, 0, RW + h * HD:RW + (h + 1) * HD]
                pe.matmul(o1, rP0[:, h, P:S], ret[:, 0, vc], start=True, stop=False)
                mm = pe.matmul(o1, rP1[:, h, :], ret[:, 1, vc], start=False, stop=True)
            mm.then_inc(ret_o_psum, 1)
            pe.wait_ge(y_ready, 1)
            for m in range(S5_C):
                for c in range(S5_C):
                    mm = pe.matmul(ps[:, 7, m * S:(m + 1) * S], glu_s[:, c, m * P:(m + 1) * P], uT[:, c, :],
                                   start=(c == 0), stop=(c == S5_C - 1))
            mm.then_inc(glu_psum, 1)
            pe.wait_ge(ya_ready, 1)
            for t in range(TT):
                for c in range(S5_C):
                    mm = pe.transpose(ps[:, 6, t * S5_CH + c * P:t * S5_CH + (c + 1) * P], uT[:, c, t * P:(t + 1) * P], ident)
            mm.then_inc(yaT_psum, 1)

            def halves_product(dst, pairs, first, last):
                for i, (s_hi, s_lo, m_hi, m_lo) in enumerate(pairs):
                    end = last and i == len(pairs) - 1
                    pe.matmul(dst, s_hi, m_hi, start=first and i == 0, stop=False)
                    pe.matmul(dst, s_hi, m_lo, start=False, stop=False)
                    mm = pe.matmul(dst, s_lo, m_hi, start=False, stop=end)
                return mm

            pe.wait_ge(mix_ready, 1)
            transpose_rows(ymix)
            pe.wait_ge(th_ready, KC)
            pe.wait_ge(tl_ready, KC)
            for n in range(2):
                for k in range(KC):
                    pe.wait_ge(lo_ready, KC * n + k + 1)
                    for t in range(TT):
                        r = slice(t * P, (t + 1) * P)
                        mm = halves_product(ps[:, 4 + 2 * n + t, :],
                                            [(h_hi[:, k, r], h_lo[:, k, r], w_hi[:, k % 4, :], w_lo[:, k % 4, :])],
                                            k == 0, k == KC - 1)
                    mm.then_inc(half_used, 1)
            pe.wait_ge(xn_ready, TT)
            transpose_rows(xn)
            pe.wait_ge(th_ready, 2 * KC)
            pe.wait_ge(tl_ready, 2 * KC)
            for n in range(2):
                for k in range(KC):
                    pe.wait_ge(lo_ready, KC * (2 + n) + k + 1)
                    for h in range(4):
                        c = slice(h * P, (h + 1) * P)
                        mm = halves_product(ps[:, 4 * (1 - n) + h, 0:S],
                                            [(w_hi[:, k % 4, c], w_lo[:, k % 4, c], h_hi[:, k, :], h_lo[:, k, :])],
                                            k == 0, k == KC - 1)
                    mm.then_inc(half_used, 1)

            def key_scores(t):
                for h in range(PH):
                    for c in range(2):
                        r = slice(HD * c, HD * (c + 1))
                        mm = pe.matmul(ps[:, 4 + 2 * c + h // 4, (h % 4) * NKEY:(h % 4 + 1) * NKEY],
                                       pqT[r, h, t * P:(t + 1) * P], keys_s[r, h, :], start=True, stop=True)
                mm.then_inc(sc_psum, 1)

            def keys_turn(t, groups=None, first=False, first_group=False):
                for s in range(UN):
                    if not (first and s < 2):
                        pe.wait_ge(act_ready, UN * t + s - 1)
                    for h in range(2):
                        pe.wait_ge(lo_ready, TAIL + 8 * t + 2 * s + h + 1)
                        slot = 2 * (s % 2) + h
                        pairs = [(w_hi[:, slot, k * P:(k + 1) * P], w_lo[:, slot, k * P:(k + 1) * P],
                                  h_hi[:, 4 * h + k, :], h_lo[:, 4 * h + k, :]) for k in range(4)]
                        halves_product(ps[:, s % 2, 0:S], pairs, h == 0, h == 1).then_inc(half_used, 1)
                    if groups is not None:
                        g = groups + s
                        pe.wait_ge(hot_ready, g + 1)
                        if not (first_group and s < 2):
                            pe.wait_ge(group_done, g - 1)
                        for q in range(GT):
                            d_ = ps[:, 2 + s % 2, q * P:(q + 1) * P]
                            pe.matmul(d_, hot_j[:, s % 2, q, :], hot_hi[:, s % 2, q, :], start=True, stop=False)
                            mm = pe.matmul(d_, hot_j[:, s % 2, q, :], hot_lo[:, s % 2, q, :], start=False, stop=True)
                        mm.then_inc(group_psum, 1)

            pe.wait_ge(pq_ready, PH)
            keys_turn(0, first=True)
            pe.wait_ge(keys_in, 16)
            key_scores(0)
            keys_turn(1)
            pe.wait_ge(sc_ready, 4)
            key_scores(1)
            with pe.Fori(2, ROUTE_TURN) as t:
                keys_turn(t)
            pe.wait_ge(sc_ready, 8)
            pe.wait_ge(tok_ready, 1)
            for t in range(TT):
                for a in range(3):
                    mm = pe.transpose(ps[:, 4 + t, a * P:(a + 1) * P], rows[:, t, a, :], ident)
            mm.then_inc(route_psum, 1)
            with pe.Fori(ROUTE_TURN, G_TURN0) as t:
                keys_turn(t)
            keys_turn(G_TURN0, groups=0, first_group=True)
            with pe.Fori(G_TURN0 + 1, TURNS) as t:
                keys_turn(t, groups=UN * t - UN * G_TURN0)

            def values_turn(t, first=False, last=False):
                for s in range(UN):
                    pe.wait_ge(w_ready, UN * t + s + 1)
                    for h in range(2):
                        pe.wait_ge(lo_ready, TAIL + 2 * NT + 8 * t + 2 * s + h + 1)
                        slot = 2 * (s % 2) + h
                        for tt_ in range(TT):
                            r = slice(tt_ * P, (tt_ + 1) * P)
                            mm = halves_product(ps[:, 4 + 2 * h + tt_, :],
                                                [(h_hi[:, s, r], h_lo[:, s, r], w_hi[:, slot, :], w_lo[:, slot, :])],
                                                first and s == 0, last and s == UN - 1)
                        mm.then_inc(half_used, 1)

            pe.wait_ge(route_ready, 2 * TT)
            values_turn(0, first=True)
            with pe.Fori(1, TURNS - 1) as t:
                values_turn(t)
            values_turn(TURNS - 1, last=True)

        def rotation(src, heads, m, cos, sin, scratch):
            views = []
            for t in range(TT):
                x_ = src[:, t, 0:heads * HD].rearrange("p (h d) -> p h d", d=HD)
                size = heads * m
                ta, tb = (scratch[:, (2 * t + i) * size:(2 * t + i + 1) * size].rearrange("p (h d) -> p h d", h=heads)
                          for i in range(2))
                co, si = (rot[:, o_ + t * m:o_ + (t + 1) * m].unsqueeze(1).to_broadcast([P, heads, m]) for o_ in (cos, sin))
                views.append((x_[:, :, 0:m], x_[:, :, m:2 * m], co, si, ta, tb))
            return views

        @block.vector
        def _(dve):
            ch = Chain(dve, dve_steps)
            did, settle = ch.did, ch.settle
            n_var = [0]

            def step(ins):
                did(ins)
                settle()

            def tt(out_, a, b, op):
                return V.tensor_tensor(out_, a, b, op)

            def rstd_from(sums_, n, width, dst=rstd):
                V.tensor_scalar(std[:, 0:n], sums_, 1.0 / width, EPS, ALU.mult, ALU.add).then_inc(var_ready, 1)
                n_var[0] += 1
                dve.wait_ge(std_ready, n_var[0])
                return V.reciprocal(dst[:, 0:n], std[:, 0:n])

            dve.wait_ge(params_in, 32)
            for k in range(4, KC):
                dve.wait_ge(t_psum, k // 2 + 1)
                V.tensor_scalar(hT[:, k, :], ps[:, k // 2, (k % 2) * S:(k % 2 + 1) * S], cols(V_G1 + k, 1), None,
                                ALU.mult).then_inc(hT_ready, 1)
            dve.wait_ge(sumsq_x, TT)
            rstd_from(ss_x, TT, D, rx).then_inc(rx_ready, 1)

            lr, li = cols(V_LR, 8), cols(V_LI, 8)
            dve.wait_ge(dt_ready, 1)
            tt(expo, lr, dt, ALU.mult).then_inc(expo_ready, 1)
            step(tt(ang, li, dt, ALU.mult))
            step(V.tensor_scalar(kk, ang, float(1 / TWO_PI), ROUND, ALU.mult, ALU.add))
            step(V.tensor_scalar(kk, kk, -ROUND, None, ALU.add))
            for part in (RC1, RC2, RC3):
                step(V.scalar_tensor_tensor(ang, kk, -part, ang, ALU.mult, ALU.add))
            step(V.tensor_scalar(ang, ang, -PI_LOW, PI_LOW, ALU.max, ALU.min))
            step(V.tensor_scalar(half, ang, -1.0, None, ALU.mult))
            step(tt(half, half, ang, ALU.min))
            V.tensor_scalar(half, half, float(np.pi / 2), None, ALU.add).then_inc(ang_ready, 1)
            did(tt(q1, lr, lr, ALU.mult))
            did(tt(q2, li, li, ALU.mult))
            settle()
            step(tt(den, q1, q2, ALU.add))
            did(V.reciprocal(den, den))
            dve.wait_ge(mag_ready, 1)
            dve.wait_ge(trig_ready, 1)
            did(tt(ar, mag, c1, ALU.mult))
            did(tt(ai, mag, s1, ALU.mult))
            settle()
            step(V.tensor_scalar(ar, ar, -1.0, None, ALU.add))
            did(tt(q1, ar, lr, ALU.mult))
            did(tt(q2, ai, li, ALU.mult))
            did(tt(q3, ai, lr, ALU.mult))
            did(tt(kk, ar, li, ALU.mult))
            settle()
            did(tt(fr, q1, q2, ALU.add))
            did(tt(fi, q3, kk, ALU.subtract))
            settle()
            did(tt(fr, fr, den, ALU.mult))
            did(tt(fi, fi, den, ALU.mult))
            settle()
            wide = lambda a: a.unsqueeze(2).to_broadcast([P, S5_T, 32])
            t_a = hj[:, 0:256].rearrange("p (j c) -> p j c", j=S5_T)
            t_b = hj[:, 256:512].rearrange("p (j c) -> p j c", j=S5_T)
            did(tt(bb[:, 0], b_s[:, 0], wide(fr), ALU.mult))
            did(tt(t_a, b_s[:, 1], wide(fi), ALU.mult))
            did(tt(bb[:, 1], b_s[:, 1], wide(fr), ALU.mult))
            did(tt(t_b, b_s[:, 0], wide(fi), ALU.mult))
            settle()
            did(tt(bb[:, 0], bb[:, 0], t_a, ALU.subtract))
            settle()
            tt(bb[:, 1], bb[:, 1], t_b, ALU.add).then_inc(bb_ready, 1)
            dve.wait_ge(bb_ready, 1)

            did(V.tensor_copy(sq_c[:, 0, :], c1))
            did(V.tensor_copy(sq_s[:, 0, :], s1))
            did(V.memset(pc[:, :, 0:1], 1.0))
            did(V.memset(pS[:, :, 0:1], 0.0))
            settle()
            for n in range(SEG_LOG + 1):
                m = 1 << n
                if n < SEG_LOG:
                    shape = [P, S5_T, m]
                    wc, ws = (a[:, n, :].unsqueeze(2).to_broadcast(shape) for a in (sq_c, sq_s))
                    lo_c, lo_s, hi_c, hi_s = pc[:, :, 0:m], pS[:, :, 0:m], pc[:, :, m:2 * m], pS[:, :, m:2 * m]
                    did(tt(hi_c, lo_c, wc, ALU.mult))
                    did(tt(zr[:, :, 0:m], lo_s, ws, ALU.mult))
                    did(tt(hi_s, lo_c, ws, ALU.mult))
                    did(tt(zi[:, :, 0:m], lo_s, wc, ALU.mult))
                    a, b = sq_c[:, n, :], sq_s[:, n, :]
                    did(tt(q1, a, a, ALU.mult))
                    did(tt(q2, b, b, ALU.mult))
                    did(tt(q3, a, b, ALU.mult))
                    settle()
                    did(tt(hi_c, hi_c, zr[:, :, 0:m], ALU.subtract))
                    did(tt(hi_s, hi_s, zi[:, :, 0:m], ALU.add))
                    did(tt(sq_c[:, n + 1, :], q1, q2, ALU.subtract))
                    did(V.tensor_scalar(sq_s[:, n + 1, :], q3, 2.0, None, ALU.mult))
                    settle()

            seg = lambda a: a.rearrange("p j (g s) -> p j g s", s=SEG)
            phase = lambda a, js: a[:, js].unsqueeze(2).to_broadcast([P, 4, S // SEG, SEG])
            for c in range(S5_C):
                js = slice(4 * c, 4 * c + 4)
                bur, bui = seg(ps[:, 4:8, 0:S]), seg(ps[:, 4:8, S:2 * S])
                dve.wait_ge(bu_psum, c + 1)
                did(tt(seg(zr[:, js]), bur, phase(pc, js), ALU.mult))
                did(tt(seg(tmp1), bui, phase(pS, js), ALU.mult))
                did(tt(seg(zi[:, js]), bui, phase(pc, js), ALU.mult))
                tt(seg(xr[:, js]), bur, phase(pS, js), ALU.mult).then_inc(bu_used, 1)
                dve.wait_ge(bu_used, c + 1)
                settle()
                did(tt(zr[:, js], zr[:, js], tmp1, ALU.add))
                tt(zi[:, js], zi[:, js], xr[:, js], ALU.subtract).then_inc(drive_ready, 1)
                dve.wait_ge(drive_ready, c + 1)
                settle()

            def scans(g, init):
                for j in range(S5_T):
                    for z, z0 in ((zr, z0r), (zi, z0i)):
                        zs = z[:, j, g * SEG:(g + 1) * SEG]
                        did(V.tensor_tensor_scan(zs, mag[:, j:j + 1].to_broadcast([P, SEG]), zs,
                                                 z0[:, j:j + 1] if init else 0.0, ALU.mult, ALU.add))
                settle()

            scans(0, False)
            er, ei = zr[:, :, SEG - 1], zi[:, :, SEG - 1]
            did(tt(q1, sq_c[:, SEG_LOG, :], er, ALU.mult))
            did(tt(q2, sq_s[:, SEG_LOG, :], ei, ALU.mult))
            did(tt(q3, sq_c[:, SEG_LOG, :], ei, ALU.mult))
            did(tt(kk, sq_s[:, SEG_LOG, :], er, ALU.mult))
            settle()
            did(tt(z0r, q1, q2, ALU.subtract))
            did(tt(z0i, q3, kk, ALU.add))
            settle()
            scans(1, True)

            dve.wait_ge(qk_sq, 1)
            sq = xn.rearrange("p t d -> p (t d)")
            qkh = qk_flat.rearrange("p (h d) -> p h d", d=HD)
            step(V.tensor_reduce(sums, sq.rearrange("p (h d) -> p h d", d=HD), AX.X, ALU.add))
            step(rstd_from(sums, 32, HD))
            step(tt(qkh, qkh, rstd[:, 0:32].unsqueeze(2).to_broadcast([P, 32, HD]), ALU.mult))
            for t in range(TT):
                for a in range(2):
                    q4 = qk[:, t, a * MW:(a + 1) * MW].rearrange("p (h d) -> p h d", h=MH)
                    did(tt(q4, q4, cols(V_GQK + a * HD, HD).unsqueeze(1).to_broadcast([P, MH, HD]), ALU.mult))
            settle()
            dve.wait_ge(consts_in, 80)
            rope_views = rotation(qk, 2 * MH, ROPE // 2, C_RC, C_RS, rot_tmp[:, 1024:2048])
            for x1, x2, co, si, ta, tb in rope_views:
                did(tt(ta, x2, si, ALU.mult))
                did(tt(tb, x1, si, ALU.mult))
            settle()
            for x1, x2, co, si, ta, tb in rope_views:
                did(tt(x1, x1, co, ALU.mult))
                did(tt(x2, x2, co, ALU.mult))
            settle()
            for x1, x2, co, si, ta, tb in rope_views:
                did(tt(x1, x1, ta, ALU.subtract))
                did(tt(x2, x2, tb, ALU.add))
            settle()
            V.tensor_copy(hj[:, 0:1], hj[:, 1:2]).then_inc(rot_ready, 1)
            dve.wait_ge(rot_ready, 1)

            def rotate_back(c):
                js = slice(4 * c, 4 * c + 4)
                did(tt(seg(xr[:, js]), seg(zr[:, js]), phase(pc, js), ALU.mult))
                did(tt(seg(tmp1), seg(zi[:, js]), phase(pS, js), ALU.mult))
                settle()
                did(tt(xr[:, js], xr[:, js], tmp1, ALU.subtract))
                did(tt(seg(zr[:, js]), seg(zr[:, js]), phase(pS, js), ALU.mult))
                did(tt(seg(zi[:, js]), seg(zi[:, js]), phase(pc, js), ALU.mult))
                settle()
                did(tt(zi[:, js], zi[:, js], zr[:, js], ALU.add))
                settle()

            rotate_back(0)
            dve.wait_ge(s_psum, 1)
            s1_ = ps[:, 4:8, :].rearrange("p b (h k) -> p (b h) k", h=2)
            V.scalar_tensor_tensor(att1, s1_, SCALE, mask_s.unsqueeze(1).to_broadcast([P, MH, S]), ALU.mult,
                                   ALU.add).then_inc(s_read, 1)
            dve.wait_ge(s_read, 1)
            V.tensor_reduce(hmax[:, 8:16], att1, AX.X, ALU.max, negate=True).then_inc(max_ready, 1)
            dve.wait_ge(s_psum, 2)
            dve.wait_ge(ret_rot_ready, 1)
            for b in range(2):
                ins = V.scalar_tensor_tensor(att0[:, b], ps[:, 4 + b, :].rearrange("p (h k) -> p h k", h=4), SCALE,
                                             mask_s[:, P:S].unsqueeze(1).to_broadcast([P, 4, P]), ALU.mult, ALU.add)
                if b:
                    ins.then_inc(s_read, 1)
                else:
                    did(ins)
            settle()
            dve.wait_ge(s_read, 2)
            V.tensor_reduce(hmax[:, 0:8].rearrange("p (t g) -> p t g", t=TT), att0, AX.X, ALU.max,
                            negate=True).then_inc(max_ready, 1)
            rotate_back(1)
            V.tensor_scalar(c_s[:, 1], c_s[:, 1], -1.0, None, ALU.mult).then_inc(states_ready, 1)
            dve.wait_ge(states_ready, 1)
            dve.wait_ge(rs_psum, 1)
            dec = decay_s.rearrange("p (h o) i -> p h o i", o=2)
            for o_ in range(2):
                did(tt(rP0.rearrange("p (h o) i -> p h o i", o=2)[:, :, o_],
                       ps[:, o_, :].rearrange("p (h i) -> p h i", h=2), dec[:, :, o_], ALU.mult))
                did(tt(rP1.rearrange("p (h o) i -> p h o i", o=2)[:, :, o_],
                       ps[:, 2 + o_, 0:256].rearrange("p (h i) -> p h i", h=2), dec[:, :, o_, 0:P], ALU.mult))
            settle()
            V.tensor_copy(hj[:, 0:1], hj[:, 1:2]).then_inc(rp_ready, 1)
            dve.wait_ge(rp_ready, 1)
            dve.wait_ge(exp_ready, 16)
            step(V.reciprocal(hsum, hsum))
            dve.wait_ge(o_psum, 1)
            for t in range(TT):
                o_v = ps[:, 4 + t, :].rearrange("p (p2 o d) -> p o p2 d", o=2, d=HD)
                y_v = ymix[:, t, S5_CH:S5_CH + MW].rearrange("p (p2 o d) -> p o p2 d", o=2, d=HD)
                for o_ in range(2):
                    r_v = hsum[:, 8 * t + 4 * o_:8 * t + 4 * o_ + 4].unsqueeze(2).to_broadcast([P, 4, HD])
                    did(tt(y_v[:, o_], o_v[:, o_], r_v, ALU.mult))
            settle()
            y_b = ymix[:, :, S5_CH:S5_CH + MW].rearrange("p t (h d) -> p t h d", d=HD)
            sq = done_proj[:, 512:1536].rearrange("p (t h d) -> p t h d", t=TT, d=HD)
            step(tt(sq, y_b, y_b, ALU.mult))
            step(V.tensor_reduce(sums[:, 0:16].rearrange("p (t h) -> p t h", t=TT), sq, AX.X, ALU.add))
            step(rstd_from(sums[:, 0:16], 16, HD))
            for t in range(TT):
                did(tt(y_b[:, t], y_b[:, t], rstd[:, 8 * t:8 * t + 8].unsqueeze(2).to_broadcast([P, MH, HD]), ALU.mult))
            settle()
            dve.wait_ge(y_psum, 1)
            for c in range(S5_C):
                V.scalar_tensor_tensor(uT[:, c, :], uT[:, c, :], cols(V_D + c, 1), ps[:, 6, c * S:(c + 1) * S],
                                       ALU.mult, ALU.add).then_inc(y_lin, 1)
            dve.wait_ge(ret_o_psum, 1)
            y_c = ymix[:, :, S5_CH + MW:D].rearrange("p t (h d) -> p t h d", d=HD)
            step(V.tensor_copy(ymix[:, :, S5_CH + MW:D], ps[:, 0, :].rearrange("p (t d) -> p t d", t=TT)))
            sq = done_proj[:, 1536:2048].rearrange("p (t h d) -> p t h d", t=TT, d=HD)
            step(tt(sq, y_c, y_c, ALU.mult))
            step(V.tensor_reduce(sums[:, 16:24].rearrange("p (t h) -> p t h", t=TT), sq, AX.X, ALU.add))
            step(rstd_from(sums[:, 16:24], 8, HD))
            for t in range(TT):
                did(tt(y_c[:, t], y_c[:, t], rstd[:, 4 * t:4 * t + 4].unsqueeze(2).to_broadcast([P, RH, HD]), ALU.mult))
            settle()
            dve.wait_ge(silu_ready, 1)
            did(tt(ymix[:, :, S5_CH + MW:D], ymix[:, :, S5_CH + MW:D], ret[:, :, 3 * RW:4 * RW], ALU.mult))
            settle()
            dve.wait_ge(gate_ready, 1)
            tt(uT[:], uT[:], hj[:, 0:S5_C * S].rearrange("p (c t) -> p c t", c=S5_C), ALU.mult).then_inc(ya_ready, 1)
            dve.wait_ge(yaT_psum, 1)
            step(V.tensor_copy(ymix[:, :, 0:S5_CH], ps[:, 6, :].rearrange("p (t d) -> p t d", t=TT)))
            sq = done_proj[:, 0:512].rearrange("p (t d) -> p t d", t=TT)
            step(tt(sq, ymix[:, :, 0:S5_CH], ymix[:, :, 0:S5_CH], ALU.mult))
            step(V.tensor_reduce(sums[:, 24:26], sq, AX.X, ALU.add))
            step(rstd_from(sums[:, 24:26], TT, S5_CH))
            for t in range(TT):
                ins = V.tensor_scalar(ymix[:, t, 0:S5_CH], ymix[:, t, 0:S5_CH], rstd[:, t:t + 1], None, ALU.mult)
                if t == TT - 1:
                    ins.then_inc(mix_ready, 1)
                else:
                    did(ins)

            def transposed_low(gain, n):
                for k in range(KC):
                    dve.wait_ge(th_ready, n * KC + 2 * (k // 2) + 2)
                    V.scalar_tensor_tensor(h_lo[:, k, :], ps[:, k // 2, (k % 2) * S:(k % 2 + 1) * S], cols(gain + k, 1),
                                           h_hi[:, k, :].bitcast(F32), ALU.mult, ALU.subtract).then_inc(tl_ready, 1)

            transposed_low(V_GM, 0)
            for n in range(2):
                dve.wait_ge(half_used, KC * (n + 1))
                for t in range(TT):
                    c = slice(CHUNK * n, CHUNK * (n + 1))
                    tt(xs[:, t, c], xs[:, t, c], ps[:, 4 + 2 * n + t, :], ALU.add).then_inc(sum2_ready, 1)
            dve.wait_ge(sumsq_2, 4)
            step(tt(ss_x, ss_2[:, 0:2], ss_2[:, 2:4], ALU.add))
            step(rstd_from(ss_x, TT, D))
            V.tensor_scalar(xn[:, 0, :], xs[:, 0, :], rstd[:, 0:1], None, ALU.mult).then_inc(xn_ready, 1)
            transposed_low(V_G2, 1)

            def best(dst, where, src, scratch):
                for d_, s_ in zip(dst, src):
                    did(V.max(d_[:, 0:8], s_))
                settle()
                for d_, w_, s_, x_ in zip(dst, where, src, scratch):
                    did(V.max_index(w_[:, 0:8], d_[:, 0:8], s_))
                    did(V.match_replace(x_, d_[:, 0:8], s_, LOWEST))
                settle()
                for d_, x_ in zip(dst, scratch):
                    did(V.max(d_[:, 8:16], x_))
                settle()
                for d_, w_, x_ in zip(dst, where, scratch):
                    did(V.max_index(w_[:, 8:16], d_[:, 8:16], x_))
                settle()

            ch_rows = [(c, h) for c in range(2) for h in range(PH)]
            shape = [P, PH, PK, PK]
            w2 = work2.rearrange("p (h a b) -> p h a b", h=PH, a=PK)
            w3 = work3.rearrange("p (h a b) -> p h a b", h=PH, a=PK)
            iota_k = iota[:, 0:PK].unsqueeze(1).unsqueeze(1).to_broadcast(shape)
            for t in range(TT):
                dve.wait_ge(sc_ready, 4 * t + 4)
                best([top[:, c, h, :] for c, h in ch_rows], [idx[:, c, h, :] for c, h in ch_rows],
                     [sc[:, t, c, h, :] for c, h in ch_rows], [work[:, c, h, :] for c, h in ch_rows])
                did(V.tensor_copy(idx_f, idx))
                step(tt(w2, top[:, 0].unsqueeze(3).to_broadcast(shape), top[:, 1].unsqueeze(2).to_broadcast(shape), ALU.add))
                pairs = [work2[:, h * 256:(h + 1) * 256] for h in range(PH)]
                best([top2[:, h, :] for h in range(PH)], [pos[:, h, :] for h in range(PH)], pairs,
                     [work3[:, h * 256:(h + 1) * 256] for h in range(PH)])
                did(tt(rows[:, t, 2, :].rearrange("p (h k) -> p h k", h=PH), top2,
                       top2[:, :, 0:1].to_broadcast([P, PH, PK]), ALU.subtract))
                did(V.tensor_scalar(ab[:, 0], pos, 4, None, ALU.logical_shift_right))
                did(V.tensor_scalar(ab[:, 1], pos, PK - 1, None, ALU.bitwise_and))
                settle()
                step(V.tensor_copy(ab_f, ab))
                for c in range(2):
                    step(tt(w2, ab_f[:, c].unsqueeze(3).to_broadcast(shape), iota_k, ALU.is_equal))
                    step(tt(w3, w2, idx_f[:, c].unsqueeze(2).to_broadcast(shape), ALU.mult))
                    step(V.tensor_reduce(rows[:, t, c, :].rearrange("p (h k) -> p h k", h=PH), w3, AX.X, ALU.add))
            V.tensor_copy(top2[:, 0, 0:1], top2[:, 0, 1:2]).then_inc(diff_ready, 1)
            dve.wait_ge(gate_exp, TT)
            gates = rows[:, :, 2, :].rearrange("p t (h k) -> p t h k", h=PH)
            step(V.tensor_reduce(gsum, gates, AX.X, ALU.add))
            step(V.reciprocal(gsum, gsum))
            for t in range(TT):
                did(tt(gates[:, t], gates[:, t], gsum[:, t].unsqueeze(2).to_broadcast([P, PH, PK]), ALU.mult))
            settle()
            V.tensor_copy(top2[:, 0, 0:1], top2[:, 0, 1:2]).then_inc(tok_ready, 1)
            for t in range(TT):
                dve.wait_ge(route_ready, TT + t + 1)
                c = slice(t * P, (t + 1) * P)
                step(tt(route_t[:, 3, c], ps[:, 4 + t, 2 * P:3 * P], route_t[:, 2, c], ALU.subtract))

            def one_hots(t, first=False):
                for s in range(UN):
                    g = UN * t + s
                    if not (first and s < 2):
                        dve.wait_ge(group_psum, g - 1)
                    tok = bass.ds(g * GT, GT)
                    tt(hot_j[:, s % 2], iota.unsqueeze(1).to_broadcast([P, GT, P]),
                       route_t[:, 1, tok].unsqueeze(2).to_broadcast([P, GT, P]), ALU.is_equal)
                    for q in range(GT):
                        one = bass.ds(g * GT + q, 1)
                        for part, dst in ((2, hot_hi), (3, hot_lo)):
                            ins = V.tensor_scalar(dst[:, s % 2, q, :], iota, route_t[:, 0, one], route_t[:, part, one],
                                                  ALU.is_equal, ALU.mult)
                    ins.then_inc(hot_ready, 1)

            one_hots(0, first=True)
            with dve.Fori(1, TURNS - G_TURN0) as t:
                one_hots(t)

            dve.wait_ge(group_done, S // GT)

            def weigh(t, tile, first=False):
                for s in range(UN):
                    n = UN * t + s
                    if first:
                        dve.wait_ge(act_ready, NT)
                        dve.wait_ge(half_used, TAIL + 2 * NT)
                    else:
                        if s % 2 == 0:
                            dve.wait_ge(acts_in[s // 2], 16 * t)
                        dve.wait_ge(half_used, TAIL + 2 * NT + 8 * t + 2 * s - 6)
                    tt(weighted[:, s % 2, :], acts[:, s, :],
                       routing[:, :, bass.ds(tile + s, 1)].rearrange("p t o -> p (t o)"), ALU.mult).then_inc(product_done, 1)
                    dve.wait_ge(product_done, n + 1)
                    V.tensor_copy(h_hi[:, s, :], weighted[:, s % 2, :]).then_inc(w_steps, 1)
                    dve.wait_ge(w_steps, n + 1)
                    tt(h_lo[:, s, :], weighted[:, s % 2, :], h_hi[:, s, :].bitcast(F32), ALU.subtract).then_inc(w_ready, 1)

            weigh(0, NT - UN, first=True)
            with dve.Fori(1, TURNS) as t:
                weigh(t, UN * t - UN)
            for h in range(2):
                dve.wait_ge(half_used, TAIL + 4 * NT - 1 + h)
                for t in range(TT):
                    c = slice(h * HALF, (h + 1) * HALF)
                    tt(xs[:, t, c], xs[:, t, c], ps[:, 4 + 2 * h + t, :], ALU.add).then_inc(sum_ready, 1)

        @block.scalar
        def _(act):
            ch = Chain(act, act_steps)
            did, settle = ch.did, ch.settle
            n_std = [0]

            def root(n):
                n_std[0] += 1
                act.wait_ge(var_ready, n_std[0])
                A.activation(std[:, 0:n], std[:, 0:n], ACT.Sqrt).then_inc(std_ready, 1)

            def slice_high(n, k):
                m = KC * n + k
                if k == 0:
                    act.wait_ge(w_in_sem[(6 + n) % W_SLOTS], 16 * ((6 + n) // W_SLOTS + 1))
                if m >= 4:
                    act.wait_ge(half_used, m - 3)
                A.activation(w_hi[:, m % 4, :], w_ring[(6 + n) % W_SLOTS][:, k, :], ACT.Copy).then_inc(hi_ready, 1)

            def transposed_high(gain, n):
                for k in range(KC):
                    act.wait_ge(t_psum, 4 * (n + 1) + k // 2 + 1)
                    A.activation(h_hi[:, k, :], ps[:, k // 2, (k % 2) * S:(k % 2 + 1) * S], ACT.Copy,
                                 scale=cols(gain + k, 1)).then_inc(th_ready, 1)

            act.wait_ge(x_in, 32)
            for t in range(TT):
                if t:
                    act.wait_ge(sumsq_x, t)
                A.activation(xn[:, t, :], xs[:, t, :], ACT.Square, accum_out=ss_x[:, t:t + 1]).then_inc(sumsq_x, 1)
            act.wait_ge(params_in, 32)
            for k in range(4):
                act.wait_ge(t_psum, k // 2 + 1)
                A.activation(hT[:, k, :], ps[:, k // 2, (k % 2) * S:(k % 2 + 1) * S], ACT.Copy,
                             scale=cols(V_G1 + k, 1)).then_inc(hT_ready, 1)
            root(TT)
            A.activation(dt, cols(V_LDT, 8), ACT.Exp).then_inc(dt_ready, 1)
            act.wait_ge(expo_ready, 1)
            A.activation(mag, expo, ACT.Exp).then_inc(mag_ready, 1)
            act.wait_ge(rx_ready, 1)
            act.wait_ge(u_psum, 1)
            for t in range(TT):
                A.activation(u_tok[:, t, :], ps[:, 4, t * S5_CH:(t + 1) * S5_CH], ACT.Copy,
                             scale=rx[:, t:t + 1]).then_inc(u_tok_ready, 1)
            act.wait_ge(ang_ready, 1)
            did(A.activation(s1, ang, ACT.Sin))
            settle()
            A.activation(c1, half, ACT.Sin).then_inc(trig_ready, 1)
            act.wait_ge(uT_psum, 1)
            A.activation(uT, ps[:, 5, :].rearrange("p (c t) -> p c t", c=S5_C), ACT.Copy).then_inc(u_ready, 1)
            act.wait_ge(bT_psum, 1)
            A.activation(bT, ps[:, 6, :].rearrange("p (a s) -> p a s", a=4), ACT.Copy).then_inc(bT_ready, 1)

            dst = [qk[:, :, 0:MW], qk[:, :, MW:2 * MW], ret[:, :, 0:2 * RW], ret[:, :, 2 * RW:4 * RW], mv]

            def projected(n, t):
                act.wait_ge(proj_psum, 2 * n + t + 1)
                A.activation(dst[n][:, t, :], ps[:, 2 * (n % 2) + t, :], ACT.Copy,
                             scale=rx[:, t:t + 1]).then_inc(proj_ready, 1)

            def exps(places):
                for a, g in places:
                    A.activation(a, a, ACT.Exp, bias=hmax[:, g:g + 1], accum_out=hsum[:, g:g + 1]).then_inc(exp_ready, 1)

            for n in range(2):
                for t in range(TT):
                    projected(n, t)
            act.wait_ge(proj_ready, 4)
            act.wait_ge(drive_ready, 2)
            A.activation(xn.rearrange("p t d -> p (t d)"), qk_flat, ACT.Square).then_inc(qk_sq, 1)
            projected(2, 0)
            projected(2, 1)
            root(32)
            act.wait_ge(rotT_psum, 1)
            for h, d_ in ((0, mqT), (2, mkT)):
                A.activation(d_, ps[:, 4 + h:6 + h, :].rearrange("p b (h t) -> p (b h) t", h=2), ACT.Copy)\
                    .then_inc(rotT_ready, 1)
            projected(3, 0)
            projected(3, 1)
            act.wait_ge(max_ready, 1)
            exps([(att1[:, g, :], 8 + g) for g in range(MH)])
            projected(4, 0)
            act.wait_ge(max_ready, 2)
            exps([(att0[:, g // 4, g % 4, :], g) for g in range(MH)])

            def probs_back(n, bank, d_):
                act.wait_ge(pT_psum, n + 1)
                A.activation(d_, ps[:, bank, :].rearrange("p (h k) -> p h k", h=4), ACT.Copy).then_inc(pT_ready, 1)

            for b in range(2):
                probs_back(b, 6 + b, att1[:, 4 * b:4 * b + 4, 0:P])
            projected(4, 1)
            act.wait_ge(retT_psum, 1)
            A.activation(rqT, ps[:, 2, :].rearrange("p (h t) -> p h t", h=2), ACT.Copy).then_inc(retT_ready, 1)
            A.activation(rkT, ps[:, 3, :].rearrange("p (h t) -> p h t", h=2), ACT.Copy).then_inc(retT_ready, 1)
            for b in range(2):
                probs_back(2 + b, 4 + b, att1[:, 4 * b:4 * b + 4, P:S])
            for b in range(2):
                probs_back(4 + b, 6 + b, att0[:, b])
            act.wait_ge(proj_ready, 10)
            A.activation(ret[:, :, 3 * RW:4 * RW], ret[:, :, 3 * RW:4 * RW], ACT.Silu).then_inc(silu_ready, 1)
            root(16)
            act.wait_ge(y_lin, 2)
            A.activation(uT, uT, ACT.Gelu_apprx_tanh).then_inc(y_ready, 1)
            root(8)
            act.wait_ge(glu_psum, 1)
            A.activation(hj[:, 0:S5_C * S], ps[:, 7, :], ACT.Sigmoid).then_inc(gate_ready, 1)
            for k in range(4):
                slice_high(0, k)
            root(TT)
            transposed_high(V_GM, 0)
            for n in range(2):
                for k in range(KC):
                    if n or k >= 4:
                        slice_high(n, k)
            for n in range(2):
                for t in range(TT):
                    c = slice(CHUNK * n, CHUNK * (n + 1))
                    act.wait_ge(sum2_ready, TT * n + t + 1)
                    A.activation(done_proj[:, CHUNK * t:CHUNK * (t + 1)] if n == 0 else
                                 done_proj[:, 1024 + CHUNK * t:1024 + CHUNK * (t + 1)], xs[:, t, c], ACT.Square,
                                 accum_out=ss_2[:, 2 * n + t:2 * n + t + 1]).then_inc(sumsq_2, 1)
            for k in range(4):
                slice_high(2, k)
            root(TT)
            act.wait_ge(xn_ready, 1)
            A.activation(xn[:, 1, :], xs[:, 1, :], ACT.Copy, scale=rstd[:, 1:2]).then_inc(xn_ready, 1)
            transposed_high(V_G2, 1)
            for k in range(4, KC):
                slice_high(2, k)

            def queries(n):
                act.wait_ge(half_used, KC * (3 + n))
                for h in range(4):
                    A.activation(pqT[:, 4 * n + h, :], ps[:, 4 * (1 - n) + h, 0:S], ACT.Copy).then_inc(pq_ready, 1)

            for k in range(4):
                slice_high(3, k)
            queries(0)
            for k in range(4, KC):
                slice_high(3, k)

            def key_scores(t):
                act.wait_ge(sc_psum, t + 1)
                for b in range(4):
                    A.activation(sc[:, t, b // 2, 4 * (b % 2):4 * (b % 2) + 4, :],
                                 ps[:, 4 + b, :].rearrange("p (h n) -> p h n", h=4), ACT.Copy).then_inc(sc_ready, 1)

            def high(n, s, turn):
                act.wait_ge(raw_in[s], 16 * turn + 16)
                for h in range(2):
                    act.wait_ge(half_used, TAIL + 2 * n + h - 3)
                    A.activation(w_hi[:, 2 * (s % 2) + h, :], raw[:, s, h * HALF:(h + 1) * HALF], ACT.Copy)\
                        .then_inc(hi_ready, 1)

            def keys_turn(t, groups=None, first=False, first_group=False):
                for s in range(UN):
                    n = UN * t + s
                    high(n + 1, (s + 1) % UN, t + (s + 1) // UN)
                    if s % 2 == 0 and not first:
                        act.wait_ge(spilled[s // 2], 16 * t)
                    act.wait_ge(half_used, TAIL + 2 * n + 2)
                    A.activation(acts[:, s, :], ps[:, s % 2, 0:S], ACT.Gelu_apprx_tanh).then_inc(act_ready, 1)
                    if groups is not None and not (first_group and s == 0):
                        group_out(groups + s - 1, (s - 1) % 2)

            def group_out(g, b):
                act.wait_ge(group_psum, g + 1)
                A.activation(routing[:, bass.ds(g * GT, GT), :], ps[:, 2 + b, :].rearrange("p (t i) -> p t i", t=GT),
                             ACT.Copy).then_inc(group_done, 1)

            high(0, 0, 0)
            queries(1)
            keys_turn(0, first=True)
            key_scores(0)
            keys_turn(1)
            key_scores(1)
            with act.Fori(2, EXP_TURN) as t:
                keys_turn(t)
            act.wait_ge(diff_ready, 1)
            for t in range(TT):
                A.activation(rows[:, t, 2, :], rows[:, t, 2, :], ACT.Exp).then_inc(gate_exp, 1)
            with act.Fori(EXP_TURN, ROUTE_TURN) as t:
                keys_turn(t)
            act.wait_ge(route_psum, 1)
            for t in range(TT):
                A.activation(route_t[:, 0:2, t * P:(t + 1) * P], ps[:, 4 + t, 0:2 * P].rearrange("p (a t) -> p a t", a=2),
                             ACT.Copy).then_inc(route_ready, 1)
            for t in range(TT):
                A.activation(route_t[:, 2, t * P:(t + 1) * P].bitcast(F32R), ps[:, 4 + t, 2 * P:3 * P],
                             ACT.Copy).then_inc(route_ready, 1)
            with act.Fori(ROUTE_TURN, G_TURN0) as t:
                keys_turn(t)
            keys_turn(G_TURN0, groups=0, first_group=True)
            with act.Fori(G_TURN0 + 1, TURNS) as t:
                keys_turn(t, groups=UN * t - UN * G_TURN0)
            group_out(S // GT - 1, 1)
            with act.Fori(TURNS, 2 * TURNS - 1) as t:
                for s in range(UN):
                    high(UN * t + s + 1, (s + 1) % UN, t + (s + 1) // UN)
            for s in range(UN - 1):
                high(2 * NT - UN + s + 1, s + 1, 2 * TURNS - 1)

        @block.gpsimd
        def _(pool):
            G = nc.gpsimd
            ch = Chain(pool, pool_steps)
            did, settle = ch.did, ch.settle
            pool.wait_ge(proj_ready, 6)
            pool.wait_ge(consts_in, 80)
            views = rotation(ret, 2 * RH, HD // 2, C_TC, C_TS, rot_tmp)
            for x1, x2, co, si, ta, tb in views:
                did(G.tensor_tensor(ta, x2, si, ALU.mult))
                did(G.tensor_tensor(tb, x1, si, ALU.mult))
            settle()
            for x1, x2, co, si, ta, tb in views:
                did(G.tensor_tensor(x1, x1, co, ALU.mult))
                did(G.tensor_tensor(x2, x2, co, ALU.mult))
            settle()
            for n, (x1, x2, co, si, ta, tb) in enumerate(views):
                did(G.tensor_tensor(x1, x1, ta, ALU.subtract))
                ins = G.tensor_tensor(x2, x2, tb, ALU.add)
                if n == TT - 1:
                    ins.then_inc(ret_rot_ready, 1)
                else:
                    did(ins)
            settle()
            for m in range(TAIL):
                n, k = m // KC, m % KC
                pool.wait_ge(hi_ready, m + 1)
                G.tensor_tensor(w_lo[:, m % 4, :], w_ring[(6 + n) % W_SLOTS][:, k, :], w_hi[:, m % 4, :].bitcast(F32),
                                ALU.subtract).then_inc(lo_ready, 1)
            def low(t):
                for s in range(UN):
                    for h in range(2):
                        pool.wait_ge(hi_ready, TAIL + 8 * t + 2 * s + h + 1)
                        slot = 2 * (s % 2) + h
                        G.tensor_tensor(w_lo[:, slot, :], raw[:, s, h * HALF:(h + 1) * HALF],
                                        w_hi[:, slot, :].bitcast(F32), ALU.subtract).then_inc(lo_ready, 1)

            with pool.Fori(0, 2 * TURNS) as t:
                low(t)


def host_constants():
    f = np.float32
    pos = np.arange(S, dtype=f)
    inv = (f(500000.0) ** (-np.arange(0, ROPE, 2, dtype=f) / f(ROPE))).astype(f)
    ang = pos[:, None] * inv[None, :]
    lin = np.linspace(0.0, 1.0, HD // 2, dtype=f)
    rang = pos[:, None] * (f(10000.0) ** (-lin)).astype(f)[None, :]
    tile = lambda a: a.astype(f).reshape(TT, P, -1).transpose(1, 0, 2).reshape(P, -1)
    consts = np.concatenate([np.eye(P, dtype=f), np.broadcast_to(np.arange(P, dtype=f), (P, P))], axis=1)
    rots = np.concatenate([tile(np.cos(ang)), tile(np.sin(ang)), tile(np.cos(rang)), tile(np.sin(rang))], axis=1)
    log_g = np.log(1.0 - 2.0 ** (-5.0 - np.arange(RH, dtype=np.float64)))
    diff = np.arange(S)[None, :] - np.arange(P)[:, None]
    decay = np.where(diff[:, None, :] >= 0, np.exp(np.maximum(diff, 0)[:, None, :] * log_g[None, :, None]), 0.0)
    decay = (decay * HD ** -0.5).astype(f)
    mask = np.zeros((P, S), f)
    mask[:, P:] = np.where(np.arange(P)[None, :] <= np.arange(P)[:, None], 0.0, MASKED)
    return consts, rots, decay, mask


def layout(inputs):
    a = {k: np.asarray(v)[0] if k != "x" else np.asarray(v) for k, v in inputs.items()}
    f = np.float32
    per = lambda v_, n: v_.reshape(n, P).T
    rep = lambda v_: np.broadcast_to(v_, (P, HD))
    vecs = np.concatenate([
        per(a["norm1_g"], KC), per(a["norm2_g"], KC), per(a["mix_out_g"], KC),
        per(a["s5_lam_re"].reshape(-1), S5_T), per(a["s5_lam_im"].reshape(-1), S5_T),
        per(np.repeat(a["s5_log_dt"], S5_STATE), S5_T), per(a["s5_d"], S5_C),
        rep(a["moba_q_g"]), rep(a["moba_k_g"])], axis=1)
    b = np.zeros((P, 2, S5_T, 32), f)
    c = np.zeros((P, 2, S5_T, 32), f)
    for r, (bn, cn) in enumerate((("s5_b_re", "s5_c_re"), ("s5_b_im", "s5_c_im"))):
        for o in range(2):
            rows, at = slice(64 * o, 64 * o + 64), slice(16 * o, 16 * o + 16)
            b[rows, r, :, at] = a[bn][o::2].transpose(1, 0, 2)
            c[rows, r, :, at] = a[cn][o::2].transpose(2, 0, 1)
    consts, rots, decay, mask = host_constants()
    u_t = a["peer_u"].reshape(NT, P, KC, P).transpose(0, 3, 2, 1).reshape(NT, P, D)
    keys = a["peer_sub_keys"].transpose(1, 3, 0, 2).reshape(P, PH, NKEY)
    return {
        "x": a["x"][0], "w_in": a["w_in"], "vecs": vecs, "consts": consts, "rots": rots, "decay": decay, "mask": mask,
        "s5_b": b.reshape(P, -1), "s5_c": c.reshape(P, -1), "w_glu": a["s5_w_glu"], "w_out": a["w_out"],
        "w_q": a["peer_w_q"], "keys": keys, "u_t": u_t, "v": a["peer_v"].reshape(NT, P, D),
    }


_OUT = (S, D)


def kernel(**inputs):
    import concourse.bacc as _bacc
    from concourse.bass_utils import run_bass_kernel_spmd as _run

    nc = _bacc.Bacc("TRN2", target_bir_lowering=False, num_devices=1)
    arrays, args = {}, {}
    for name, a in layout(inputs).items():
        a = np.ascontiguousarray(a)
        arrays[f"in_{name}"] = a
        args[name] = nc.dram_tensor(f"in_{name}", a.shape, mybir.dt.from_np(a.dtype), kind="ExternalInput").ap()
    args["out"] = nc.dram_tensor("out_0", _OUT, F32, kind="ExternalOutput").ap()
    args["spill"] = nc.dram_tensor("act_spill", (NT // 2, P, 2 * S), F32, kind="Internal").ap()
    build(nc, **args)
    r = _run(nc, [arrays], core_ids=[0])
    return r.results[0]["out_0"].reshape(1, S, D)
```

```python
from contextlib import ExitStack

import numpy as np

import concourse.bass as bass
from concourse import mybir

F32 = mybir.dt.float32
F32R = mybir.dt.float32r
U32 = mybir.dt.uint32
ALU = mybir.AluOpType
ACT = mybir.ActivationFunctionType
AX = mybir.AxisListType

P = 128
S = 256
TT = S // P
D = 1024
KC = D // P
EPS = 1e-6

S5_CH, S5_GROUP, S5_STATE = 256, 16, 64
S5_NG = S5_CH // S5_GROUP
S5_T = S5_NG * S5_STATE // P
S5_C = S5_CH // P
SEG = P
SEG_LOG = 7

HD = 64
MH, MW = 8, 512
RH, RW = 4, 256
ROPE = HD // 4
SCALE = HD ** -0.5
MASKED = -1e30

NKEY = 128
EXPERTS = NKEY * NKEY
PH, PK = 8, 16
NT = EXPERTS // P

CHUNK = 512
W_SLOTS = 3

SPLIT_CHUNKS = (0, 1, 2, 4)
FRONT = len(SPLIT_CHUNKS) * KC
TAIL = FRONT + 4 * KC
UN = 4
TURNS = NT // UN
HALF = D // 2
GT = 4
G_TURN0 = TURNS - 1 - S // GT // UN
ROUTE_TURN = G_TURN0 - 1
EXP_TURN = G_TURN0 - 2
LOWEST = -3e38

TWO_PI = 2 * np.pi
RC1 = 6.28125
RC2 = float(np.array([np.float32(TWO_PI - RC1)]).view(np.uint32).__and__(np.uint32(0xFFFFF000)).view(np.float32)[0])
RC3 = float(TWO_PI - RC1 - RC2)
LN2_1 = 0.693359375
LN2_2 = float(np.log(2) - LN2_1)
EXP_C = [1 / 40320, 1 / 5040, 1 / 720, 1 / 120, 1 / 24, 1 / 6, 0.5, 1.0]
ROUND = 1.5 * 2.0 ** 23
PI_LOW = 3.1415925

V_G1, V_G2, V_GM = 0, 8, 16
V_LR, V_LI, V_LDT = 24, 32, 40
V_D = 48
V_GQK = 50
V_N = V_GQK + 2 * HD
C_ID, C_IOTA = 0, P
C_N = 2 * P
C_RC = 0
C_RS = C_RC + TT * (ROPE // 2)
C_TC = C_RS + TT * (ROPE // 2)
C_TS = C_TC + TT * (HD // 2)
ROT_N = C_TS + TT * (HD // 2)


def slice_place(m):
    chunk = SPLIT_CHUNKS[m // KC] if m < FRONT else 6 + (m - FRONT) // KC
    return chunk, m % KC, S5_CH if chunk == 0 else CHUNK


class Chain:

    def __init__(self, eng, sem):
        self.eng, self.sem, self.n = eng, sem, 0

    def did(self, ins):
        self.n += 1
        ins.then_inc(self.sem, 1)

    def settle(self):
        self.eng.wait_ge(self.sem, self.n)


def build(nc, x, w_in, vecs, consts, rots, decay, mask, s5_b, s5_c, w_glu, w_out, w_q, keys, u_t, v, out, spill):
    with ExitStack() as ctx:
        def sb(name, shape, dt=F32):
            return ctx.enter_context(nc.sbuf_tensor(name, shape, dt))

        def sem(name):
            return ctx.enter_context(nc.semaphore(name))

        xs = sb("xs", [P, TT, D])
        vec = sb("vec", [P, V_N])
        con = sb("con", [P, C_N])
        small = sb("small", [P, 512])
        routing = sb("routing", [P, S, NKEY])
        h_hi = sb("h_hi", [P, KC, S], F32R)
        h_lo = sb("h_lo", [P, KC, S], F32R)
        raw = sb("raw", [P, UN, D])
        w_hi = sb("w_hi", [P, 4, HALF], F32R)
        w_lo = sb("w_lo", [P, 4, HALF], F32R)
        acts = sb("acts", [P, UN, S])
        hot_j = sb("hot_j", [P, 2, GT, NKEY], F32R)
        hot_gate = sb("hot_gate", [P, 2, GT, 2, NKEY], F32R)
        route_t = sb("route_t", [P, 4, S])
        weighted = route_t[:, 0:2, :]
        ps = ctx.enter_context(nc.psum_tensor("ps", [P, 8, 512], F32))

        ident = con[:, C_ID:C_ID + P]
        iota = con[:, C_IOTA:C_IOTA + P]

        arena = routing[:].rearrange("p a b -> p (a b)")
        cursor = [0]

        def take(n):
            a = cursor[0]
            cursor[0] += n
            assert cursor[0] <= S * NKEY, cursor[0]
            return arena[:, a:a + n]

        w_ring = [take(KC * CHUNK).rearrange("p (k n) -> p k n", k=KC) for _ in range(W_SLOTS)]
        hT = take(KC * S).rearrange("p (k t) -> p k t", k=KC)
        done_proj = hT.rearrange("p k t -> p (k t)")
        xn = take(TT * D).rearrange("p (t d) -> p t d", t=TT)
        qk = take(TT * 2 * MW).rearrange("p (t d) -> p t d", t=TT)
        mv = take(TT * MW).rearrange("p (t d) -> p t d", t=TT)
        ret = take(TT * 4 * RW).rearrange("p (t d) -> p t d", t=TT)
        uT = take(S5_C * S).rearrange("p (c t) -> p c t", c=S5_C)
        ymix = take(TT * D).rearrange("p (t d) -> p t d", t=TT)
        rot_tmp = ymix.rearrange("p t d -> p (t d)")
        r3 = lambda a, k: a.rearrange("p (k t) -> p k t", k=k)
        pc, pS = (r3(take(S5_T * SEG), S5_T) for _ in range(2))
        zr, zi = (r3(take(S5_T * S), S5_T) for _ in range(2))
        squares = zr.rearrange("p j t -> p (j t)")
        xr = xn.rearrange("p t d -> p (t d)").rearrange("p (j t) -> p j t", j=S5_T)
        att1 = take(MH * S).rearrange("p (g k) -> p g k", g=MH)
        att0 = ymix[:, :, S5_CH:S5_CH + MW].rearrange("p t (g k) -> p t g k", g=4)
        qk_flat = qk.rearrange("p t d -> p (t d)")
        mqT = qk_flat[:, 0:1024].rearrange("p (h t) -> p h t", h=4)
        mkT = qk_flat[:, 1024:2048].rearrange("p (h t) -> p h t", h=4)
        rqT = ret[:, 0, 0:2 * RW].rearrange("p (h t) -> p h t", h=2)
        rkT = ret[:, 1, 0:2 * RW].rearrange("p (h t) -> p h t", h=2)
        rP0 = qk_flat[:, 0:1024].rearrange("p (h t) -> p h t", h=RH)
        rP1 = qk_flat[:, 1024:1536].rearrange("p (h t) -> p h t", h=RH)
        tables = w_ring[1].rearrange("p k n -> p (k n)")
        keys_s = tables[:, 1024:2048].rearrange("p (h n) -> p h n", h=PH)
        cursor[0] = W_SLOTS * KC * CHUNK + 2 * KC * S
        pqT = take(PH * S).rearrange("p (h t) -> p h t", h=PH)
        sc = take(TT * 2 * PH * NKEY).rearrange("p (t c h n) -> p t c h n", t=TT, c=2, h=PH)
        work = take(2 * PH * NKEY).rearrange("p (c h n) -> p c h n", c=2, h=PH)
        work2 = take(2 * PH * NKEY)
        work3 = take(2 * PH * NKEY)
        rawf = raw[:].rearrange("p a b -> p (a b)")
        mask_s = rawf[:, 0:S]
        rot = rawf[:, 256:256 + ROT_N]
        u_tok = rawf[:, 512:1024].rearrange("p (t d) -> p t d", t=TT)
        glu_s = rawf[:, 1280:1280 + S5_C * S5_CH].rearrange("p (c n) -> p c n", c=S5_C)
        bT = rawf[:, 1792:1792 + 4 * P].rearrange("p (a s) -> p a s", a=4)
        b_s = rawf[:, 2304:2304 + 512].rearrange("p (r j c) -> p r j c", r=2, j=S5_T)
        c_s = rawf[:, 2816:2816 + 512].rearrange("p (r j c) -> p r j c", r=2, j=S5_T)
        bb = rawf[:, 3328:3328 + 512].rearrange("p (r j c) -> p r j c", r=2, j=S5_T)
        decay_s = acts[:]
        hj = route_t[:].rearrange("p a b -> p (a b)")
        gate_s = hj[:, 0:S5_C * S]
        tmp1 = hj.rearrange("p (j t) -> p j t", j=4)

        zeros_ready = sem("zeros_ready")
        x_in, con_in = [sem("x_in0"), sem("x_in1")], sem("identity_in")
        params_in, s5_b_in, consts_in = sem("params_in"), sem("s5_b_in"), sem("consts_in")
        w_in_sem = [sem(f"weights_in{i}") for i in range(W_SLOTS)]
        keys_in = sem("keys_in")
        dve_steps, act_steps, pool_steps = sem("dve_steps"), sem("act_steps"), sem("pool_steps")
        sumsq_x, var_ready, std_ready, xn_ready = sem("sumsq_x"), sem("var_ready"), sem("std_ready"), sem("xn_ready")
        rx_ready = sem("rstd_x_ready")
        t_psum, hT_ready = sem("transposes_in_psum"), sem("hT_ready")
        expo_ready, mag_ready = sem("exponent_ready"), sem("mag_ready")
        ang_ready, trig_ready = sem("angles_ready"), sem("trig_ready")
        bb_ready, bT_psum, bT_ready = sem("bb_ready"), sem("bT_in_psum"), sem("bT_ready")
        u_tok_ready, uT_psum, u_ready = sem("u_tok_ready"), sem("u_t_in_psum"), sem("u_ready")
        bu_psum, bu_used, drive_ready = sem("bu_in_psum"), sem("bu_used"), sem("drive_ready")
        proj_psum, proj_ready = sem("proj_in_psum"), sem("proj_ready")
        states_ready, y_psum, y_lin, y_ready = sem("states_ready"), sem("y_in_psum"), sem("y_linear"), sem("y_ready")
        glu_psum, gate_ready, ya_ready = sem("glu_in_psum"), sem("glu_gate_ready"), sem("ya_ready")
        yaT_psum, ya_read = sem("ya_t_in_psum"), sem("ya_t_read")
        qk_sq, qk_rstd_ready = sem("qk_squares"), sem("qk_rstd_ready")
        rot_ready, ret_rot_ready = sem("rotated_ready"), sem("ret_rotated_ready")
        rotT_psum, rotT_ready = sem("rotated_t_in_psum"), sem("rotated_t_ready")
        retT_psum, retT_ready = sem("ret_rotated_t_in_psum"), sem("ret_rotated_t_ready")
        ret_read, o_sq = sem("ret_scores_read"), sem("moba_out_squares")
        s_psum, s_read, max_ready, exp_ready = sem("scores_in_psum"), sem("scores_read"), sem("max_ready"), sem("exp_ready")
        pT_psum, pT_ready = sem("probs_t_in_psum"), sem("probs_t_ready")
        o_psum, ret_o_psum = sem("moba_out_in_psum"), sem("ret_out_in_psum")
        rs_psum, rp_ready, silu_ready = sem("ret_scores_in_psum"), sem("ret_probs_ready"), sem("silu_ready")
        mix_ready, sum2_ready, sumsq_2 = sem("mix_ready"), sem("residual_ready"), sem("sumsq_2")
        th_ready, tl_ready = sem("transposed_high_ready"), sem("transposed_low_ready")
        pq_ready, sc_psum, sc_ready = sem("pq_ready"), sem("keys_scores_in_psum"), sem("keys_scores_ready")
        raw_in = [sem(f"raw_in{i}") for i in range(UN)]
        hi_ready, lo_ready = sem("hi_ready"), sem("lo_ready")
        half_used = sem("half_used")
        act_ready = sem("act_ready")
        spilled = [sem("spilled0"), sem("spilled1")]
        acts_in = [sem("acts_in0"), sem("acts_in1")]
        diff_ready, gate_exp = sem("gate_exponents_ready"), sem("gate_exp_ready")
        route_low = sem("gate_low_ready")
        tok_ready, route_psum, route_ready = sem("route_rows_ready"), sem("route_t_in_psum"), sem("route_t_ready")
        hot_ready, group_psum = sem("one_hots_ready"), sem("group_in_psum")
        group_high, group_done = sem("group_high_out"), sem("group_done")
        w_steps, w_ready, product_done = sem("weighted_steps"), sem("weighted_ready"), sem("product_done")
        sum_ready, stored = sem("sum_ready"), sem("stored")

        V = nc.vector
        A = nc.scalar

        def cols(off, n):
            return vec[:, off:off + n]

        def sm(off, n):
            return small[:, off:off + n]

        o = [0]

        def tiny(n):
            a = sm(o[0], n)
            o[0] += n
            assert o[0] <= 512, o[0]
            return a

        ss_x, ss_2, rx, rstd = tiny(TT), tiny(4), tiny(TT), tiny(32)
        dt, expo, mag, ang, kk, s1, c1, half = (tiny(8) for _ in range(8))
        ar, ai, den, fr, fi, q1, q2, q3 = (tiny(8) for _ in range(8))
        rest, power = tiny(8), tiny(8)
        z0r, z0i, sums, qk_rstd = tiny(8), tiny(8), tiny(32), tiny(32)
        sq_c, sq_s = tiny(64).rearrange("p (n j) -> p n j", j=8), tiny(64).rearrange("p (n j) -> p n j", j=8)
        std = tiny(32)
        hmax, hsum = tiny(16), tiny(16)

        assert MW == CHUNK and 2 * RW == CHUNK
        q_at = S5_CH
        ret_at = q_at + 3 * MW
        starts = [q_at, q_at + MW, ret_at + 2 * RW, ret_at, q_at + 2 * MW]
        w_src = [w_in[:, 0:S5_CH]] + [w_in[:, a:a + CHUNK] for a in starts]
        w_src += [w[:, CHUNK * n:CHUNK * (n + 1)] for w in (w_out, w_q) for n in range(2)]
        W_N = len(w_src)
        top = tables[:, 0:256].rearrange("p (c h k) -> p c h k", c=2, h=PH)
        idx = tables[:, 256:512].bitcast(U32).rearrange("p (c h k) -> p c h k", c=2, h=PH)
        pos = tables[:, 512:640].bitcast(U32).rearrange("p (h k) -> p h k", h=PH)
        tab = hT.rearrange("p k t -> p (k t)")
        rows = tab[:, 0:768].rearrange("p (t a k) -> p t a k", t=TT, a=3)
        idx_f = tab[:, 768:1024].rearrange("p (c h k) -> p c h k", c=2, h=PH)
        ab = tab[:, 1024:1280].bitcast(U32).rearrange("p (c h k) -> p c h k", c=2, h=PH)
        ab_f = tab[:, 1280:1536].rearrange("p (c h k) -> p c h k", c=2, h=PH)
        top2 = tab[:, 1536:1664].rearrange("p (h k) -> p h k", h=PH)
        gsum = tab[:, 1664:1680].rearrange("p (t h) -> p t h", t=TT)
        block = ctx.enter_context(nc.Block())

        @block.sync
        def _(sp):
            sp.dma_start(con[:], consts).then_inc(con_in, 16)
            for t in range(TT):
                sp.dma_start(xs[:, t, :], x[t * P:(t + 1) * P, :]).then_inc(x_in[t], 16)
            sp.dma_start(vec[:], vecs).then_inc(params_in, 16)
            for n in range(W_N):
                if n == 1:
                    sp.dma_start(rawf[:, 2304:2816], s5_b).then_inc(s5_b_in, 16)
                if n == 2:
                    sp.dma_start(rot, rots).then_inc(consts_in, 16)
                    sp.dma_start(rawf[:, 2816:3328], s5_c).then_inc(consts_in, 16)
                    sp.dma_start(glu_s, w_glu.rearrange("(c p) n -> p c n", p=P)).then_inc(consts_in, 16)
                    sp.dma_start(mask_s, mask).then_inc(consts_in, 16)
                    sp.dma_start(decay_s, decay).then_inc(consts_in, 16)
                old = n - W_SLOTS
                if old in SPLIT_CHUNKS:
                    sp.wait_ge(lo_ready, KC * (SPLIT_CHUNKS.index(old) + 1))
                elif 0 <= old < 6:
                    sp.wait_ge(proj_psum, TT * (old // 2))
                elif old >= 6:
                    sp.wait_ge(lo_ready, FRONT + KC * (old - 5))
                width = w_src[n].shape[1]
                sp.dma_start(w_ring[n % W_SLOTS][:, :, 0:width],
                             w_src[n].rearrange("(k p) n -> p k n", p=P)).then_inc(w_in_sem[n % W_SLOTS], 16)

            def load_tile(weights, tile, s):
                sp.dma_start(raw[:, s, :], weights[tile]).then_inc(raw_in[s], 16)

            sp.wait_ge(mix_ready, 1)
            for s in range(UN):
                load_tile(u_t, s, s)
            sp.wait_ge(lo_ready, FRONT + 2 * KC)
            sp.dma_start(keys_s, keys).then_inc(keys_in, 16)

            def keys_turn(t, weights, nxt, store):
                for s in range(UN):
                    sp.wait_ge(lo_ready, TAIL + 8 * t + 2 * s + 2)
                    load_tile(weights, nxt + s, s)
                    if store and s % 2:
                        sp.wait_ge(act_ready, UN * t + s + 1)
                        sp.dma_start(spill[2 * t + s // 2], acts[:, s - 1:s + 1, :].rearrange("p a t -> p (a t)"))\
                            .then_inc(spilled[s // 2], 16)

            with sp.Fori(0, TURNS - 1) as t:
                keys_turn(t, u_t, UN * t + UN, True)
            keys_turn(TURNS - 1, v, NT - UN, False)

            for b in range(2):
                sp.wait_ge(spilled[b], 16 * (TURNS - 1))
            with sp.Fori(0, TURNS - 1) as t:
                for s in range(UN):
                    sp.wait_ge(lo_ready, TAIL + 2 * NT + 8 * t + 2 * s + 2)
                    load_tile(v, UN * t + s, s)
                    if s % 2:
                        sp.wait_ge(product_done, UN * t + s + 1)
                        sp.dma_start(acts[:, s - 1:s + 1, :].rearrange("p a t -> p (a t)"), spill[2 * t + s // 2])\
                            .then_inc(acts_in[s // 2], 16)
            for n in range(2 * TT):
                sp.wait_ge(sum_ready, n + 1)
                h, t = n // TT, n % TT
                sp.dma_start(out[t * P:(t + 1) * P, h * HALF:(h + 1) * HALF],
                             xs[:, t, h * HALF:(h + 1) * HALF]).then_inc(stored, 16)
            sp.wait_ge(stored, 16 * 2 * TT)

        @block.tensor
        def _(pe):
            def chunk_in(n):
                pe.wait_ge(w_in_sem[n % W_SLOTS], 16 * (n // W_SLOTS + 1))
                return w_ring[n % W_SLOTS]

            def transpose_rows(src, loaded=None):
                for t in range(TT):
                    if loaded:
                        pe.wait_ge(loaded[t], 16)
                    for k in range(KC):
                        mm = pe.transpose(ps[:, k // 2, (k % 2) * S + t * P:(k % 2) * S + (t + 1) * P],
                                          src[:, t, k * P:(k + 1) * P], ident)
                        if t == TT - 1 and k % 2:
                            mm.then_inc(t_psum, 1)

            def keep_warm(operand, bank, n):
                for _ in range(n):
                    pe.matmul(ps[:, bank, 0:P], operand, operand, start=True, stop=True)

            def project(n, t):
                w = chunk_in(n)
                pe.wait_ge(proj_ready, 2 * (n - 3) + t + 1)
                pe.wait_ge(hT_ready, 2)
                for k in range(KC):
                    mm = pe.matmul(ps[:, 2 * ((n - 1) % 2) + t, :], hT[:, k, t * P:(t + 1) * P], w[:, k, :],
                                   start=(k == 0), stop=(k == KC - 1))
                mm.then_inc(proj_psum, 1)

            def drive(c):
                for r in range(2):
                    for j in range(4):
                        mm = pe.matmul(ps[:, 4 + j, r * S:(r + 1) * S],
                                       bT[32 * j:32 * j + 32, r * 2 + c, :], uT[32 * j:32 * j + 32, c, :],
                                       start=True, stop=True)
                mm.then_inc(bu_psum, 1)

            def halves_product(dst, pairs, first, last):
                for i, (s_hi, s_lo, m_hi, m_lo) in enumerate(pairs):
                    end = last and i == len(pairs) - 1
                    pe.matmul(dst, s_hi, m_hi, start=first and i == 0, stop=False)
                    pe.matmul(dst, s_hi, m_lo, start=False, stop=False)
                    mm = pe.matmul(dst, s_lo, m_hi, start=False, stop=end)
                return mm

            pe.wait_ge(zeros_ready, 1)
            keep_warm(mv[:, 0, 0:P], 7, 9)
            pe.wait_ge(con_in, 16)
            transpose_rows(xs, x_in)
            def by_slices(n, ks, dst, last=None):
                for k in ks:
                    m = KC * SPLIT_CHUNKS.index(n) + k
                    if n == 0:
                        pe.wait_ge(th_ready, k + 1)
                        pe.wait_ge(tl_ready, k + 1)
                    pe.wait_ge(lo_ready, m + 1)
                    width = slice_place(m)[2]
                    for t in range(TT):
                        r = slice(t * P, (t + 1) * P)
                        mm = halves_product(dst(t), [(h_hi[:, k, r], h_lo[:, k, r], w_hi[:, m % 4, 0:width],
                                                      w_lo[:, m % 4, 0:width])], k == 0, k == KC - 1)
                    mm.then_inc(half_used, 1)

            by_slices(0, range(KC), lambda t: ps[:, 4 + 3 * t, 0:S5_CH])

            def part(n, a):
                if n >= 3 and a == 0:
                    pe.wait_ge(proj_ready, 2 * (n - 2))
                by_slices(n, range(4 * a, 4 * a + 4), lambda t: ps[:, 2 * ((n - 1) % 2) + t, :])

            part(1, 0)
            pe.wait_ge(u_tok_ready, TT)
            for c in range(S5_C):
                for t in range(TT):
                    mm = pe.transpose(ps[:, 5, c * S + t * P:c * S + (t + 1) * P], u_tok[:, t, c * P:(c + 1) * P], ident)
            mm.then_inc(uT_psum, 1)
            pe.wait_ge(bb_ready, 1)
            for r in range(2):
                for c in range(S5_C):
                    mm = pe.transpose(ps[:, 6, (r * 2 + c) * P:(r * 2 + c + 1) * P],
                                      bb[:, r, 4 * c:4 * c + 4, :].rearrange("p j c -> p (j c)"), ident)
            mm.then_inc(bT_psum, 1)
            part(1, 1)
            pe.wait_ge(u_ready, 1)
            pe.wait_ge(bT_ready, 1)
            drive(0)
            part(2, 0)
            part(2, 1)
            pe.wait_ge(bu_used, 1)
            drive(1)
            project(3, 0)
            project(3, 1)
            part(4, 0)

            pe.wait_ge(bu_used, 2)
            pe.wait_ge(rot_ready, 2)
            for a in range(2):
                for h in range(4):
                    for t in range(TT):
                        mm = pe.transpose(ps[:, 4 + 2 * a + h // 2, (h % 2) * S + t * P:(h % 2) * S + (t + 1) * P],
                                          qk[:, t, a * MW + h * P:a * MW + (h + 1) * P], ident)
            mm.then_inc(rotT_psum, 1)
            part(4, 1)
            pe.wait_ge(rotT_ready, 2)
            for h in range(4):
                for o_ in range(2):
                    r = slice(HD * o_, HD * (o_ + 1))
                    mm = pe.matmul(ps[:, 4 + 2 * o_ + h // 2, (h % 2) * S:(h % 2 + 1) * S], mqT[r, h, P:S], mkT[r, h, :],
                                   start=True, stop=True)
            mm.then_inc(s_psum, 1)
            project(5, 0)
            pe.wait_ge(s_read, 1)
            for h in range(4):
                for o_ in range(2):
                    r = slice(HD * o_, HD * (o_ + 1))
                    mm = pe.matmul(ps[:, 4 + o_, h * P:(h + 1) * P], mqT[r, h, 0:P], mkT[r, h, 0:P], start=True, stop=True)
            mm.then_inc(s_psum, 1)
            project(5, 1)
            pe.wait_ge(consts_in, 80)
            pe.wait_ge(states_ready, 1)
            for c in range(S5_C):
                for j in range(4):
                    for r, st in ((0, xr), (1, zi)):
                        mm = pe.matmul(ps[32 * j:32 * j + 32, 6, c * S:(c + 1) * S], c_s[:, r, 4 * c + j, :],
                                       st[:, 4 * c + j, :], start=(r == 0), stop=(r == 1))
            mm.then_inc(y_psum, 1)
            pe.wait_ge(ret_rot_ready, 1)
            pe.wait_ge(proj_ready, 8)
            for a in range(2):
                for h in range(2):
                    for t in range(TT):
                        mm = pe.transpose(ps[:, 2 + a, h * S + t * P:h * S + (t + 1) * P],
                                          ret[:, t, a * RW + h * P:a * RW + (h + 1) * P], ident)
            mm.then_inc(retT_psum, 1)


            def turn(bank, blocks):
                for h, src in enumerate(blocks):
                    mm = pe.transpose(ps[:, bank, h * P:(h + 1) * P], src, ident)
                mm.then_inc(pT_psum, 1)

            pe.wait_ge(exp_ready, 8)
            pe.wait_ge(s_read, 2)
            for b in range(2):
                turn(4 + b, [att1[:, 4 * b + h, 0:P] for h in range(4)])
            pe.wait_ge(retT_ready, 2)
            pe.wait_ge(proj_ready, 10)
            for h in range(2):
                for o_ in range(2):
                    r = slice(HD * o_, HD * (o_ + 1))
                    pe.matmul(ps[:, o_, h * S:(h + 1) * S], rkT[r, h, 0:P], rqT[r, h, :], start=True, stop=True)
            for h in range(2):
                for o_ in range(2):
                    r = slice(HD * o_, HD * (o_ + 1))
                    mm = pe.matmul(ps[:, 2 + o_, h * P:(h + 1) * P], rkT[r, h, P:S], rqT[r, h, P:S], start=True, stop=True)
            mm.then_inc(rs_psum, 1)
            pe.wait_ge(y_ready, 1)
            for m in range(S5_C):
                for c in range(S5_C):
                    mm = pe.matmul(ps[:, 7, m * S:(m + 1) * S], glu_s[:, c, m * P:(m + 1) * P], uT[:, c, :],
                                   start=(c == 0), stop=(c == S5_C - 1))
            mm.then_inc(glu_psum, 1)
            pe.wait_ge(ya_ready, 1)
            for t in range(TT):
                for c in range(S5_C):
                    mm = pe.transpose(ps[:, 6, t * S5_CH + c * P:t * S5_CH + (c + 1) * P], uT[:, c, t * P:(t + 1) * P], ident)
            mm.then_inc(yaT_psum, 1)
            pe.wait_ge(exp_ready, 16)
            pe.wait_ge(pT_ready, 2)
            for b in range(2):
                turn(4 + b, [att0[:, b, h, :] for h in range(4)])
            pe.wait_ge(rp_ready, 1)
            for h in range(RH):
                vc = slice(2 * RW + h * HD, 2 * RW + (h + 1) * HD)
                pe.matmul(ps[:, 2, h * HD:(h + 1) * HD], rP0[:, h, 0:P], ret[:, 0, vc], start=True, stop=True)
                o1 = ps[:, 2, RW + h * HD:RW + (h + 1) * HD]
                pe.matmul(o1, rP0[:, h, P:S], ret[:, 0, vc], start=True, stop=False)
                mm = pe.matmul(o1, rP1[:, h, :], ret[:, 1, vc], start=False, stop=True)
            mm.then_inc(ret_o_psum, 1)
            pe.wait_ge(ya_read, 1)
            for b in range(2):
                turn(6 + b, [att1[:, 4 * b + h, P:S] for h in range(4)])
            pe.wait_ge(pT_ready, 4)
            for h in range(MH):
                g = 4 * (h % 2) + h // 2
                c = slice(h * HD, (h + 1) * HD)
                mm = pe.matmul(ps[:, 4, c], att0[:, g // 4, g % 4, :], mv[:, 0, c], start=True, stop=True)
            mm.then_inc(o_psum, 1)
            pe.wait_ge(pT_ready, 6)
            pe.wait_ge(proj_ready, 10)
            for h in range(MH):
                g = 4 * (h % 2) + h // 2
                c = slice(h * HD, (h + 1) * HD)
                pe.matmul(ps[:, 5, c], att1[:, g, 0:P], mv[:, 0, c], start=True, stop=False)
                mm = pe.matmul(ps[:, 5, c], att1[:, g, P:S], mv[:, 1, c], start=False, stop=True)
            mm.then_inc(o_psum, 1)

            keep_warm(ident, 7, 16)
            pe.wait_ge(mix_ready, 1)
            transpose_rows(ymix)
            for n in range(2):
                for k in range(KC):
                    if n == 0:
                        pe.wait_ge(th_ready, KC + k + 1)
                        pe.wait_ge(tl_ready, KC + k + 1)
                    pe.wait_ge(lo_ready, FRONT + KC * n + k + 1)
                    for t in range(TT):
                        r = slice(t * P, (t + 1) * P)
                        mm = halves_product(ps[:, 4 + 2 * n + t, :],
                                            [(h_hi[:, k, r], h_lo[:, k, r], w_hi[:, k % 4, :], w_lo[:, k % 4, :])],
                                            k == 0, k == KC - 1)
                    mm.then_inc(half_used, 1)
            keep_warm(ident, 3, 30)
            pe.wait_ge(xn_ready, TT)
            transpose_rows(xn)
            for n in range(2):
                for k in range(KC):
                    if n == 0:
                        pe.wait_ge(th_ready, 2 * KC + k + 1)
                        pe.wait_ge(tl_ready, 2 * KC + k + 1)
                    pe.wait_ge(lo_ready, FRONT + KC * (2 + n) + k + 1)
                    for h in range(4):
                        c = slice(h * P, (h + 1) * P)
                        mm = halves_product(ps[:, 4 * (1 - n) + h, 0:S],
                                            [(w_hi[:, k % 4, c], w_lo[:, k % 4, c], h_hi[:, k, :], h_lo[:, k, :])],
                                            k == 0, k == KC - 1)
                    mm.then_inc(half_used, 1)

            def key_scores(t):
                for h in range(PH):
                    for c in range(2):
                        r = slice(HD * c, HD * (c + 1))
                        mm = pe.matmul(ps[:, 4 + 2 * c + h // 4, (h % 4) * NKEY:(h % 4 + 1) * NKEY],
                                       pqT[r, h, t * P:(t + 1) * P], keys_s[r, h, :], start=True, stop=True)
                mm.then_inc(sc_psum, 1)

            def keys_turn(t, groups=None, first=False, first_group=False):
                for s in range(UN):
                    if first:
                        pe.wait_ge(pq_ready, 4 + s + 1)
                    else:
                        pe.wait_ge(act_ready, UN * t + s - 3)
                    for h in range(2):
                        pe.wait_ge(lo_ready, TAIL + 8 * t + 2 * s + h + 1)
                        slot = 2 * (s % 2) + h
                        pairs = [(w_hi[:, slot, k * P:(k + 1) * P], w_lo[:, slot, k * P:(k + 1) * P],
                                  h_hi[:, 4 * h + k, :], h_lo[:, 4 * h + k, :]) for k in range(4)]
                        halves_product(ps[:, s, 0:S], pairs, h == 0, h == 1).then_inc(half_used, 1)
                    if groups is not None:
                        g = groups + s
                        pe.wait_ge(hot_ready, g + 1)
                        if not (first_group and s < 2):
                            pe.wait_ge(group_done, g - 1)
                        for q in range(GT):
                            mm = pe.matmul(ps[:, 4 + 2 * (s % 2) + q // 2, (q % 2) * 2 * NKEY:(q % 2 + 1) * 2 * NKEY],
                                           hot_j[:, s % 2, q, :], hot_gate[:, s % 2, q].rearrange("p a i -> p (a i)"),
                                           start=True, stop=True)
                        mm.then_inc(group_psum, 1)

            keys_turn(0, first=True)
            pe.wait_ge(keys_in, 16)
            key_scores(0)
            keys_turn(1)
            pe.wait_ge(sc_ready, 4)
            key_scores(1)
            with pe.Fori(2, ROUTE_TURN) as t:
                keys_turn(t)
            pe.wait_ge(sc_ready, 8)
            pe.wait_ge(tok_ready, 1)
            for t in range(TT):
                for a in range(3):
                    mm = pe.transpose(ps[:, 4 + t, a * P:(a + 1) * P], rows[:, t, a, :], ident)
            mm.then_inc(route_psum, 1)
            keys_turn(ROUTE_TURN)
            pe.wait_ge(route_low, TT)
            keys_turn(G_TURN0, groups=0, first_group=True)
            with pe.Fori(G_TURN0 + 1, TURNS - 1) as t:
                keys_turn(t, groups=UN * t - UN * G_TURN0)
            keys_turn(TURNS - 1)

            def values_turn(t, first=False, last=False):
                for s in range(UN):
                    pe.wait_ge(w_ready, UN * t + s + 1)
                    for h in range(2):
                        pe.wait_ge(lo_ready, TAIL + 2 * NT + 8 * t + 2 * s + h + 1)
                        slot = 2 * (s % 2) + h
                        for tt_ in range(TT):
                            r = slice(tt_ * P, (tt_ + 1) * P)
                            mm = halves_product(ps[:, 4 + 2 * h + tt_, :],
                                                [(h_hi[:, s, r], h_lo[:, s, r], w_hi[:, slot, :], w_lo[:, slot, :])],
                                                first and s == 0, last and s == UN - 1)
                        mm.then_inc(half_used, 1)

            pe.wait_ge(group_done, S // GT)
            values_turn(0, first=True)
            with pe.Fori(1, TURNS - 1) as t:
                values_turn(t)
            values_turn(TURNS - 1, last=True)

        def rotation(src, heads, m, cos, sin, scratch):
            views = []
            for t in range(TT):
                x_ = src[:, t, 0:heads * HD].rearrange("p (h d) -> p h d", d=HD)
                size = heads * m
                ta, tb = (scratch[:, (2 * t + i) * size:(2 * t + i + 1) * size].rearrange("p (h d) -> p h d", h=heads)
                          for i in range(2))
                co, si = (rot[:, o_ + t * m:o_ + (t + 1) * m].unsqueeze(1).to_broadcast([P, heads, m]) for o_ in (cos, sin))
                views.append((x_[:, :, 0:m], x_[:, :, m:2 * m], co, si, ta, tb))
            return views

        @block.vector
        def _(dve):
            ch = Chain(dve, dve_steps)
            did, settle = ch.did, ch.settle
            n_var = [0]

            def step(ins):
                did(ins)
                settle()

            def tt(out_, a, b, op):
                return V.tensor_tensor(out_, a, b, op)

            def rstd_from(sums_, n, width, dst=rstd):
                V.tensor_scalar(std[:, 0:n], sums_, 1.0 / width, EPS, ALU.mult, ALU.add).then_inc(var_ready, 1)
                n_var[0] += 1
                dve.wait_ge(std_ready, n_var[0])
                return V.reciprocal(dst[:, 0:n], std[:, 0:n])

            V.memset(mv[:, 0, 0:P], 0.0).then_inc(zeros_ready, 1)
            dve.wait_ge(params_in, 16)
            step(V.tensor_scalar(kk, cols(V_LDT, 8), float(1 / np.log(2)), ROUND, ALU.mult, ALU.add))
            step(V.tensor_scalar(kk, kk, -ROUND, None, ALU.add))
            step(V.scalar_tensor_tensor(rest, kk, -LN2_1, cols(V_LDT, 8), ALU.mult, ALU.add))
            step(V.scalar_tensor_tensor(rest, kk, -LN2_2, rest, ALU.mult, ALU.add))
            step(V.tensor_scalar(kk, kk, -127.0, 127.0, ALU.max, ALU.min))
            step(V.tensor_scalar(power.bitcast(mybir.dt.int32), kk, 127.0, float(2 ** 23), ALU.add, ALU.mult))
            step(V.tensor_scalar(dt, rest, EXP_C[0], None, ALU.mult))
            for c_ in EXP_C[1:]:
                step(V.scalar_tensor_tensor(dt, dt, c_, rest, ALU.add, ALU.mult))
            step(V.scalar_tensor_tensor(dt, dt, 1.0, power, ALU.add, ALU.mult))
            tt(expo, cols(V_LR, 8), dt, ALU.mult).then_inc(expo_ready, 1)

            def transposed_low(gain, n):
                for k in range(KC):
                    dve.wait_ge(th_ready, n * KC + 2 * (k // 2) + 2)
                    V.scalar_tensor_tensor(h_lo[:, k, :], ps[:, k // 2, (k % 2) * S:(k % 2 + 1) * S], cols(gain + k, 1),
                                           h_hi[:, k, :].bitcast(F32), ALU.mult, ALU.subtract).then_inc(tl_ready, 1)

            transposed_low(V_G1, 0)
            dve.wait_ge(sumsq_x, TT)
            rstd_from(ss_x, TT, D, rx).then_inc(rx_ready, 1)

            lr, li = cols(V_LR, 8), cols(V_LI, 8)
            step(tt(ang, li, dt, ALU.mult))
            step(V.tensor_scalar(kk, ang, float(1 / TWO_PI), ROUND, ALU.mult, ALU.add))
            step(V.tensor_scalar(kk, kk, -ROUND, None, ALU.add))
            for part in (RC1, RC2, RC3):
                step(V.scalar_tensor_tensor(ang, kk, -part, ang, ALU.mult, ALU.add))
            step(V.tensor_scalar(ang, ang, -PI_LOW, PI_LOW, ALU.max, ALU.min))
            step(V.tensor_scalar(half, ang, -1.0, None, ALU.mult))
            step(tt(half, half, ang, ALU.min))
            V.tensor_scalar(half, half, float(np.pi / 2), None, ALU.add).then_inc(ang_ready, 1)
            did(tt(q1, lr, lr, ALU.mult))
            did(tt(q2, li, li, ALU.mult))
            settle()
            step(tt(den, q1, q2, ALU.add))
            did(V.reciprocal(den, den))
            dve.wait_ge(mag_ready, 1)
            dve.wait_ge(trig_ready, 1)
            did(tt(ar, mag, c1, ALU.mult))
            did(tt(ai, mag, s1, ALU.mult))
            settle()
            step(V.tensor_scalar(ar, ar, -1.0, None, ALU.add))
            did(tt(q1, ar, lr, ALU.mult))
            did(tt(q2, ai, li, ALU.mult))
            did(tt(q3, ai, lr, ALU.mult))
            did(tt(kk, ar, li, ALU.mult))
            settle()
            did(tt(fr, q1, q2, ALU.add))
            did(tt(fi, q3, kk, ALU.subtract))
            settle()
            did(tt(fr, fr, den, ALU.mult))
            did(tt(fi, fi, den, ALU.mult))
            settle()
            dve.wait_ge(s5_b_in, 16)
            wide = lambda a: a.unsqueeze(2).to_broadcast([P, S5_T, 32])
            t_a = hj[:, 0:256].rearrange("p (j c) -> p j c", j=S5_T)
            t_b = hj[:, 256:512].rearrange("p (j c) -> p j c", j=S5_T)
            did(tt(bb[:, 0], b_s[:, 0], wide(fr), ALU.mult))
            did(tt(t_a, b_s[:, 1], wide(fi), ALU.mult))
            did(tt(bb[:, 1], b_s[:, 1], wide(fr), ALU.mult))
            did(tt(t_b, b_s[:, 0], wide(fi), ALU.mult))
            settle()
            did(tt(bb[:, 0], bb[:, 0], t_a, ALU.subtract))
            settle()
            tt(bb[:, 1], bb[:, 1], t_b, ALU.add).then_inc(bb_ready, 1)
            dve.wait_ge(bb_ready, 1)

            did(V.tensor_copy(sq_c[:, 0, :], c1))
            did(V.tensor_copy(sq_s[:, 0, :], s1))
            did(V.memset(pc[:, :, 0:1], 1.0))
            did(V.memset(pS[:, :, 0:1], 0.0))
            settle()
            for n in range(SEG_LOG + 1):
                m = 1 << n
                if n < SEG_LOG:
                    shape = [P, S5_T, m]
                    wc, ws = (a[:, n, :].unsqueeze(2).to_broadcast(shape) for a in (sq_c, sq_s))
                    lo_c, lo_s, hi_c, hi_s = pc[:, :, 0:m], pS[:, :, 0:m], pc[:, :, m:2 * m], pS[:, :, m:2 * m]
                    did(tt(hi_c, lo_c, wc, ALU.mult))
                    did(tt(zr[:, :, 0:m], lo_s, ws, ALU.mult))
                    did(tt(hi_s, lo_c, ws, ALU.mult))
                    did(tt(zi[:, :, 0:m], lo_s, wc, ALU.mult))
                    a, b = sq_c[:, n, :], sq_s[:, n, :]
                    did(tt(q1, a, a, ALU.mult))
                    did(tt(q2, b, b, ALU.mult))
                    did(tt(q3, a, b, ALU.mult))
                    settle()
                    did(tt(hi_c, hi_c, zr[:, :, 0:m], ALU.subtract))
                    did(tt(hi_s, hi_s, zi[:, :, 0:m], ALU.add))
                    did(tt(sq_c[:, n + 1, :], q1, q2, ALU.subtract))
                    did(V.tensor_scalar(sq_s[:, n + 1, :], q3, 2.0, None, ALU.mult))
                    settle()

            def head_rms(a):
                dve.wait_ge(qk_sq, a + 1)
                d_ = slice(16 * a, 16 * a + 16)
                step(V.tensor_reduce(sums[:, d_].rearrange("p (t h) -> p t h", t=TT),
                                     mv.rearrange("p t (h d) -> p t h d", d=HD), AX.X, ALU.add))
                rstd_from(sums[:, d_], 16, HD, qk_rstd[:, d_]).then_inc(qk_rstd_ready, 1)

            seg = lambda a: a.rearrange("p j (g s) -> p j g s", s=SEG)
            phase = lambda a, js: a[:, js].unsqueeze(2).to_broadcast([P, 4, S // SEG, SEG])
            head_rms(0)
            for c in range(S5_C):
                js = slice(4 * c, 4 * c + 4)
                bur, bui = seg(ps[:, 4:8, 0:S]), seg(ps[:, 4:8, S:2 * S])
                dve.wait_ge(bu_psum, c + 1)
                did(tt(seg(zr[:, js]), bur, phase(pc, js), ALU.mult))
                did(tt(seg(tmp1), bui, phase(pS, js), ALU.mult))
                did(tt(seg(zi[:, js]), bui, phase(pc, js), ALU.mult))
                tt(seg(xr[:, js]), bur, phase(pS, js), ALU.mult).then_inc(bu_used, 1)
                dve.wait_ge(bu_used, c + 1)
                settle()
                did(tt(zr[:, js], zr[:, js], tmp1, ALU.add))
                tt(zi[:, js], zi[:, js], xr[:, js], ALU.subtract).then_inc(drive_ready, 1)
                dve.wait_ge(drive_ready, c + 1)
                settle()
                if c == 0:
                    head_rms(1)

            def scans(g, init):
                for j in range(S5_T):
                    for z, z0 in ((zr, z0r), (zi, z0i)):
                        zs = z[:, j, g * SEG:(g + 1) * SEG]
                        did(V.tensor_tensor_scan(zs, mag[:, j:j + 1].to_broadcast([P, SEG]), zs,
                                                 z0[:, j:j + 1] if init else 0.0, ALU.mult, ALU.add))
                settle()

            scans(0, False)
            er, ei = zr[:, :, SEG - 1], zi[:, :, SEG - 1]
            did(tt(q1, sq_c[:, SEG_LOG, :], er, ALU.mult))
            did(tt(q2, sq_s[:, SEG_LOG, :], ei, ALU.mult))
            did(tt(q3, sq_c[:, SEG_LOG, :], ei, ALU.mult))
            did(tt(kk, sq_s[:, SEG_LOG, :], er, ALU.mult))
            settle()
            did(tt(z0r, q1, q2, ALU.subtract))
            did(tt(z0i, q3, kk, ALU.add))
            settle()
            scans(1, True)

            def rotate_back(c):
                js = slice(4 * c, 4 * c + 4)
                did(tt(seg(xr[:, js]), seg(zr[:, js]), phase(pc, js), ALU.mult))
                did(tt(seg(tmp1), seg(zi[:, js]), phase(pS, js), ALU.mult))
                settle()
                did(tt(xr[:, js], xr[:, js], tmp1, ALU.subtract))
                did(tt(seg(zr[:, js]), seg(zr[:, js]), phase(pS, js), ALU.mult))
                did(tt(seg(zi[:, js]), seg(zi[:, js]), phase(pc, js), ALU.mult))
                settle()
                did(tt(zi[:, js], zi[:, js], zr[:, js], ALU.add))
                settle()

            dve.wait_ge(consts_in, 80)
            rotate_back(0)
            rotate_back(1)
            V.tensor_scalar(c_s[:, 1], c_s[:, 1], -1.0, None, ALU.mult).then_inc(states_ready, 1)
            dve.wait_ge(states_ready, 1)
            dve.wait_ge(s_psum, 1)
            s1_ = ps[:, 4:8, :].rearrange("p b (h k) -> p (b h) k", h=2)
            V.scalar_tensor_tensor(att1, s1_, SCALE, mask_s.unsqueeze(1).to_broadcast([P, MH, S]), ALU.mult,
                                   ALU.add).then_inc(s_read, 1)
            dve.wait_ge(s_read, 1)
            V.tensor_reduce(hmax[:, 8:16], att1, AX.X, ALU.max, negate=True).then_inc(max_ready, 1)
            dve.wait_ge(s_psum, 2)
            dve.wait_ge(ret_rot_ready, 1)
            for b in range(2):
                ins = V.scalar_tensor_tensor(att0[:, b], ps[:, 4 + b, :].rearrange("p (h k) -> p h k", h=4), SCALE,
                                             mask_s[:, P:S].unsqueeze(1).to_broadcast([P, 4, P]), ALU.mult, ALU.add)
                if b:
                    ins.then_inc(s_read, 1)
                else:
                    did(ins)
            settle()
            dve.wait_ge(s_read, 2)
            V.tensor_reduce(hmax[:, 0:8].rearrange("p (t g) -> p t g", t=TT), att0, AX.X, ALU.max,
                            negate=True).then_inc(max_ready, 1)
            dve.wait_ge(y_psum, 1)
            for c in range(S5_C):
                V.scalar_tensor_tensor(uT[:, c, :], uT[:, c, :], cols(V_D + c, 1), ps[:, 6, c * S:(c + 1) * S],
                                       ALU.mult, ALU.add).then_inc(y_lin, 1)
            dve.wait_ge(exp_ready, 16)
            step(V.reciprocal(hsum, hsum))
            dve.wait_ge(rs_psum, 1)
            dec = decay_s.rearrange("p (h o) i -> p h o i", o=2)
            for o_ in range(2):
                ins = tt(rP0.rearrange("p (h o) i -> p h o i", o=2)[:, :, o_],
                         ps[:, o_, :].rearrange("p (h i) -> p h i", h=2), dec[:, :, o_], ALU.mult)
                if o_:
                    ins.then_inc(ret_read, 1)
            for o_ in range(2):
                ins = tt(rP1.rearrange("p (h o) i -> p h o i", o=2)[:, :, o_],
                         ps[:, 2 + o_, 0:256].rearrange("p (h i) -> p h i", h=2), dec[:, :, o_, 0:P], ALU.mult)
                if o_:
                    ins.then_inc(rp_ready, 1)
            dve.wait_ge(gate_ready, 1)
            tt(uT[:], uT[:], gate_s.rearrange("p (c t) -> p c t", c=S5_C), ALU.mult).then_inc(ya_ready, 1)
            dve.wait_ge(yaT_psum, 1)
            V.tensor_copy(ymix[:, :, 0:S5_CH], ps[:, 6, :].rearrange("p (t d) -> p t d", t=TT)).then_inc(ya_read, 1)
            dve.wait_ge(ya_read, 1)
            sq = squares[:, 0:512].rearrange("p (t d) -> p t d", t=TT)
            step(tt(sq, ymix[:, :, 0:S5_CH], ymix[:, :, 0:S5_CH], ALU.mult))
            step(V.tensor_reduce(sums[:, 0:2], sq, AX.X, ALU.add))
            step(rstd_from(sums[:, 0:2], TT, S5_CH))
            for t in range(TT):
                did(V.tensor_scalar(ymix[:, t, 0:S5_CH], ymix[:, t, 0:S5_CH], rstd[:, t:t + 1], None, ALU.mult))
            settle()
            dve.wait_ge(ret_o_psum, 1)
            y_c = ymix[:, :, S5_CH + MW:D].rearrange("p t (h d) -> p t h d", d=HD)
            step(V.tensor_copy(ymix[:, :, S5_CH + MW:D], ps[:, 2, :].rearrange("p (t d) -> p t d", t=TT)))
            sq = squares[:, 512:1024].rearrange("p (t h d) -> p t h d", t=TT, d=HD)
            step(tt(sq, y_c, y_c, ALU.mult))
            step(V.tensor_reduce(sums[:, 16:24].rearrange("p (t h) -> p t h", t=TT), sq, AX.X, ALU.add))
            step(rstd_from(sums[:, 16:24], 8, HD))
            for t in range(TT):
                did(tt(y_c[:, t], y_c[:, t], rstd[:, 4 * t:4 * t + 4].unsqueeze(2).to_broadcast([P, RH, HD]), ALU.mult))
            settle()
            dve.wait_ge(silu_ready, 1)
            did(tt(ymix[:, :, S5_CH + MW:D], ymix[:, :, S5_CH + MW:D], ret[:, :, 3 * RW:4 * RW], ALU.mult))
            for t in range(TT):
                ds = slice(8 * t, 8 * t + 8)
                dve.wait_ge(o_sq, t + 1)
                by_g = lambda a: a.rearrange("p (p2 o d) -> p o p2 d", o=2, d=HD)
                step(V.tensor_reduce(sums[:, ds].rearrange("p (o p2) -> p o p2", o=2),
                                     by_g(squares[:, 1024 + MW * t:1024 + MW * (t + 1)]), AX.X, ALU.add))
                step(tt(sums[:, ds], sums[:, ds], hsum[:, ds], ALU.mult))
                step(tt(sums[:, ds], sums[:, ds], hsum[:, ds], ALU.mult))
                step(rstd_from(sums[:, ds], 8, HD))
                step(tt(hsum[:, ds], hsum[:, ds], rstd[:, 0:8], ALU.mult))
                factor = hsum[:, ds].rearrange("p (o p2) -> p o p2", o=2)
                ins = tt(by_g(ymix[:, t, S5_CH:S5_CH + MW]), by_g(ps[:, 4 + t, :]),
                         factor.unsqueeze(3).to_broadcast([P, 2, 4, HD]), ALU.mult)
                if t == TT - 1:
                    ins.then_inc(mix_ready, 1)
                else:
                    did(ins)

            transposed_low(V_GM, 1)
            for n in range(2):
                dve.wait_ge(half_used, FRONT + KC * (n + 1))
                for t in range(TT):
                    c = slice(CHUNK * n, CHUNK * (n + 1))
                    tt(xs[:, t, c], xs[:, t, c], ps[:, 4 + 2 * n + t, :], ALU.add).then_inc(sum2_ready, 1)
            dve.wait_ge(sumsq_2, 4)
            step(tt(ss_x, ss_2[:, 0:2], ss_2[:, 2:4], ALU.add))
            step(rstd_from(ss_x, TT, D))
            V.tensor_scalar(xn[:, 0, :], xs[:, 0, :], rstd[:, 0:1], None, ALU.mult).then_inc(xn_ready, 1)
            transposed_low(V_G2, 2)

            def best(dst, where, src, scratch):
                for d_, s_ in zip(dst, src):
                    did(V.max(d_[:, 0:8], s_))
                settle()
                for d_, w_, s_, x_ in zip(dst, where, src, scratch):
                    did(V.max_index(w_[:, 0:8], d_[:, 0:8], s_))
                    did(V.match_replace(x_, d_[:, 0:8], s_, LOWEST))
                settle()
                for d_, x_ in zip(dst, scratch):
                    did(V.max(d_[:, 8:16], x_))
                settle()
                for d_, w_, x_ in zip(dst, where, scratch):
                    did(V.max_index(w_[:, 8:16], d_[:, 8:16], x_))
                settle()

            ch_rows = [(c, h) for c in range(2) for h in range(PH)]
            shape = [P, PH, PK, PK]
            w2 = work2.rearrange("p (h a b) -> p h a b", h=PH, a=PK)
            w3 = work3.rearrange("p (h a b) -> p h a b", h=PH, a=PK)
            iota_k = iota[:, 0:PK].unsqueeze(1).unsqueeze(1).to_broadcast(shape)
            for t in range(TT):
                dve.wait_ge(sc_ready, 4 * t + 4)
                best([top[:, c, h, :] for c, h in ch_rows], [idx[:, c, h, :] for c, h in ch_rows],
                     [sc[:, t, c, h, :] for c, h in ch_rows], [work[:, c, h, :] for c, h in ch_rows])
                did(V.tensor_copy(idx_f, idx))
                step(tt(w2, top[:, 0].unsqueeze(3).to_broadcast(shape), top[:, 1].unsqueeze(2).to_broadcast(shape), ALU.add))
                pairs = [work2[:, h * 256:(h + 1) * 256] for h in range(PH)]
                best([top2[:, h, :] for h in range(PH)], [pos[:, h, :] for h in range(PH)], pairs,
                     [work3[:, h * 256:(h + 1) * 256] for h in range(PH)])
                did(tt(rows[:, t, 2, :].rearrange("p (h k) -> p h k", h=PH), top2,
                       top2[:, :, 0:1].to_broadcast([P, PH, PK]), ALU.subtract))
                did(V.tensor_scalar(ab[:, 0], pos, 4, None, ALU.logical_shift_right))
                did(V.tensor_scalar(ab[:, 1], pos, PK - 1, None, ALU.bitwise_and))
                settle()
                step(V.tensor_copy(ab_f, ab))
                for c in range(2):
                    step(tt(w2, ab_f[:, c].unsqueeze(3).to_broadcast(shape), iota_k, ALU.is_equal))
                    step(tt(w3, w2, idx_f[:, c].unsqueeze(2).to_broadcast(shape), ALU.mult))
                    step(V.tensor_reduce(rows[:, t, c, :].rearrange("p (h k) -> p h k", h=PH), w3, AX.X, ALU.add))
            V.tensor_copy(top2[:, 0, 0:1], top2[:, 0, 1:2]).then_inc(diff_ready, 1)
            dve.wait_ge(gate_exp, TT)
            gates = rows[:, :, 2, :].rearrange("p t (h k) -> p t h k", h=PH)
            step(V.tensor_reduce(gsum, gates, AX.X, ALU.add))
            step(V.reciprocal(gsum, gsum))
            for t in range(TT):
                did(tt(gates[:, t], gates[:, t], gsum[:, t].unsqueeze(2).to_broadcast([P, PH, PK]), ALU.mult))
            settle()
            V.tensor_copy(top2[:, 0, 0:1], top2[:, 0, 1:2]).then_inc(tok_ready, 1)
            for t in range(TT):
                dve.wait_ge(route_ready, TT + t + 1)
                c = slice(t * P, (t + 1) * P)
                tt(route_t[:, 3, c], ps[:, 4 + t, 2 * P:3 * P], route_t[:, 2, c], ALU.subtract).then_inc(route_low, 1)
            dve.wait_ge(route_low, TT)

            def group_out(g, b):
                dve.wait_ge(group_high, g + 1)
                parts = ps[:, 4 + 2 * b:6 + 2 * b, :].rearrange("p b (t a i) -> p (b t) a i", t=2, a=2)
                tt(routing[:, bass.ds(g * GT, GT), :], routing[:, bass.ds(g * GT, GT), :], parts[:, :, 1, :],
                   ALU.add).then_inc(group_done, 1)

            def one_hots(t, first=False):
                for s in range(UN):
                    g = UN * t + s
                    if not (first and s < 2):
                        dve.wait_ge(group_psum, g - 1)
                    tok = bass.ds(g * GT, GT)
                    tt(hot_j[:, s % 2], iota.unsqueeze(1).to_broadcast([P, GT, P]),
                       route_t[:, 1, tok].unsqueeze(2).to_broadcast([P, GT, P]), ALU.is_equal)
                    for q in range(GT):
                        one = bass.ds(g * GT + q, 1)
                        ins = V.scalar_tensor_tensor(hot_gate[:, s % 2, q], iota.unsqueeze(1).to_broadcast([P, 2, NKEY]),
                                                     route_t[:, 0, one], route_t[:, 2:4, one].to_broadcast([P, 2, NKEY]),
                                                     ALU.is_equal, ALU.mult)
                    ins.then_inc(hot_ready, 1)
                    if not (first and s == 0):
                        group_out(g - 1, (s - 1) % 2)

            one_hots(0, first=True)
            with dve.Fori(1, TURNS - 1 - G_TURN0) as t:
                one_hots(t)

            group_out(S // GT - 1, 1)
            dve.wait_ge(group_done, S // GT)

            def weigh(t, tile, first=False):
                for s in range(UN):
                    n = UN * t + s
                    if first:
                        dve.wait_ge(act_ready, NT - UN + s + 1)
                    else:
                        if s % 2 == 0:
                            dve.wait_ge(acts_in[s // 2], 16 * t)
                        dve.wait_ge(half_used, TAIL + 2 * NT + 8 * t + 2 * s - 6)
                    tt(weighted[:, s % 2, :], acts[:, s, :],
                       routing[:, :, bass.ds(tile + s, 1)].rearrange("p t o -> p (t o)"), ALU.mult).then_inc(product_done, 1)
                    dve.wait_ge(product_done, n + 1)
                    if first:
                        dve.wait_ge(half_used, TAIL + 2 * NT - 1)
                    V.tensor_copy(h_hi[:, s, :], weighted[:, s % 2, :]).then_inc(w_steps, 1)
                    dve.wait_ge(w_steps, n + 1)
                    tt(h_lo[:, s, :], weighted[:, s % 2, :], h_hi[:, s, :].bitcast(F32), ALU.subtract).then_inc(w_ready, 1)

            weigh(0, NT - UN, first=True)
            with dve.Fori(1, TURNS) as t:
                weigh(t, UN * t - UN)
            for h in range(2):
                dve.wait_ge(half_used, TAIL + 4 * NT - 1 + h)
                for t in range(TT):
                    c = slice(h * HALF, (h + 1) * HALF)
                    tt(xs[:, t, c], xs[:, t, c], ps[:, 4 + 2 * h + t, :], ALU.add).then_inc(sum_ready, 1)

        @block.scalar
        def _(act):
            ch = Chain(act, act_steps)
            did, settle = ch.did, ch.settle
            n_std = [0]

            def root(n):
                n_std[0] += 1
                act.wait_ge(var_ready, n_std[0])
                A.activation(std[:, 0:n], std[:, 0:n], ACT.Sqrt).then_inc(std_ready, 1)

            def slices_high(ms):
                for m in ms:
                    n, k, width = slice_place(m)
                    if k == 0:
                        act.wait_ge(w_in_sem[n % W_SLOTS], 16 * (n // W_SLOTS + 1))
                    if m >= 4:
                        act.wait_ge(half_used, m - 3)
                    A.activation(w_hi[:, m % 4, 0:width], w_ring[n % W_SLOTS][:, k, 0:width], ACT.Copy)\
                        .then_inc(hi_ready, 1)

            def transposed_high(gain, n, ks=range(KC)):
                for k in ks:
                    act.wait_ge(t_psum, 4 * n + k // 2 + 1)
                    A.activation(h_hi[:, k, :], ps[:, k // 2, (k % 2) * S:(k % 2 + 1) * S], ACT.Copy,
                                 scale=cols(gain + k, 1)).then_inc(th_ready, 1)

            for t in range(TT):
                act.wait_ge(x_in[t], 16)
                if t:
                    act.wait_ge(sumsq_x, t)
                A.activation(xn[:, t, :], xs[:, t, :], ACT.Square, accum_out=ss_x[:, t:t + 1]).then_inc(sumsq_x, 1)
            act.wait_ge(params_in, 16)
            transposed_high(V_G1, 0, range(0, 4))
            slices_high(range(0, 2))
            transposed_high(V_G1, 0, range(4, KC))
            slices_high(range(2, 4))
            root(TT)
            act.wait_ge(expo_ready, 1)
            A.activation(mag, expo, ACT.Exp).then_inc(mag_ready, 1)
            slices_high(range(4, 9))
            act.wait_ge(ang_ready, 1)
            did(A.activation(s1, ang, ACT.Sin))
            settle()
            A.activation(c1, half, ACT.Sin).then_inc(trig_ready, 1)
            slices_high(range(9, 12))
            act.wait_ge(rx_ready, 1)
            act.wait_ge(half_used, KC)
            for t in range(TT):
                A.activation(u_tok[:, t, :], ps[:, 4 + 3 * t, 0:S5_CH], ACT.Copy,
                             scale=rx[:, t:t + 1]).then_inc(u_tok_ready, 1)
            slices_high(range(12, 16))
            act.wait_ge(uT_psum, 1)
            A.activation(uT, ps[:, 5, :].rearrange("p (c t) -> p c t", c=S5_C), ACT.Copy).then_inc(u_ready, 1)
            act.wait_ge(bT_psum, 1)
            A.activation(bT, ps[:, 6, :].rearrange("p (a s) -> p a s", a=4), ACT.Copy).then_inc(bT_ready, 1)
            slices_high(range(16, 20))

            dst = [qk[:, :, 0:MW], qk[:, :, MW:2 * MW], ret[:, :, 2 * RW:4 * RW], ret[:, :, 0:2 * RW], mv]

            def projected(n, t):
                if n + 1 in SPLIT_CHUNKS:
                    act.wait_ge(half_used, KC * (SPLIT_CHUNKS.index(n + 1) + 1))
                else:
                    act.wait_ge(proj_psum, 2 * (n // 2 - 1) + t + 1)
                A.activation(dst[n][:, t, :], ps[:, 2 * (n % 2) + t, :], ACT.Copy,
                             scale=rx[:, t:t + 1]).then_inc(proj_ready, 1)

            def exps(places):
                for a, g in places:
                    A.activation(a, a, ACT.Exp, bias=hmax[:, g:g + 1], accum_out=hsum[:, g:g + 1]).then_inc(exp_ready, 1)

            def square_heads(n):
                act.wait_ge(proj_ready, 2 * n + 2)
                if n:
                    act.wait_ge(qk_rstd_ready, 1)
                A.activation(mv, dst[n], ACT.Square).then_inc(qk_sq, 1)

            projected(0, 0)
            projected(0, 1)
            square_heads(0)
            slices_high(range(20, 22))
            root(16)
            slices_high(range(22, 24))
            projected(1, 0)
            projected(1, 1)
            square_heads(1)
            root(16)
            slices_high(range(24, 28))
            projected(2, 0)
            projected(2, 1)
            slices_high(range(28, 32))
            act.wait_ge(rotT_psum, 1)
            for h, d_ in ((0, mqT), (2, mkT)):
                A.activation(d_, ps[:, 4 + h:6 + h, :].rearrange("p b (h t) -> p (b h) t", h=2), ACT.Copy)\
                    .then_inc(rotT_ready, 1)
            projected(3, 0)
            projected(3, 1)
            act.wait_ge(max_ready, 1)
            exps([(att1[:, g, :], 8 + g) for g in range(MH)])
            projected(4, 0)
            act.wait_ge(max_ready, 2)
            exps([(att0[:, g // 4, g % 4, :], g) for g in range(MH)])
            projected(4, 1)
            act.wait_ge(retT_psum, 1)
            A.activation(rqT, ps[:, 2, :].rearrange("p (h t) -> p h t", h=2), ACT.Copy).then_inc(retT_ready, 1)
            A.activation(rkT, ps[:, 3, :].rearrange("p (h t) -> p h t", h=2), ACT.Copy).then_inc(retT_ready, 1)
            act.wait_ge(y_lin, 2)
            A.activation(uT, uT, ACT.Gelu_apprx_tanh).then_inc(y_ready, 1)

            def probs_back(n, bank, d_):
                act.wait_ge(pT_psum, n + 1)
                A.activation(d_, ps[:, bank, :].rearrange("p (h k) -> p h k", h=4), ACT.Copy).then_inc(pT_ready, 1)

            for b in range(2):
                probs_back(b, 4 + b, att1[:, 4 * b:4 * b + 4, 0:P])
            act.wait_ge(glu_psum, 1)
            A.activation(gate_s, ps[:, 7, :], ACT.Sigmoid).then_inc(gate_ready, 1)
            A.activation(ret[:, :, 3 * RW:4 * RW], ret[:, :, 3 * RW:4 * RW], ACT.Silu).then_inc(silu_ready, 1)
            for b in range(2):
                probs_back(2 + b, 4 + b, att0[:, b])
            root(TT)
            for b in range(2):
                probs_back(4 + b, 6 + b, att1[:, 4 * b:4 * b + 4, P:S])
            root(8)
            for t in range(TT):
                act.wait_ge(o_psum, t + 1)
                A.activation(squares[:, 1024 + MW * t:1024 + MW * (t + 1)], ps[:, 4 + t, :], ACT.Square).then_inc(o_sq, 1)
                root(8)
            slices_high(range(FRONT, FRONT + 4))
            transposed_high(V_GM, 1)
            slices_high(range(FRONT + 4, FRONT + 2 * KC))
            for n in range(2):
                for t in range(TT):
                    c = slice(CHUNK * n, CHUNK * (n + 1))
                    act.wait_ge(sum2_ready, TT * n + t + 1)
                    A.activation(done_proj[:, CHUNK * t:CHUNK * (t + 1)] if n == 0 else
                                 done_proj[:, 1024 + CHUNK * t:1024 + CHUNK * (t + 1)], xs[:, t, c], ACT.Square,
                                 accum_out=ss_2[:, 2 * n + t:2 * n + t + 1]).then_inc(sumsq_2, 1)
            slices_high(range(FRONT + 2 * KC, FRONT + 2 * KC + 4))
            root(TT)
            act.wait_ge(xn_ready, 1)
            A.activation(xn[:, 1, :], xs[:, 1, :], ACT.Copy, scale=rstd[:, 1:2]).then_inc(xn_ready, 1)
            transposed_high(V_G2, 2)
            slices_high(range(FRONT + 2 * KC + 4, FRONT + 3 * KC))

            def queries(n):
                act.wait_ge(half_used, FRONT + KC * (3 + n))
                for h in range(4):
                    A.activation(pqT[:, 4 * n + h, :], ps[:, 4 * (1 - n) + h, 0:S], ACT.Copy).then_inc(pq_ready, 1)

            slices_high(range(FRONT + 3 * KC, FRONT + 3 * KC + 4))
            queries(0)
            slices_high(range(FRONT + 3 * KC + 4, TAIL))

            def key_scores(t, b):
                act.wait_ge(sc_psum, t + 1)
                A.activation(sc[:, t, b // 2, 4 * (b % 2):4 * (b % 2) + 4, :],
                             ps[:, 4 + b, :].rearrange("p (h n) -> p h n", h=4), ACT.Copy).then_inc(sc_ready, 1)

            def high(n, s, turn):
                act.wait_ge(raw_in[s], 16 * turn + 16)
                for h in range(2):
                    act.wait_ge(half_used, TAIL + 2 * n + h - 3)
                    A.activation(w_hi[:, 2 * (s % 2) + h, :], raw[:, s, h * HALF:(h + 1) * HALF], ACT.Copy)\
                        .then_inc(hi_ready, 1)

            def keys_turn(t, groups=None, first=False, first_group=False, extra=None):
                for s in range(UN):
                    n = UN * t + s
                    high(n + 1, (s + 1) % UN, t + (s + 1) // UN)
                    if extra is not None:
                        extra(s)
                    if groups is not None and not (first_group and s == 0):
                        group_out(groups + s - 1, (s - 1) % 2)
                    if s % 2 == 0 and not first:
                        act.wait_ge(spilled[s // 2], 16 * t)
                    act.wait_ge(half_used, TAIL + 2 * n + 2)
                    A.activation(acts[:, s, :], ps[:, s, 0:S], ACT.Gelu_apprx_tanh).then_inc(act_ready, 1)

            def group_out(g, b):
                act.wait_ge(group_psum, g + 1)
                parts = ps[:, 4 + 2 * b:6 + 2 * b, :].rearrange("p b (t a i) -> p (b t) a i", t=2, a=2)
                A.activation(routing[:, bass.ds(g * GT, GT), :], parts[:, :, 0, :], ACT.Copy).then_inc(group_high, 1)

            high(0, 0, 0)
            queries(1)
            keys_turn(0, first=True)
            keys_turn(1, extra=lambda s: key_scores(0, s))
            keys_turn(2, extra=lambda s: key_scores(1, s))
            with act.Fori(3, EXP_TURN) as t:
                keys_turn(t)

            def gate_exps(s):
                if s == 0:
                    act.wait_ge(diff_ready, 1)
                    for t in range(TT):
                        A.activation(rows[:, t, 2, :], rows[:, t, 2, :], ACT.Exp).then_inc(gate_exp, 1)

            def route_rows(s):
                if s < 2:
                    act.wait_ge(route_psum, 1)
                    for t in range(TT):
                        c = slice(t * P, (t + 1) * P)
                        if s == 0:
                            A.activation(route_t[:, 0:2, c], ps[:, 4 + t, 0:2 * P].rearrange("p (a t) -> p a t", a=2),
                                         ACT.Copy).then_inc(route_ready, 1)
                        else:
                            A.activation(route_t[:, 2, c].bitcast(F32R), ps[:, 4 + t, 2 * P:3 * P],
                                         ACT.Copy).then_inc(route_ready, 1)

            keys_turn(EXP_TURN, extra=gate_exps)
            keys_turn(ROUTE_TURN, extra=route_rows)
            keys_turn(G_TURN0, groups=0, first_group=True)
            with act.Fori(G_TURN0 + 1, TURNS - 1) as t:
                keys_turn(t, groups=UN * t - UN * G_TURN0)
            group_out(S // GT - 1, 1)
            keys_turn(TURNS - 1)
            with act.Fori(TURNS, 2 * TURNS - 1) as t:
                for s in range(UN):
                    high(UN * t + s + 1, (s + 1) % UN, t + (s + 1) // UN)
            for s in range(UN - 1):
                high(2 * NT - UN + s + 1, s + 1, 2 * TURNS - 1)

        @block.gpsimd
        def _(pool):
            G = nc.gpsimd
            ch = Chain(pool, pool_steps)
            did, settle = ch.did, ch.settle
            def rotate(views, ready):
                for x1, x2, co, si, ta, tb in views:
                    did(G.tensor_tensor(ta, x2, si, ALU.mult))
                    did(G.tensor_tensor(tb, x1, si, ALU.mult))
                settle()
                for x1, x2, co, si, ta, tb in views:
                    did(G.tensor_tensor(x1, x1, co, ALU.mult))
                    did(G.tensor_tensor(x2, x2, co, ALU.mult))
                settle()
                for n, (x1, x2, co, si, ta, tb) in enumerate(views):
                    did(G.tensor_tensor(x1, x1, ta, ALU.subtract))
                    ins = G.tensor_tensor(x2, x2, tb, ALU.add)
                    if n == TT - 1:
                        ins.then_inc(ready, 1)
                    else:
                        did(ins)
                settle()

            def slices_low(ms):
                for m in ms:
                    n, k, width = slice_place(m)
                    pool.wait_ge(hi_ready, m + 1)
                    G.tensor_tensor(w_lo[:, m % 4, 0:width], w_ring[n % W_SLOTS][:, k, 0:width],
                                    w_hi[:, m % 4, 0:width].bitcast(F32), ALU.subtract).then_inc(lo_ready, 1)

            slices_low(range(0, 16))
            pool.wait_ge(tl_ready, KC)
            for c in range(2):
                d_ = slice(4 * c, 4 * c + 4)
                G.tensor_tensor(hT[:, d_], h_hi[:, d_].bitcast(F32), h_lo[:, d_].bitcast(F32), ALU.add).then_inc(hT_ready, 1)
            slices_low(range(16, 24))
            for a in range(2):
                heads = qk[:, :, a * MW:(a + 1) * MW]
                h4 = heads.rearrange("p t (h d) -> p t h d", d=HD)
                pool.wait_ge(qk_rstd_ready, a + 1)
                for t in range(TT):
                    r_v = qk_rstd[:, 16 * a + 8 * t:16 * a + 8 * t + 8].unsqueeze(2).to_broadcast([P, MH, HD])
                    did(G.tensor_tensor(h4[:, t], h4[:, t], r_v, ALU.mult))
                settle()
                for t in range(TT):
                    did(G.tensor_tensor(h4[:, t], h4[:, t],
                                        cols(V_GQK + a * HD, HD).unsqueeze(1).to_broadcast([P, MH, HD]), ALU.mult))
                settle()
                pool.wait_ge(consts_in, 80)
                rotate(rotation(heads, MH, ROPE // 2, C_RC, C_RS, rot_tmp[:, 1024:2048]), rot_ready)
                slices_low(range(24 + 4 * a, 28 + 4 * a))
            pool.wait_ge(proj_ready, 8)
            rotate(rotation(ret, 2 * RH, HD // 2, C_TC, C_TS, rot_tmp), ret_rot_ready)
            slices_low(range(FRONT, TAIL))
            def low(t):
                for s in range(UN):
                    for h in range(2):
                        pool.wait_ge(hi_ready, TAIL + 8 * t + 2 * s + h + 1)
                        slot = 2 * (s % 2) + h
                        G.tensor_tensor(w_lo[:, slot, :], raw[:, s, h * HALF:(h + 1) * HALF],
                                        w_hi[:, slot, :].bitcast(F32), ALU.subtract).then_inc(lo_ready, 1)

            with pool.Fori(0, 2 * TURNS) as t:
                low(t)


def host_constants():
    f = np.float32
    pos = np.arange(S, dtype=f)
    inv = (f(500000.0) ** (-np.arange(0, ROPE, 2, dtype=f) / f(ROPE))).astype(f)
    ang = pos[:, None] * inv[None, :]
    lin = np.linspace(0.0, 1.0, HD // 2, dtype=f)
    rang = pos[:, None] * (f(10000.0) ** (-lin)).astype(f)[None, :]
    tile = lambda a: a.astype(f).reshape(TT, P, -1).transpose(1, 0, 2).reshape(P, -1)
    consts = np.concatenate([np.eye(P, dtype=f), np.broadcast_to(np.arange(P, dtype=f), (P, P))], axis=1)
    rots = np.concatenate([tile(np.cos(ang)), tile(np.sin(ang)), tile(np.cos(rang)), tile(np.sin(rang))], axis=1)
    log_g = np.log(1.0 - 2.0 ** (-5.0 - np.arange(RH, dtype=np.float64)))
    diff = np.arange(S)[None, :] - np.arange(P)[:, None]
    decay = np.where(diff[:, None, :] >= 0, np.exp(np.maximum(diff, 0)[:, None, :] * log_g[None, :, None]), 0.0)
    decay = (decay * HD ** -0.5).astype(f)
    mask = np.zeros((P, S), f)
    mask[:, P:] = np.where(np.arange(P)[None, :] <= np.arange(P)[:, None], 0.0, MASKED)
    return consts, rots, decay, mask


def layout(inputs):
    a = {k: np.asarray(v)[0] if k != "x" else np.asarray(v) for k, v in inputs.items()}
    f = np.float32
    per = lambda v_, n: v_.reshape(n, P).T
    rep = lambda v_: np.broadcast_to(v_, (P, HD))
    vecs = np.concatenate([
        per(a["norm1_g"], KC), per(a["norm2_g"], KC), per(a["mix_out_g"], KC),
        per(a["s5_lam_re"].reshape(-1), S5_T), per(a["s5_lam_im"].reshape(-1), S5_T),
        per(np.repeat(a["s5_log_dt"], S5_STATE), S5_T), per(a["s5_d"], S5_C),
        rep(a["moba_q_g"]), rep(a["moba_k_g"])], axis=1)
    b = np.zeros((P, 2, S5_T, 32), f)
    c = np.zeros((P, 2, S5_T, 32), f)
    for r, (bn, cn) in enumerate((("s5_b_re", "s5_c_re"), ("s5_b_im", "s5_c_im"))):
        for o in range(2):
            rows, at = slice(64 * o, 64 * o + 64), slice(16 * o, 16 * o + 16)
            b[rows, r, :, at] = a[bn][o::2].transpose(1, 0, 2)
            c[rows, r, :, at] = a[cn][o::2].transpose(2, 0, 1)
    consts, rots, decay, mask = host_constants()
    u_t = a["peer_u"].reshape(NT, P, KC, P).transpose(0, 3, 2, 1).reshape(NT, P, D)
    keys = a["peer_sub_keys"].transpose(1, 3, 0, 2).reshape(P, PH, NKEY)
    return {
        "x": a["x"][0], "w_in": a["w_in"], "vecs": vecs, "consts": consts, "rots": rots, "decay": decay, "mask": mask,
        "s5_b": b.reshape(P, -1), "s5_c": c.reshape(P, -1), "w_glu": a["s5_w_glu"], "w_out": a["w_out"],
        "w_q": a["peer_w_q"], "keys": keys, "u_t": u_t, "v": a["peer_v"].reshape(NT, P, D),
    }


_OUT = (S, D)


def kernel(**inputs):
    import concourse.bacc as _bacc
    from concourse.bass_utils import run_bass_kernel_spmd as _run

    nc = _bacc.Bacc("TRN2", target_bir_lowering=False, num_devices=1)
    arrays, args = {}, {}
    for name, a in layout(inputs).items():
        a = np.ascontiguousarray(a)
        arrays[f"in_{name}"] = a
        args[name] = nc.dram_tensor(f"in_{name}", a.shape, mybir.dt.from_np(a.dtype), kind="ExternalInput").ap()
    args["out"] = nc.dram_tensor("out_0", _OUT, F32, kind="ExternalOutput").ap()
    args["spill"] = nc.dram_tensor("act_spill", (NT // 2, P, 2 * S), F32, kind="Internal").ap()
    build(nc, **args)
    r = _run(nc, [arrays], core_ids=[0])
    return r.results[0]["out_0"].reshape(1, S, D)
```
